# Optimizing a Trainium2 kernel written in Bass

```python
import math
import jax, jax.numpy as jnp
from jax import lax
import numpy as np

D_MODEL = 1024
BATCH = 1
SEQ = 128
DEPTH = 2
DEC_BATCH = 1
DEC_SEQ = 1024
PAST_LEN = 128

GRID_W = 64
NORM_EPS = 1e-6
SSD_HEADS = 8
SSD_HEAD_DIM = 64
SSD_STATE = 64
SSD_GROUPS = 2
SSD_CONV = 3
SSD_CHUNK = 64
SSD_WIDTH = SSD_HEADS * SSD_HEAD_DIM
SSD_BC = SSD_GROUPS * SSD_STATE
SSD_XBC = SSD_WIDTH + 2 * SSD_BC
SSD_IN = SSD_WIDTH + SSD_XBC + 2 * SSD_HEADS
NA_HEADS = 8
NA_HEAD_DIM = 64
NA_WIDTH = NA_HEADS * NA_HEAD_DIM
NA_IN = 3 * NA_WIDTH
NA_WIN_ROWS = 8
NA_WIN_COLS = 16
NA_SCALE = NA_HEAD_DIM ** -0.5
GLA_HEADS = 4
GLA_DK = 64
GLA_DV = 128
GLA_QK = GLA_HEADS * GLA_DK
GLA_V = GLA_HEADS * GLA_DV
GLA_RANK = 16
GLA_GATE_NORM = 16.0
HGRN_HEADS = 4
HGRN_DK = 64
HGRN_DV = 128
HGRN_QK = HGRN_HEADS * HGRN_DK
HGRN_V = HGRN_HEADS * HGRN_DV
LIN_CHUNK = 16
IN_L0 = SSD_IN + NA_IN
IN_L1 = 2 * GLA_QK + 2 * GLA_V + 2 * GLA_RANK + 3 * HGRN_QK + 2 * HGRN_V
MIX_OUT = D_MODEL
FFN_DIM = 2816
FFN_CONV = 3

kernel_name = 'hybrid_diffusion_trunk_step'

def _rms(x, w):
    xf = x.astype(jnp.float32)
    y = xf * lax.rsqrt(jnp.mean(xf * xf, axis=-1, keepdims=True) + NORM_EPS)
    return y.astype(x.dtype) * w

def _split(u, sizes):
    offs = [int(o) for o in np.cumsum(sizes)[:-1]]
    return jnp.split(u, offs, axis=-1)

def _heads(x, h):
    b, t, _ = x.shape
    return x.reshape(b, t, h, -1).transpose(0, 2, 1, 3)

def _unheads(x):
    b, h, t, d = x.shape
    return x.transpose(0, 2, 1, 3).reshape(b, t, h * d)

def _dwconv(x, w, b):
    k = w.shape[0]
    p = k // 2
    t = x.shape[1]
    xp = jnp.pad(x, ((0, 0), (p, p), (0, 0)))
    out = b
    for i in range(k):
        out = out + xp[:, i:i + t] * w[i]
    return out

def _chunk_scan(q, k, v, g, s0, chunk):
    out_dtype = q.dtype
    b, h, t, _ = q.shape
    dv = v.shape[-1]
    n = t // chunk

    def blk(a):
        return a.astype(jnp.float32).reshape(b, h, n, chunk, a.shape[-1])

    q, k, v, g = blk(q), blk(k), blk(v), blk(g)
    G = jnp.cumsum(g, axis=3)
    mask = jnp.tril(jnp.ones((chunk, chunk), bool))
    diff = G[:, :, :, :, None, :] - G[:, :, :, None, :, :]
    decay = jnp.exp(jnp.where(mask[:, :, None], diff, -jnp.inf))
    if g.shape[-1] == 1:
        scores = jnp.einsum('bhntd,bhnsd->bhnts', q, k) * decay[..., 0]
    else:
        scores = jnp.einsum('bhntd,bhnsd,bhntsd->bhnts', q, k, decay)
    o_intra = jnp.einsum('bhnts,bhnsv->bhntv', scores, v)
    G_last = G[:, :, :, -1:, :]
    q_in = q * jnp.exp(G)
    k_end = k * jnp.exp(G_last - G)
    d_last = jnp.exp(G_last[:, :, :, 0, :])

    def step(S, xs):
        qc, kc, vc, dc = xs
        o = jnp.einsum('bhtd,bhdv->bhtv', qc, S)
        S = dc[..., None] * S + jnp.einsum('bhtd,bhtv->bhdv', kc, vc)
        return S, o

    xs = (jnp.moveaxis(q_in, 2, 0), jnp.moveaxis(k_end, 2, 0), jnp.moveaxis(v, 2, 0), jnp.moveaxis(d_last, 2, 0))
    S, o_inter = lax.scan(step, s0.astype(jnp.float32), xs)
    o = o_intra + jnp.moveaxis(o_inter, 0, 2)
    return o.reshape(b, h, t, dv).astype(out_dtype), S

def _bidir(q, kf, kb, vf, vb, gf, gb, s0f, s0b, chunk):
    of, sf = _chunk_scan(q, kf, vf, gf, s0f, chunk)
    fl = lambda a: jnp.flip(a, axis=2)
    ob, sb = _chunk_scan(fl(q), fl(kb), fl(vb), fl(gb), s0b, chunk)
    return of + fl(ob), sf, sb

def _ssd(ua, conv_w, conv_b, dt_bias, a_log, d_skip, norm_w, s0f, s0b):
    bsz, t, _ = ua.shape
    z, xbc, dt_raw = _split(ua, [SSD_WIDTH, SSD_XBC, 2 * SSD_HEADS])
    xbc = jax.nn.silu(_dwconv(xbc, conv_w, conv_b))
    xs, bm, cm = _split(xbc, [SSD_WIDTH, SSD_BC, SSD_BC])
    x_h = _heads(xs, SSD_HEADS)
    rep = SSD_HEADS // SSD_GROUPS
    k = jnp.repeat(_heads(bm, SSD_GROUPS), rep, axis=1)
    q = jnp.repeat(_heads(cm, SSD_GROUPS), rep, axis=1)
    dt = jax.nn.softplus(dt_raw.reshape(bsz, t, 2, SSD_HEADS).astype(jnp.float32) + dt_bias)
    dt = dt.transpose(2, 0, 3, 1)
    a = -jnp.exp(a_log.astype(jnp.float32))
    g = (dt * a[:, None, :, None])[..., None]
    vf = x_h * dt[0][..., None]
    vb = x_h * dt[1][..., None]
    y, sf, sb = _bidir(q, k, k, vf, vb, g[0], g[1], s0f, s0b, SSD_CHUNK)
    y = y + d_skip[None, :, None, None] * x_h
    y = _unheads(y)
    return _rms(y * jax.nn.silu(z), norm_w), sf, sb

def _na_context(ub, q_norm, k_norm):
    q, k, v = [_heads(a, NA_HEADS) for a in _split(ub, [NA_WIDTH] * 3)]
    q = _rms(q, q_norm)
    k = _rms(k, k_norm)
    s = jnp.einsum('bhqd,bhkd->bhqk', q, k).astype(jnp.float32) * NA_SCALE
    p = jax.nn.softmax(s, axis=-1).astype(v.dtype)
    o = jnp.einsum('bhqk,bhkd->bhqd', p, v)
    return _unheads(o), k, v

def _na_latent(ub, k_ctx, v_ctx, q_norm, k_norm, rpb):
    bsz, t, _ = ub.shape
    rows = t // GRID_W
    wr = min(NA_WIN_ROWS, rows)
    q, k, v = [_heads(a, NA_HEADS) for a in _split(ub, [NA_WIDTH] * 3)]
    q = _rms(q, q_norm)
    k = _rms(k, k_norm)
    grid = lambda a: a.reshape(bsz, NA_HEADS, rows, GRID_W, NA_HEAD_DIM)
    q, k, v = grid(q), grid(k), grid(v)
    r = jnp.arange(rows)
    row_start = jnp.clip(r - wr // 2, 0, rows - wr)
    row_idx = row_start[:, None] + jnp.arange(wr)[None, :]
    n_loc = wr * GRID_W
    k_loc = k[:, :, row_idx].reshape(bsz, NA_HEADS, rows, n_loc, NA_HEAD_DIM)
    v_loc = v[:, :, row_idx].reshape(bsz, NA_HEADS, rows, n_loc, NA_HEAD_DIM)
    col = jnp.arange(GRID_W)
    col_start = jnp.clip(col - NA_WIN_COLS // 2, 0, GRID_W - NA_WIN_COLS)
    col_ok = (col[None, :] >= col_start[:, None]) & (col[None, :] < col_start[:, None] + NA_WIN_COLS)
    valid = jnp.tile(col_ok, (1, wr))
    d_row = row_idx - r[:, None] + (NA_WIN_ROWS - 1)
    d_col = jnp.clip(col[None, :] - col[:, None], -(NA_WIN_COLS - 1), NA_WIN_COLS - 1) + (NA_WIN_COLS - 1)
    bias = rpb[:, d_row][:, :, :, d_col]
    bias = bias.transpose(0, 1, 3, 2, 4).reshape(NA_HEADS, rows, GRID_W, n_loc)
    s_loc = jnp.einsum('bhrqd,bhrkd->bhrqk', q, k_loc).astype(jnp.float32) * NA_SCALE + bias
    s_loc = jnp.where(valid, s_loc, -jnp.inf)
    s_ctx = jnp.einsum('bhrqd,bhkd->bhrqk', q, k_ctx).astype(jnp.float32) * NA_SCALE
    p = jax.nn.softmax(jnp.concatenate([s_loc, s_ctx], axis=-1), axis=-1).astype(v.dtype)
    o = (jnp.einsum('bhrqk,bhrkd->bhrqd', p[..., :n_loc], v_loc)
         + jnp.einsum('bhrqk,bhkd->bhrqd', p[..., n_loc:], v_ctx))
    return _unheads(o.reshape(bsz, NA_HEADS, t, NA_HEAD_DIM))

def _mixer_ab(h, cache, w_in, w_out, conv_w, conv_b, dt_bias, a_log, d_skip, ssd_norm_w, q_norm, k_norm, rpb):
    u = h @ w_in
    ua, ub = _split(u, [SSD_IN, NA_IN])
    if cache is None:
        z0 = jnp.zeros((h.shape[0], SSD_HEADS, SSD_STATE, SSD_HEAD_DIM), jnp.float32)
        y_a, s_f, s_b = _ssd(ua, conv_w, conv_b, dt_bias, a_log, d_skip, ssd_norm_w, z0, z0)
        y_b, k_c, v_c = _na_context(ub, q_norm, k_norm)
        new = (k_c, v_c, s_f, s_b)
    else:
        k_c, v_c, s_f0, s_b0 = cache
        y_a, _, _ = _ssd(ua, conv_w, conv_b, dt_bias, a_log, d_skip, ssd_norm_w, s_f0, s_b0)
        y_b = _na_latent(ub, k_c, v_c, q_norm, k_norm, rpb)
        new = ()
    return jnp.concatenate([y_a, y_b], axis=-1) @ w_out, new

def _mixer_cd(h, cache, w_in, w_out, gla_wa2, gla_ba2, gla_norm_w, hgrn_lb, hgrn_norm_w):
    bsz = h.shape[0]
    u = h @ w_in
    gq, gk, gv, gg, gaf, gab, hq, hff, hfb, hi, hg = _split(
        u, [GLA_QK, GLA_QK, GLA_V, GLA_V, GLA_RANK, GLA_RANK, HGRN_QK, HGRN_QK, HGRN_QK, HGRN_V, HGRN_V])
    if cache is None:
        zg = jnp.zeros((bsz, GLA_HEADS, GLA_DK, GLA_DV), jnp.float32)
        zh = jnp.zeros((bsz, HGRN_HEADS, HGRN_DK, HGRN_DV), jnp.float32)
        s_gf, s_gb, s_hf, s_hb = zg, zg, zh, zh
    else:
        s_gf, s_gb, s_hf, s_hb = cache
    q = _heads(gq, GLA_HEADS) * GLA_DK ** -0.5
    k = _heads(gk, GLA_HEADS)
    v = _heads(gv, GLA_HEADS)
    la_f = _heads(jax.nn.log_sigmoid((gaf @ gla_wa2[0] + gla_ba2[0]).astype(jnp.float32)) / GLA_GATE_NORM, GLA_HEADS)
    la_b = _heads(jax.nn.log_sigmoid((gab @ gla_wa2[1] + gla_ba2[1]).astype(jnp.float32)) / GLA_GATE_NORM, GLA_HEADS)
    o_c, n_gf, n_gb = _bidir(q, k, k, v, v, la_f, la_b, s_gf, s_gb, LIN_CHUNK)
    y_c = _unheads(_rms(o_c, gla_norm_w) * jax.nn.silu(_heads(gg, GLA_HEADS)))
    f_f = hgrn_lb[0] + (1.0 - hgrn_lb[0]) * jax.nn.sigmoid(hff.astype(jnp.float32))
    f_b = hgrn_lb[1] + (1.0 - hgrn_lb[1]) * jax.nn.sigmoid(hfb.astype(jnp.float32))
    qh = _heads(hq, HGRN_HEADS)
    ih = _heads(hi, HGRN_HEADS)
    o_d, n_hf, n_hb = _bidir(qh, _heads(1.0 - f_f, HGRN_HEADS), _heads(1.0 - f_b, HGRN_HEADS), ih, ih,
                             _heads(jnp.log(f_f), HGRN_HEADS), _heads(jnp.log(f_b), HGRN_HEADS),
                             s_hf, s_hb, LIN_CHUNK)
    y_d = _unheads(_rms(o_d, hgrn_norm_w) * jax.nn.silu(_heads(hg, HGRN_HEADS)))
    new = (n_gf, n_gb, n_hf, n_hb) if cache is None else ()
    return jnp.concatenate([y_c, y_d], axis=-1) @ w_out, new

def _conv_ffn(h, w_up, conv_w, conv_b, w_down):
    u = _dwconv(h @ w_up, conv_w, conv_b)
    a, b = jnp.split(u, 2, axis=-1)
    return (jax.nn.silu(a) * b) @ w_down

def setup_inputs(seed: int = 0) -> dict:
    key = jax.random.key(seed)
    keys = iter(jax.random.split(key, 64))
    D = D_MODEL

    def nrm(shape, scale):
        return jax.random.normal(next(keys), shape, jnp.float32) * scale

    def gain(shape):
        return 1.0 + nrm(shape, 0.02)

    dt0 = jnp.exp(jax.random.uniform(next(keys), (2, SSD_HEADS), jnp.float32, math.log(1e-3), math.log(1e-1)))
    dt_bias = dt0 + jnp.log(-jnp.expm1(-dt0))
    a_log = jnp.log(jax.random.uniform(next(keys), (2, SSD_HEADS), jnp.float32, 1.0, 16.0))
    return {
        'x_prompt': nrm((BATCH, SEQ, D), 1.0),
        'x_sample': nrm((DEC_BATCH, DEC_SEQ, D), 1.0),
        'cache_na_k_l0': nrm((DEC_BATCH, NA_HEADS, PAST_LEN, NA_HEAD_DIM), 1.0),
        'cache_na_v_l0': nrm((DEC_BATCH, NA_HEADS, PAST_LEN, NA_HEAD_DIM), 1.0),
        'state_ssd_fwd_l0': nrm((DEC_BATCH, SSD_HEADS, SSD_STATE, SSD_HEAD_DIM), 0.5),
        'state_ssd_bwd_l0': nrm((DEC_BATCH, SSD_HEADS, SSD_STATE, SSD_HEAD_DIM), 0.5),
        'state_gla_fwd_l1': nrm((DEC_BATCH, GLA_HEADS, GLA_DK, GLA_DV), 0.5),
        'state_gla_bwd_l1': nrm((DEC_BATCH, GLA_HEADS, GLA_DK, GLA_DV), 0.5),
        'state_hgrn_fwd_l1': nrm((DEC_BATCH, HGRN_HEADS, HGRN_DK, HGRN_DV), 0.5),
        'state_hgrn_bwd_l1': nrm((DEC_BATCH, HGRN_HEADS, HGRN_DK, HGRN_DV), 0.5),
        'c': nrm((DEC_BATCH, D), 1.0),
        'c_ctx': nrm((D,), 1.0),
        'w_ada': nrm((DEPTH, D, 6 * D), 0.5 * D ** -0.5),
        'b_ada': nrm((DEPTH, 6 * D), 0.02),
        'norm_w': gain((DEPTH, 2, D)),
        'ffn_w_up': nrm((DEPTH, D, 2 * FFN_DIM), D ** -0.5),
        'ffn_conv_w': nrm((DEPTH, FFN_CONV, 2 * FFN_DIM), 0.5),
        'ffn_conv_b': nrm((DEPTH, 2 * FFN_DIM), 0.02),
        'ffn_w_down': nrm((DEPTH, FFN_DIM, D), FFN_DIM ** -0.5),
        'w_in_l0': nrm((D, IN_L0), D ** -0.5),
        'w_out_l0': nrm((MIX_OUT, D), MIX_OUT ** -0.5),
        'ssd_conv_w_l0': nrm((SSD_CONV, SSD_XBC), 0.5),
        'ssd_conv_b_l0': nrm((SSD_XBC,), 0.02),
        'ssd_dt_bias_l0': dt_bias,
        'ssd_a_log_l0': a_log,
        'ssd_d_l0': gain((SSD_HEADS,)),
        'ssd_norm_w_l0': gain((SSD_WIDTH,)),
        'na_q_norm_l0': gain((NA_HEAD_DIM,)),
        'na_k_norm_l0': gain((NA_HEAD_DIM,)),
        'na_rpb_l0': nrm((NA_HEADS, 2 * NA_WIN_ROWS - 1, 2 * NA_WIN_COLS - 1), 0.02),
        'w_in_l1': nrm((D, IN_L1), D ** -0.5),
        'w_out_l1': nrm((MIX_OUT, D), MIX_OUT ** -0.5),
        'gla_wa2_l1': nrm((2, GLA_RANK, GLA_QK), GLA_RANK ** -0.5),
        'gla_ba2_l1': nrm((2, GLA_QK), 0.1),
        'gla_norm_w_l1': gain((GLA_DV,)),
        'hgrn_lb_logits': nrm((2, DEPTH, HGRN_QK), 0.1),
        'hgrn_norm_w_l1': gain((HGRN_DV,)),
    }

def reference(x_prompt, x_sample, cache_na_k_l0, cache_na_v_l0, state_ssd_fwd_l0, state_ssd_bwd_l0,
              state_gla_fwd_l1, state_gla_bwd_l1, state_hgrn_fwd_l1, state_hgrn_bwd_l1, c,
              c_ctx, w_ada, b_ada, norm_w, ffn_w_up, ffn_conv_w, ffn_conv_b, ffn_w_down,
              w_in_l0, w_out_l0, ssd_conv_w_l0, ssd_conv_b_l0, ssd_dt_bias_l0, ssd_a_log_l0, ssd_d_l0,
              ssd_norm_w_l0, na_q_norm_l0, na_k_norm_l0, na_rpb_l0,
              w_in_l1, w_out_l1, gla_wa2_l1, gla_ba2_l1, gla_norm_w_l1, hgrn_lb_logits, hgrn_norm_w_l1):
    p_lb = jax.nn.softmax(hgrn_lb_logits.astype(jnp.float32), axis=1)
    lb_all = jnp.cumsum(p_lb, axis=1) - p_lb[:, :1]
    mixer_weights = (
        (w_in_l0, w_out_l0, ssd_conv_w_l0, ssd_conv_b_l0, ssd_dt_bias_l0, ssd_a_log_l0, ssd_d_l0,
         ssd_norm_w_l0, na_q_norm_l0, na_k_norm_l0, na_rpb_l0),
        (w_in_l1, w_out_l1, gla_wa2_l1, gla_ba2_l1, gla_norm_w_l1, lb_all[:, 1], hgrn_norm_w_l1),
    )
    caches = (
        (cache_na_k_l0, cache_na_v_l0, state_ssd_fwd_l0, state_ssd_bwd_l0),
        (state_gla_fwd_l1, state_gla_bwd_l1, state_hgrn_fwd_l1, state_hgrn_bwd_l1),
    )

    def run_layer(x, cvec, l, cache):
        mods = jax.nn.silu(cvec) @ w_ada[l] + b_ada[l]
        sh1, sc1, g1, sh2, sc2, g2 = jnp.split(mods[:, None, :], 6, axis=-1)
        h = _rms(x, norm_w[l, 0]) * (1.0 + sc1) + sh1
        mixer = _mixer_ab if l % 2 == 0 else _mixer_cd
        y, new = mixer(h, cache, *mixer_weights[l])
        x = x + g1 * y
        h = _rms(x, norm_w[l, 1]) * (1.0 + sc2) + sh2
        x = x + g2 * _conv_ffn(h, ffn_w_up[l], ffn_conv_w[l], ffn_conv_b[l], ffn_w_down[l])
        return x, new

    c_ctx_b = c_ctx[None, :]
    y_p, y_s = x_prompt, x_sample
    new_state = []
    for l in range(DEPTH):
        y_p, st = run_layer(y_p, c_ctx_b, l, None)
        new_state.append(st)
        y_s, _ = run_layer(y_s, c, l, caches[l])
    na_k0, na_v0, ssd_f0, ssd_b0 = new_state[0]
    gla_f1, gla_b1, hgrn_f1, hgrn_b1 = new_state[1]
    return (y_p, y_s, na_k0, na_v0, ssd_f0, ssd_b0, gla_f1, gla_b1, hgrn_f1, hgrn_b1)


_drawn_inputs = setup_inputs


def setup_inputs(seed=0):
    import zlib

    import numpy as np

    out = dict(_drawn_inputs(seed))
    spreads = {}
    factors = {'cache_na_k_l0': 4.165,
     'cache_na_v_l0': 3.047,
     'state_gla_fwd_l1': 8.0,
     'state_gla_bwd_l1': 8.0,
     'state_hgrn_fwd_l1': 8.0,
     'state_hgrn_bwd_l1': 8.0,
     'ffn_conv_b': 8.0,
     'ssd_d_l0': 8.0,
     'ssd_norm_w_l0': 8.0,
     'na_q_norm_l0': 8.0,
     'na_k_norm_l0': 7.273,
     'na_rpb_l0': 64.0,
     'gla_norm_w_l1': 49.979,
     'hgrn_norm_w_l1': 47.285}
    for name, (base, spread) in spreads.items():
        noise = np.random.default_rng([zlib.crc32(name.encode()), seed]).standard_normal(out[name].shape)
        drawn = base * np.exp(spread * noise) if base else spread * noise
        out[name] = __import__('jax').numpy.asarray(drawn.astype(out[name].dtype))
    for name, factor in factors.items():
        out[name] = (out[name] * factor).astype(out[name].dtype)
    return out
```

```python
from contextlib import ExitStack

import concourse.bass as bass
from concourse import mybir

F32 = mybir.dt.float32
F32R = mybir.dt.float32r
BF16 = mybir.dt.bfloat16
I16 = mybir.dt.int16
ACT = mybir.ActivationFunctionType
ALU = mybir.AluOpType
AX = mybir.AxisListType

P = 128
D = 1024
KT = D // P
CTX = 128
LAT = 1024
TOK = CTX + LAT
NT = TOK // P
BLK = 384
NB = TOK // BLK
DEPTH = 2
EPS = 1e-6
RANGES = ((0, CTX, 0), (CTX, TOK, 1))
UPAD = TOK + 4
URANGES = ((0, CTX, 1), (CTX, TOK, CTX + 2))
FFN = 2816
FT = FFN // P
GT = FT // 2
ADA = 6 * D // P
SH1, SC1, G1, SH2, SC2, G2 = range(6)


class Scope:

    def __init__(self, nc, tag):
        self.nc, self.tag, self.stack, self.sems = nc, tag, ExitStack(), []

    def sb(self, name, shape, dt=F32):
        return self.stack.enter_context(self.nc.sbuf_tensor(f"{self.tag}__{name}", shape, dt))

    def banks(self, n):
        return [self.stack.enter_context(self.nc.psum_tensor(f"{self.tag}__bank{i}", [P, 512], F32)) for i in range(n)]

    def sem(self, name, for_pool_dma=False):
        s = self.stack.enter_context(self.nc.semaphore(f"{self.tag}__{name}"))
        if not for_pool_dma:
            self.sems.append(s)
        return s

    def __enter__(self):
        return self

    def __exit__(self, *exc):
        self.stack.close()
        if exc[0] is None and self.sems:
            with self.nc.Block() as block:
                @block.gpsimd
                def _(pool):
                    for s in self.sems:
                        pool.sem_clear(s)


def split_matmul(pe, out, w_hi, w_lo, v_hi, v_lo, first, last):
    pe.matmul(out, w_hi, v_lo, start=first, stop=False)
    pe.matmul(out, w_lo, v_hi, start=False, stop=False)
    return pe.matmul(out, w_hi, v_hi, start=False, stop=last)


def modulation(nc, d, mods, gains):
    per = 4
    slots = 4
    rounds = DEPTH * ADA // (slots * per)
    wide = 96
    with Scope(nc, "ada") as s:
        c_in = s.sb("c_in", [P, KT, 2])
        c_act = s.sb("c_act", [P, KT, wide])
        bias = s.sb("bias", [P, DEPTH * ADA, 2])
        norm_w = s.sb("norm_w", [P, DEPTH, 2, KT, 2])
        w = s.sb("w", [P, slots, per, KT, P])
        ps = s.banks(slots)
        small_in, silu_done = s.sem("small_in"), s.sem("silu_done")
        w_in = [s.sem(f"w_in{u}") for u in range(slots)]
        product, added, gained = s.sem("product"), s.sem("added"), s.sem("gained")
        with nc.Block() as block:
            @block.sync
            def _(sp):
                sp.dma_start(c_in[:, :, :], d["c_t"]).then_inc(small_in, 16)
                sp.dma_start(bias[:, :, :], d["b_ada"]).then_inc(small_in, 16)
                sp.dma_start(norm_w[:, :, :, :, :], d["norm_w"]).then_inc(small_in, 16)

                def load(i, u):
                    sp.dma_start(w[:, u, :, :, :], d["w_ada"][bass.ds(slots * i + u, 1), :, :, :, :]
                                 .rearrange("a t p k c -> p (a t) k c")).then_inc(w_in[u], 16)
                for u in range(slots):
                    load(0, u)
                with sp.Fori(1, rounds) as i:
                    for u in range(slots):
                        sp.wait_ge(product, slots * (i - 1) + u + 1)
                        load(i, u)

            @block.scalar
            def _(act):
                act.wait_ge(small_in, 48)
                act.activation(c_act[:, :, :].rearrange("p k (a c) -> p k a c", c=2),
                               c_in[:, :, :].rearrange("p k (a c) -> p k a c", a=1)
                               .to_broadcast([P, KT, wide // 2, 2]), ACT.Silu).then_inc(silu_done, 1)

            @block.tensor
            def _(pe):
                pe.wait_ge(silu_done, 1)

                def round_(i, u, wait):
                    pe.wait_ge(w_in[u], 16 * (i + 1))
                    if wait:
                        pe.wait_ge(added, slots * (i - 1) + u + 1)
                    for t in range(per):
                        for k in range(KT):
                            last = pe.matmul(ps[u][:, wide * t:wide * (t + 1)], w[:, u, t, k, :], c_act[:, k, :],
                                             start=(k == 0), stop=(k == KT - 1))
                    last.then_inc(product, 1)
                for u in range(slots):
                    round_(0, u, False)
                with pe.Fori(1, rounds) as i:
                    for u in range(slots):
                        round_(i, u, True)

            @block.vector
            def _(dve):
                dve.wait_ge(small_in, 48)
                mods_r = mods[:, :, :].rearrange("p (r t) c -> p r t c", t=per)
                bias_r = bias[:, :, :].rearrange("p (r t) c -> p r t c", t=per)
                with dve.Fori(0, rounds) as i:
                    for u in range(slots):
                        dve.wait_ge(product, slots * i + u + 1)
                        dve.tensor_tensor(mods_r[:, bass.ds(slots * i + u, 1), :, :],
                                          ps[u][:, 0:wide * per].rearrange("p (a t n) -> p a t n", a=1, t=per)[:, :, :, 0:2],
                                          bias_r[:, bass.ds(slots * i + u, 1), :, :], ALU.add).then_inc(added, 1)
                dve.wait_ge(added, slots * rounds)
                for l in range(DEPTH):
                    for w_, part in enumerate((SC1, SC2)):
                        dve.scalar_tensor_tensor(gains[:, l, w_, :, :],
                                                 mods[:, l * ADA + part * KT:l * ADA + (part + 1) * KT, :], 1.0,
                                                 norm_w[:, l, w_, :, :], ALU.add, ALU.mult).then_inc(gained, 1)


def mod(mods, l, part, k, c):
    return mods[:, l * ADA + part * KT + k, c:c + 1]


def norm(nc, tag, l, which, x_t, ones, eps, mods, gains, h_hi, h_lo):
    shift = (SH1, SH2)[which]
    with Scope(nc, tag) as s:
        sq = s.sb("sq", [P, 2, TOK])
        root = s.sb("root", [P, TOK])
        inv = s.sb("inv", [P, TOK])
        xn = s.sb("xn", [P, 2, TOK])
        h = s.sb("h", [P, 2, TOK])
        ps = s.banks(NB)
        squared, summed, rooted, inverted = s.sem("squared"), s.sem("summed"), s.sem("rooted"), s.sem("inverted")
        rescaled = s.sem("rescaled")
        scaled, shifted, hi_done, lo_done = s.sem("scaled"), s.sem("shifted"), s.sem("hi_done"), s.sem("lo_done")
        with nc.Block() as block:
            @block.scalar
            def _(act):
                for k in range(KT):
                    if k >= 2:
                        act.wait_ge(summed, NB * (k - 1))
                    act.activation(sq[:, k % 2, :], x_t[:, k, :], ACT.Square).then_inc(squared, 1)
                for b in range(NB):
                    act.wait_ge(summed, NB * (KT - 1) + b + 1)
                    act.activation(root[:, b * BLK:(b + 1) * BLK], ps[b][:, 0:BLK], ACT.Sqrt, bias=eps[:, 0:1],
                                   scale=1.0 / D).then_inc(rooted, 1)
                for k in range(KT):
                    act.wait_ge(shifted, 2 * (k + 1))
                    act.activation(h_hi[:, k, :], h[:, k % 2, :], ACT.Copy).then_inc(hi_done, 1)

            @block.tensor
            def _(pe):
                for k in range(KT):
                    pe.wait_ge(squared, k + 1)
                    for b in range(NB):
                        pe.matmul(ps[b][:, 0:BLK], ones[:, :], sq[:, k % 2, b * BLK:(b + 1) * BLK],
                                  start=(k == 0), stop=(k == KT - 1)).then_inc(summed, 1)

            @block.gpsimd
            def _(pool):
                for k in range(1, KT, 2):
                    pool.wait_ge(inverted, NB)
                    if k >= 3:
                        pool.wait_ge(shifted, 2 * (k - 1))
                    pool.tensor_tensor(xn[:, 1, :], x_t[:, k, :], inv[:, :], ALU.mult).then_inc(scaled, 1)

            def low(dve, k):
                dve.wait_ge(hi_done, k + 1)
                dve.tensor_tensor(h_lo[:, k, :], h[:, k % 2, :], h_hi[:, k, :].bitcast(F32), ALU.subtract)\
                    .then_inc(lo_done, 1)

            @block.vector
            def _(dve):
                for b in range(NB):
                    dve.wait_ge(rooted, b + 1)
                    dve.reciprocal(inv[:, b * BLK:(b + 1) * BLK], root[:, b * BLK:(b + 1) * BLK])\
                        .then_inc(inverted, 1)
                dve.wait_ge(inverted, NB)
                own = 0
                for k in range(KT):
                    if k % 2 == 0:
                        if k:
                            dve.wait_ge(shifted, 2 * k - 2)
                        dve.tensor_tensor(xn[:, 0, :], x_t[:, k, :], inv[:, :], ALU.mult).then_inc(rescaled, 1)
                        own += 1
                        dve.wait_ge(rescaled, own)
                    else:
                        dve.wait_ge(scaled, (k + 1) // 2)
                    if k >= 2:
                        dve.wait_ge(lo_done, k - 1)
                    for a, b, c in RANGES:
                        dve.tensor_scalar(h[:, k % 2, a:b], xn[:, k % 2, a:b], gains[:, l, which, k, c:c + 1],
                                          mod(mods, l, shift, k, c), ALU.mult, ALU.add).then_inc(shifted, 1)
                    if k >= 1:
                        low(dve, k - 1)
                low(dve, KT - 1)


def load_split_ring(s, name, cols, slots=2):
    return dict(raw=s.sb(name + "_raw", [P, slots, cols]), hi=s.sb(name + "_hi", [P, slots, cols], F32R),
                lo=s.sb(name + "_lo", [P, slots, cols], F32R),
                arrived=[s.sem(f"{name}_arrived{i}") for i in range(slots)],
                hi_done=s.sem(name + "_hi_done"), lo_done=s.sem(name + "_lo_done"))


def conv_ffn(nc, tag, l, d, x_t, mods, h_hi, h_lo):
    units = KT * NB
    with Scope(nc, tag) as s:
        up = load_split_ring(s, "up", KT * P)
        dn_raw = s.sb("dn_raw", [P, D])
        dn_hi, dn_lo = s.sb("dn_hi", [P, 2, D], F32R), s.sb("dn_lo", [P, 2, D], F32R)
        u = s.sb("u", [P, 2, UPAD])
        ca = s.sb("ca", [P, TOK])
        g_hi, g_lo = s.sb("g_hi", [P, 4, TOK], F32R), s.sb("g_lo", [P, 4, TOK], F32R)
        cw = s.sb("cw", [P, FT, 2, 4])
        ps = s.banks(8)
        cw_in, padded = s.sem("cw_in"), s.sem("padded")
        dn_arrived, dn_hi_done, dn_lo_done = s.sem("dn_arrived"), s.sem("dn_hi_done"), s.sem("dn_lo_done")
        up_mm, evicted, tapped, silu_done = s.sem("up_mm"), s.sem("evicted"), s.sem("tapped"), s.sem("silu_done")
        gated, g_hi_done, g_lo_done = s.sem("gated"), s.sem("g_hi_done"), s.sem("g_lo_done")
        dn_mm, x_added = s.sem("dn_mm"), s.sem("x_added")

        def groups(eng, first, body, last=None):
            first()
            with eng.Fori(0, (GT - 1) // 2) as q:
                for v in range(2):
                    body(2 * q + v + 1, (v + 1) % 2)
            if last:
                last()

        with nc.Block() as block:
            @block.sync
            def _(sp):
                sp.dma_start(cw[:, :, :, :], d["ffn_conv"][l]).then_inc(cw_in, 16)

                def load_up(t, half, wait=True):
                    if wait:
                        sp.wait_ge(up["lo_done"], 2 * t + half - 1)
                    sp.dma_start(up["raw"][:, half, :], d["w_up"][l, bass.ds(2 * t + half, 1), :, :]
                                 .rearrange("a p n -> p (a n)")).then_inc(up["arrived"][half], 16)

                def load_down(f, wait=True):
                    if wait:
                        sp.wait_ge(dn_lo_done, f)
                    sp.dma_start(dn_raw[:, :], d["w_down"][l, bass.ds(f, 1), :, :]
                                 .rearrange("a p n -> p (a n)")).then_inc(dn_arrived, 16)

                def first():
                    for half in range(2):
                        load_up(0, half, False)
                    for half in range(2):
                        load_up(1, half)
                    load_down(0, False)

                def group(m, par):
                    for j in range(2):
                        for half in range(2):
                            load_up(2 * m + j, half)
                        load_down(2 * m + j - 1)
                groups(sp, first, group, lambda: load_down(FT - 1))

            @block.scalar
            def _(act):
                def hi_up(t, half, wait=True):
                    act.wait_ge(up["arrived"][half], 16 * (t + 1))
                    if wait:
                        act.wait_ge(up_mm, 6 * t + 3 * half - 3)
                    act.activation(up["hi"][:, half, :], up["raw"][:, half, :], ACT.Copy)\
                        .then_inc(up["hi_done"], 1)

                def hi_down(m, j, wait=True):
                    act.wait_ge(dn_arrived, 16 * (2 * m + j + 1))
                    if wait:
                        act.wait_ge(dn_mm, units * m)
                    act.activation(dn_hi[:, j, :], dn_raw[:, :], ACT.Copy).then_inc(dn_hi_done, 1)

                def evict(t, half, wait=True):
                    if wait and half == 0:
                        act.wait_ge(gated, 2 * t)
                    if wait and half == 1:
                        act.wait_ge(tapped, 12 * t)
                    for b in range(NB):
                        act.wait_ge(up_mm, 6 * t + 3 * half + b + 1)
                        for lo, hi, at in ((0, CTX, 1), (CTX, BLK, CTX + 2)) if b == 0 else \
                                ((b * BLK, (b + 1) * BLK, b * BLK + 2),):
                            last = act.activation(u[:, half, at:at + hi - lo],
                                                  ps[3 * half + b][:, lo - b * BLK:hi - b * BLK], ACT.Copy)
                        last.then_inc(evicted, 1)

                def gate(t, slot, group, wait):
                    act.wait_ge(tapped, 12 * t + 6)
                    act.activation(ca[:, :], ca[:, :], ACT.Silu).then_inc(silu_done, 1)
                    act.wait_ge(gated, 2 * t + 2)
                    if wait:
                        act.wait_ge(dn_mm, units * (group - 1))
                    act.activation(g_hi[:, slot, :], ca[:, :], ACT.Copy).then_inc(g_hi_done, 1)

                def tile(m, par, j, first):
                    t = 2 * m + j
                    more = not (first and j == 0)
                    evict(t, 0, more)
                    hi_up(t + 1, 0)
                    if j == 1:
                        hi_down(m, 0, not first)
                    evict(t, 1, more)
                    hi_up(t + 1, 1)
                    if j == 1:
                        hi_down(m, 1, not first)
                    gate(t, 2 * par + j, m, not first)

                act.wait_ge(padded, 1)
                for half in range(2):
                    hi_up(0, half, False)
                for j in range(2):
                    tile(0, 0, j, True)
                with act.Fori(0, (GT - 3) // 2) as q:
                    for v in range(2):
                        for j in range(2):
                            tile(2 * q + v + 1, (v + 1) % 2, j, False)
                tail_act = [(GT - 2, (GT - 2) % 2), (GT - 1, (GT - 1) % 2)]
                for m, par in tail_act:
                    for j in range(2):
                        t = 2 * m + j
                        if t < FT - 1:
                            tile(m, par, j, False)
                        else:
                            evict(t, 0)
                            hi_down(m, 0)
                            evict(t, 1)
                            hi_down(m, 1)
                            gate(t, 2 * par + j, m, True)

            @block.tensor
            def _(pe):
                def up_tile(t, wait=True):
                    for half in range(2):
                        pe.wait_ge(up["lo_done"], 2 * t + half + 1)
                        for b in range(NB):
                            if wait:
                                pe.wait_ge(evicted, 6 * t + 3 * half + b - 5)
                            for k in range(KT):
                                w = slice(k * P, (k + 1) * P)
                                c = slice(b * BLK, (b + 1) * BLK)
                                last = split_matmul(pe, ps[3 * half + b][:, 0:BLK], up["hi"][:, half, w],
                                                    up["lo"][:, half, w], h_hi[:, k, c], h_lo[:, k, c],
                                                    k == 0, k == KT - 1)
                            last.then_inc(up_mm, 1)

                def down(m, par, wait=True):
                    pe.wait_ge(g_lo_done, 2 * m + 2)
                    pe.wait_ge(dn_lo_done, 2 * m + 2)
                    for v in range(units):
                        k, b = divmod(v, NB)
                        if wait or v >= 2:
                            pe.wait_ge(x_added, units * m + v - 1)
                        for j in range(2):
                            w, c = slice(k * P, (k + 1) * P), slice(b * BLK, (b + 1) * BLK)
                            last = split_matmul(pe, ps[6 + v % 2][:, 0:BLK], dn_hi[:, j, w], dn_lo[:, j, w],
                                                g_hi[:, 2 * par + j, c], g_lo[:, 2 * par + j, c], j == 0, j == 1)
                        last.then_inc(dn_mm, 1)

                up_tile(0, False)
                up_tile(1)
                up_tile(2)
                down(0, 0, False)
                up_tile(3)
                with pe.Fori(0, (GT - 3) // 2) as q:
                    for v in range(2):
                        m = 2 * q + v + 2
                        up_tile(2 * m)
                        down(m - 1, (v + 1) % 2)
                        up_tile(2 * m + 1)
                up_tile(2 * (GT - 1))
                down(GT - 2, (GT - 2) % 2)
                up_tile(2 * (GT - 1) + 1)
                down(GT - 1, (GT - 1) % 2)

            @block.vector
            def _(dve):
                dve.memset(u[:, :, :], 0.0).then_inc(padded, 1)
                dve.wait_ge(cw_in, 16)

                def lo_up(t, half):
                    dve.wait_ge(up["hi_done"], 2 * t + half + 1)
                    dve.tensor_tensor(up["lo"][:, half, :], up["raw"][:, half, :], up["hi"][:, half, :].bitcast(F32),
                                      ALU.subtract).then_inc(up["lo_done"], 1)

                def lo_down(m, j):
                    dve.wait_ge(dn_hi_done, 2 * m + j + 1)
                    dve.tensor_tensor(dn_lo[:, j, :], dn_raw[:, :], dn_hi[:, j, :].bitcast(F32), ALU.subtract)\
                        .then_inc(dn_lo_done, 1)

                def taps(t, half, n, wait=True):
                    if n == 0:
                        dve.wait_ge(evicted, 6 * t + 3 * half + 3)
                        if half == 0 and wait:
                            dve.wait_ge(g_lo_done, t)
                        if half == 1:
                            dve.wait_ge(tapped, 12 * t + 6)
                    else:
                        dve.wait_ge(tapped, 12 * t + 6 * half + 2 * n)
                    for a, b, at in URANGES:
                        out = ca[:, a:b] if half == 0 else u[:, 0, at:at + b - a]
                        w = cw[:, bass.ds(t, 1), half, :].rearrange("p a n -> p (a n)")
                        if n == 0:
                            op = dve.tensor_scalar(out, u[:, half, at:at + b - a], w[:, 1:2], w[:, 3:4],
                                                   ALU.mult, ALU.add)
                        else:
                            off, tap = ((-1, 0), (1, 2))[n - 1]
                            op = dve.scalar_tensor_tensor(out, u[:, half, at + off:at + off + b - a],
                                                          w[:, tap:tap + 1], out, ALU.mult, ALU.add)
                        op.then_inc(tapped, 1)

                def product(t):
                    dve.wait_ge(silu_done, t + 1)
                    dve.wait_ge(tapped, 12 * t + 12)
                    for a, b, at in URANGES:
                        dve.tensor_tensor(ca[:, a:b], ca[:, a:b], u[:, 0, at:at + b - a], ALU.mult)\
                            .then_inc(gated, 1)

                def g_low(t, slot):
                    dve.wait_ge(g_hi_done, t + 1)
                    dve.tensor_tensor(g_lo[:, slot, :], ca[:, :], g_hi[:, slot, :].bitcast(F32), ALU.subtract)\
                        .then_inc(g_lo_done, 1)

                def add_x(m, v, again):
                    k, b = divmod(v, NB)
                    dve.wait_ge(dn_mm, units * m + v + 1)
                    if again:
                        dve.wait_ge(x_added, units * (m - 1) + v + 1)
                    for lo, hi, c in ((0, CTX, 0), (CTX, BLK, 1)) if b == 0 else ((b * BLK, (b + 1) * BLK, 1),):
                        last = dve.scalar_tensor_tensor(x_t[:, k, lo:hi], ps[6 + v % 2][:, lo - b * BLK:hi - b * BLK],
                                                        mod(mods, l, G2, k, c), x_t[:, k, lo:hi], ALU.mult, ALU.add)
                    last.then_inc(x_added, 1)

                def tile(m, par, j, last_tile=False, down=True, again=True):
                    t = 2 * m + j
                    slot = 2 * par + j
                    if not last_tile:
                        lo_up(t + 1, 0)
                    for n in range(3):
                        taps(t, 0, n, down or j == 1)
                    if j == 1:
                        lo_down(m, 0)
                    if not last_tile:
                        lo_up(t + 1, 1)
                    if j == 1:
                        lo_down(m, 1)
                    rest = [lambda n=n: taps(t, 1, n) for n in range(3)] + [lambda: product(t), lambda: g_low(t, slot)]
                    for v in range(units if j == 0 and down else 0):
                        add_x(m - 1, v, again)
                        if v % 3 == 2 and rest:
                            rest.pop(0)()
                    for step in rest:
                        step()

                for half in range(2):
                    lo_up(0, half)
                tile(0, 0, 0, down=False)
                tile(0, 0, 1)
                tile(1, 1, 0, again=False)
                tile(1, 1, 1)
                with dve.Fori(0, (GT - 3) // 2) as q:
                    for v in range(2):
                        for j in range(2):
                            tile(2 * q + v + 2, v % 2, j)
                for j in range(2):
                    tile(GT - 1, (GT - 1) % 2, j, j == 1)
                for v in range(units):
                    add_x(GT - 1, v, True)


TC = 256


def in_project(nc, tag, stored, w_t, w_tok, w_small, h_hi, h_lo, u_t, u_tok, u_small):
    n_t, n_tok = w_t.shape[0], w_tok.shape[0]
    small = w_small.shape[2] if w_small is not None else 0
    loops = n_t // 2
    with Scope(nc, tag) as s:
        wt = load_split_ring(s, "wt", KT * P)
        wk = load_split_ring(s, "wk", KT * TC)
        out_t = s.sb("out_t", [P, 2, TOK])
        out_tok = s.sb("out_tok", [P, 2, TC])
        ps = s.banks(8)
        t_mm, t_out = s.sem("t_mm"), s.sem("t_out")
        t_stored, k_stored, s_stored = stored[0:2], stored[2:4], stored[4]
        k_mm, k_out = s.sem("k_mm"), s.sem("k_out")
        if small:
            ws = load_split_ring(s, "ws", KT * small, 1)
            out_s = s.sb("out_s", [P, NT, small])
            s_mm, s_out = s.sem("s_mm"), s.sem("s_out")
        with nc.Block() as block:
            @block.sync
            def _(sp):
                def load_tok(c):
                    if c >= 2:
                        sp.wait_ge(wk["lo_done"], c - 1)
                    sp.dma_start(wk["raw"][:, c % 2, :], w_tok[c]).then_inc(wk["arrived"][c % 2], 16)

                def load_t(i, j, wait=True):
                    if wait:
                        sp.wait_ge(wt["lo_done"], 2 * i + j - 1)
                    sp.dma_start(wt["raw"][:, j, :], w_t[bass.ds(2 * i + j, 1), :, :]
                                 .rearrange("a p n -> p (a n)")).then_inc(wt["arrived"][j], 16)
                for j in range(2):
                    load_t(0, j, False)
                if small:
                    sp.dma_start(ws["raw"][:, 0, :], w_small.rearrange("p k n -> p (k n)"))\
                        .then_inc(ws["arrived"][0], 16)
                for c in range(2):
                    load_tok(c)
                with sp.Fori(1, loops) as i:
                    for j in range(2):
                        load_t(i, j)
                for c in range(2, n_tok):
                    load_tok(c)

            def split_hi(act, ring, slot, n, free=None):
                act.wait_ge(ring["arrived"][slot], 16 * n)
                if free:
                    act.wait_ge(*free)
                act.activation(ring["hi"][:, slot, :], ring["raw"][:, slot, :], ACT.Copy)\
                    .then_inc(ring["hi_done"], 1)

            def split_lo(dve, ring, slot, n):
                dve.wait_ge(ring["hi_done"], n)
                dve.tensor_tensor(ring["lo"][:, slot, :], ring["raw"][:, slot, :],
                                  ring["hi"][:, slot, :].bitcast(F32), ALU.subtract).then_inc(ring["lo_done"], 1)

            @block.scalar
            def _(act):
                def evict_t(i, j, wait=True):
                    if wait:
                        act.wait_ge(t_stored[j], 16 * i)
                    for b in range(NB):
                        act.wait_ge(t_mm, NB * (2 * i + j) + b + 1)
                        act.activation(out_t[:, j, b * BLK:(b + 1) * BLK], ps[3 * j + b][:, 0:BLK], ACT.Copy)\
                            .then_inc(t_out, 1)

                for j in range(2):
                    split_hi(act, wt, j, 1)
                if small:
                    split_hi(act, ws, 0, 1)
                for c in range(2):
                    split_hi(act, wk, c, 1)
                evict_t(0, 0, False)
                split_hi(act, wt, 0, 2, (t_mm, NB))
                evict_t(0, 1, False)
                split_hi(act, wt, 1, 2, (t_mm, 2 * NB))
                with act.Fori(1, loops - 1) as i:
                    for j in range(2):
                        evict_t(i, j)
                        split_hi(act, wt, j, i + 2, (t_mm, NB * (2 * i + j + 1)))
                for j in range(2):
                    evict_t(loops - 1, j)
                if small:
                    act.wait_ge(s_mm, 1)
                    act.activation(out_s[:, :, :], ps[0][:, 0:NT * small].rearrange("p (t n) -> p t n", n=small),
                                   ACT.Copy).then_inc(s_out, 1)
                for c in range(n_tok):
                    for i in range(NT):
                        n = c * NT + i
                        if i == 0 and 2 <= c + 1 < n_tok:
                            split_hi(act, wk, (c + 1) % 2, (c + 1) // 2 + 1, (k_mm, NT * c))
                        if n >= 2:
                            act.wait_ge(k_stored[n % 2], 16 * (n // 2))
                        act.wait_ge(k_mm, n + 1)
                        act.activation(out_tok[:, n % 2, :], ps[6 + n % 2][:, 0:TC], ACT.Copy).then_inc(k_out, 1)

            @block.vector
            def _(dve):
                for j in range(2):
                    split_lo(dve, wt, j, j + 1)
                if small:
                    split_lo(dve, ws, 0, 1)
                for c in range(2):
                    split_lo(dve, wk, c, c + 1)
                with dve.Fori(1, loops) as i:
                    for j in range(2):
                        split_lo(dve, wt, j, 2 * i + j + 1)
                for c in range(2, n_tok):
                    split_lo(dve, wk, c % 2, c + 1)

            @block.tensor
            def _(pe):
                def t_tile(i, j, wait=True):
                    pe.wait_ge(wt["lo_done"], 2 * i + j + 1)
                    for b in range(NB):
                        if wait:
                            pe.wait_ge(t_out, NB * (2 * i + j - 2) + b + 1)
                        for k in range(KT):
                            w, c = slice(k * P, (k + 1) * P), slice(b * BLK, (b + 1) * BLK)
                            last = split_matmul(pe, ps[3 * j + b][:, 0:BLK], wt["hi"][:, j, w], wt["lo"][:, j, w],
                                                h_hi[:, k, c], h_lo[:, k, c], k == 0, k == KT - 1)
                        last.then_inc(t_mm, 1)

                for j in range(2):
                    t_tile(0, j, False)
                with pe.Fori(1, loops) as i:
                    for j in range(2):
                        t_tile(i, j)
                if small:
                    pe.wait_ge(ws["lo_done"], 1)
                    pe.wait_ge(t_out, NB * n_t)
                    for i in range(NT):
                        for k in range(KT):
                            w, c = slice(k * small, (k + 1) * small), slice(i * P, (i + 1) * P)
                            last = split_matmul(pe, ps[0][:, i * small:(i + 1) * small], h_hi[:, k, c], h_lo[:, k, c],
                                                ws["hi"][:, 0, w], ws["lo"][:, 0, w], k == 0, k == KT - 1)
                    last.then_inc(s_mm, 1)
                for c in range(n_tok):
                    pe.wait_ge(wk["lo_done"], c + 1)
                    for i in range(NT):
                        n = c * NT + i
                        if n >= 2:
                            pe.wait_ge(k_out, n - 1)
                        for k in range(KT):
                            w, t = slice(k * TC, (k + 1) * TC), slice(i * P, (i + 1) * P)
                            last = split_matmul(pe, ps[6 + n % 2][:, 0:TC], h_hi[:, k, t], h_lo[:, k, t],
                                                wk["hi"][:, c % 2, w], wk["lo"][:, c % 2, w], k == 0, k == KT - 1)
                        last.then_inc(k_mm, 1)

            @block.gpsimd
            def _(pool):
                with pool.Fori(0, loops) as i:
                    for j in range(2):
                        pool.wait_ge(t_out, NB * (2 * i + j + 1))
                        pool.dma_start(u_t[bass.ds(2 * i + j, 1), :, :].rearrange("a p n -> p (a n)"),
                                       out_t[:, j, :]).then_inc(t_stored[j], 16)
                for c in range(n_tok):
                    for i in range(NT):
                        n = c * NT + i
                        pool.wait_ge(k_out, n + 1)
                        pool.dma_start(u_tok[i, :, c * TC:(c + 1) * TC], out_tok[:, n % 2, :])\
                            .then_inc(k_stored[n % 2], 16)
                for j in range(2):
                    pool.wait_ge(t_stored[j], 16 * loops)
                    pool.wait_ge(k_stored[j], 16 * ((n_tok * NT + 1 - j) // 2))
                if small:
                    pool.wait_ge(s_out, 1)
                    pool.dma_start(u_small, out_s[:, :, :]).then_inc(s_stored, 16)
                    pool.wait_ge(s_stored, 16)


def out_project(nc, tag, l, w_out, y_tok, ident, x_t, mods):
    with Scope(nc, tag) as s:
        y_hi, y_lo = s.sb("y_hi", [P, KT, TOK], F32R), s.sb("y_lo", [P, KT, TOK], F32R)
        w = load_split_ring(s, "w", KT * P)
        ps = s.banks(8)
        turned, y_hi_done, y_lo_done = s.sem("turned"), s.sem("y_hi_done"), s.sem("y_lo_done")
        mm, x_added = s.sem("mm"), s.sem("x_added")
        quads = [(k, i, min(3, NT - i)) for k in range(KT) for i in range(0, NT, 3)]
        with nc.Block() as block:
            @block.sync
            def _(sp):
                for n in range(KT):
                    if n >= 2:
                        sp.wait_ge(w["lo_done"], n - 1)
                    sp.dma_start(w["raw"][:, n % 2, :], w_out[n]).then_inc(w["arrived"][n % 2], 16)

            @block.scalar
            def _(act):
                def split(n):
                    act.wait_ge(w["arrived"][n % 2], 16 * (n // 2 + 1))
                    if n >= 2:
                        act.wait_ge(mm, NB * (n - 1))
                    act.activation(w["hi"][:, n % 2, :], w["raw"][:, n % 2, :], ACT.Copy).then_inc(w["hi_done"], 1)
                split(0)
                split(1)
                for n, (k, i, m) in enumerate(quads):
                    act.wait_ge(turned, n + 1)
                    act.activation(y_hi[:, k, i * P:(i + m) * P], ps[n % 2][:, 0:m * P], ACT.Copy)\
                        .then_inc(y_hi_done, 1)
                for n in range(2, KT):
                    split(n)

            @block.tensor
            def _(pe):
                for n, (k, i, m) in enumerate(quads):
                    if n >= 2:
                        pe.wait_ge(y_lo_done, n - 1)
                    for t in range(m):
                        last = pe.transpose(ps[n % 2][:, t * P:(t + 1) * P], y_tok[:, i + t, k * P:(k + 1) * P],
                                            ident[:, :])
                    last.then_inc(turned, 1)
                pe.wait_ge(y_lo_done, len(quads))
                for n in range(KT):
                    pe.wait_ge(w["lo_done"], n + 1)
                    for b in range(NB):
                        v = n * NB + b
                        if v >= 6:
                            pe.wait_ge(x_added, v - 5)
                        for k in range(KT):
                            c, t = slice(k * P, (k + 1) * P), slice(b * BLK, (b + 1) * BLK)
                            last = split_matmul(pe, ps[2 + v % 6][:, 0:BLK], w["hi"][:, n % 2, c], w["lo"][:, n % 2, c],
                                                y_hi[:, k, t], y_lo[:, k, t], k == 0, k == KT - 1)
                        last.then_inc(mm, 1)

            @block.vector
            def _(dve):
                def split(n):
                    dve.wait_ge(w["hi_done"], n + 1)
                    dve.tensor_tensor(w["lo"][:, n % 2, :], w["raw"][:, n % 2, :], w["hi"][:, n % 2, :].bitcast(F32),
                                      ALU.subtract).then_inc(w["lo_done"], 1)
                split(0)
                split(1)
                for n, (k, i, m) in enumerate(quads):
                    dve.wait_ge(y_hi_done, n + 1)
                    c = slice(i * P, (i + m) * P)
                    dve.tensor_tensor(y_lo[:, k, c], ps[n % 2][:, 0:m * P], y_hi[:, k, c].bitcast(F32), ALU.subtract)\
                        .then_inc(y_lo_done, 1)
                for n in range(KT):
                    for b in range(NB):
                        v = n * NB + b
                        dve.wait_ge(mm, v + 1)
                        for lo, hi, c in ((0, CTX, 0), (CTX, BLK, 1)) if b == 0 else ((b * BLK, (b + 1) * BLK, 1),):
                            last = dve.scalar_tensor_tensor(x_t[:, n, lo:hi], ps[2 + v % 6][:, lo - b * BLK:hi - b * BLK],
                                                            mod(mods, l, G1, n, c), x_t[:, n, lo:hi],
                                                            ALU.mult, ALU.add)
                        last.then_inc(x_added, 1)
                    if n + 2 < KT:
                        split(n + 2)


LE, GE, LT, GT_ = range(4)
SSD_H, SSD_P, SSD_G = 8, 64, 2
SSD_W = SSD_H * SSD_P
HG = SSD_H // SSD_G
LIN_H, LIN_K, LIN_V = 8, 64, 128
FWD, BWD = 0, 1


def scan_steps():
    steps, seen, last = [], set(), {}
    order = [(FWD, 0), (BWD, 0)]
    for c in range(1, NT):
        order += [(FWD, c), (BWD, NT - c)]
    for n, (way, c) in enumerate(order):
        state = way if c == 0 else 2 + way
        steps.append((way, c, state, c not in seen, last.get(state)))
        seen.add(c)
        last[state] = n
    return steps


def bcast(ap, n):
    return ap.rearrange("p (h a) -> p h a", a=1).to_broadcast([ap.shape[0], ap.shape[1], n])


def conv_rows(s, nc, d_u, n_tiles, ident, cw_src, kept, turned_out, ps):
    cw = s.sb("cw", [P, n_tiles, 4])
    u = s.sb("u", [P, 2, UPAD])
    acc = s.sb("acc", [P, 2, TOK])
    out = s.sb("act_out", [P, 2, TOK])
    ready, padded, tapped, active = s.sem("cw_ready"), s.sem("padded"), s.sem("tapped"), s.sem("active")
    arrived = [s.sem("u_arrived0"), s.sem("u_arrived1")]
    turned, copied = s.sem("turned"), s.sem("copied")
    parts = [(i, min(4, NT - i)) for i in range(0, NT, 4)]
    jobs = [(j, i, m) for j in range(n_tiles) if turned_out[j] for i, m in parts]
    upto = [sum(1 for q in jobs if q[0] <= j) for j in range(n_tiles)]

    def result(j):
        return kept[j] if kept[j] is not None else out[:, j % 2, :]

    def copy_out(act, j):
        for n, (jj, i, m) in enumerate(jobs):
            if jj == j:
                act.wait_ge(turned, n + 1)
                act.activation(turned_out[j](i, m), ps[n % 2][:, 0:m * P].rearrange("p (t n) -> p t n", n=P),
                               ACT.Copy).then_inc(copied, 1)

    with nc.Block() as block:
        @block.sync
        def _(sp):
            sp.dma_start(cw[:, :, :], cw_src).then_inc(ready, 16)
            sp.wait_ge(padded, 1)
            for j in range(n_tiles):
                if j >= 2:
                    sp.wait_ge(tapped, 6 * (j - 1))
                for a, b, at in URANGES:
                    sp.dma_start(u[:, j % 2, at:at + b - a], d_u[j, :, a:b]).then_inc(arrived[j % 2], 16)

        @block.vector
        def _(dve):
            dve.memset(u[:, :, :], 0.0).then_inc(padded, 1)
            dve.wait_ge(ready, 16)
            for j in range(n_tiles):
                dve.wait_ge(arrived[j % 2], 32 * (j // 2 + 1))
                if j >= 2:
                    dve.wait_ge(active, j - 1)
                for n in range(3):
                    if n:
                        dve.wait_ge(tapped, 6 * j + 2 * n)
                    for a, b, at in URANGES:
                        if n == 0:
                            op = dve.tensor_scalar(acc[:, j % 2, a:b], u[:, j % 2, at:at + b - a], cw[:, j, 1:2],
                                                   cw[:, j, 3:4], ALU.mult, ALU.add)
                        else:
                            off, tap = ((-1, 0), (1, 2))[n - 1]
                            op = dve.scalar_tensor_tensor(acc[:, j % 2, a:b], u[:, j % 2, at + off:at + off + b - a],
                                                          cw[:, j, tap:tap + 1], acc[:, j % 2, a:b],
                                                          ALU.mult, ALU.add)
                        op.then_inc(tapped, 1)

        @block.scalar
        def _(act):
            for j in range(n_tiles):
                act.wait_ge(tapped, 6 * (j + 1))
                if j >= 2 and upto[j - 2]:
                    act.wait_ge(turned, upto[j - 2])
                act.activation(result(j), acc[:, j % 2, :], ACT.Silu).then_inc(active, 1)
                if j >= 1:
                    copy_out(act, j - 1)
            copy_out(act, n_tiles - 1)

        @block.tensor
        def _(pe):
            for n, (j, i, m) in enumerate(jobs):
                pe.wait_ge(active, j + 1)
                if n >= 2:
                    pe.wait_ge(copied, n - 1)
                for t in range(m):
                    last = pe.transpose(ps[n % 2][:, t * P:(t + 1) * P], result(j)[:, (i + t) * P:(i + t + 1) * P],
                                        ident[:, :])
                last.then_inc(turned, 1)


def ssd(nc, tag, d, y_tok, ident, tri, ones, eps):
    steps = scan_steps()
    with Scope(nc, tag) as s:
        x_tok = s.sb("x_tok", [P, NT, SSD_W])
        k_tok = s.sb("k_tok", [P, NT, P])
        k_t, q_t = s.sb("k_t", [P, TOK]), s.sb("q_t", [P, TOK])
        dt, g = s.sb("dt", [P, NT, 2, SSD_H]), s.sb("g", [P, NT, 2, SSD_H])
        row = s.sb("row", [P, 2 * SSD_H * 2 + SSD_H + SSD_W])
        bias, a_log, skip = row[:, 0:16], row[:, 16:32], row[:, 32:40]
        norm_w = row[:, 40:40 + SSD_W]
        ps = s.banks(8)
        with Scope(nc, tag + "c") as c:
            conv_rows(c, nc, d["u0_t"], 6, ident, d["ssd_conv"],
                      [None] * 4 + [k_t[:, :], q_t[:, :]],
                      [lambda i, m, j=j: x_tok[:, i:i + m, j * P:(j + 1) * P] for j in range(4)]
                      + [lambda i, m: k_tok[:, i:i + m, :], None], ps)

        state = s.sb("state", [P, 4, HG * SSD_P])
        gu = s.sb("gu", [P, 2, SSD_H, P])
        w = s.sb("w", [P, 2, SSD_H, P])
        sm = s.sb("sm", [P, 2, SSD_G, P])
        xdt, xw = s.sb("xdt", [P, 2, SSD_W]), s.sb("xw", [P, 2, SSD_W])
        e3 = s.sb("e3", [P, 2, 3 * SSD_H])
        t1 = s.sb("t1", [P, 2, SSD_W])
        st = s.sb("st", [P, 3, NT * 2 * SSD_H])
        neg_a = s.sb("neg_a", [P, 2 * SSD_H])
        z = s.sb("z", [P, NT, SSD_W])
        dx = s.sb("dx", [P, SSD_W])
        ss, rs = s.sb("ss", [P, NT]), s.sb("rs", [P, 2, NT])
        row_in, dt_in, state_in, z_in = s.sem("row_in"), s.sem("dt_in"), s.sem("state_in"), s.sem("z_in")
        zeroed, dt_step, g_ready = s.sem("zeroed"), s.sem("dt_step"), s.sem("g_ready")
        gu_done, xdt_done, xw_done = s.sem("gu_done"), s.sem("xdt_done"), s.sem("xw_done")
        sums_mm, diff_mm, score_mm = s.sem("sums_mm"), s.sem("diff_mm"), s.sem("score_mm")
        exps_done, decay_done = s.sem("exps_done"), s.sem("decay_done")
        sm_done, w_done = s.sem("sm_done"), s.sem("w_done")
        intra_mm, inter_mm, state_mm = s.sem("intra_mm"), s.sem("inter_mm"), s.sem("state_mm")
        scaled, y_step, y_done, faded, s_done = (s.sem("scaled"), s.sem("y_step"), s.sem("y_done"), s.sem("faded"),
                                                 s.sem("s_done"))
        z_act, skipped, gated, squared, rooted, normed, out = (
            s.sem("z_act"), s.sem("skipped"), s.sem("gated"), s.sem("squared"), s.sem("rooted"), s.sem("normed"),
            s.sem("out"))
        n_steps = len(steps)
        with nc.Block() as block:
            @block.sync
            def _(sp):
                sp.dma_start(dt[:, :, :, :].rearrange("p t w h -> p (t w h)"), d["u0_small"]).then_inc(dt_in, 16)
                sp.dma_start(row[:, :], d["ssd_row"]).then_inc(row_in, 16)
                sp.dma_start(state[:, 2:4, :], d["ssd_state"]).then_inc(state_in, 16)
                sp.dma_start(z[:, :, :], d["u0_tok"][:, :, 0:SSD_W].rearrange("t p n -> p t n")).then_inc(z_in, 16)
                sp.wait_ge(s_done, 2)
                sp.dma_start(d["o_ssd"], state[:, 0:2, :]).then_inc(out, 16)
                sp.wait_ge(out, 16)

            @block.scalar
            def _(act):
                act.wait_ge(row_in, 16)
                act.activation(neg_a[:, :], a_log, ACT.Exp).then_inc(dt_step, 1)
                act.wait_ge(dt_step, 2)
                act.activation(st[:, 1, :], st[:, 0, :], ACT.Abs).then_inc(dt_step, 1)
                act.wait_ge(dt_step, 3)
                act.activation(st[:, 1, :], st[:, 1, :], ACT.Exp, scale=-1.0).then_inc(dt_step, 1)
                for n in range(n_steps):
                    act.wait_ge(sums_mm, n + 1)
                    if n >= 2:
                        act.wait_ge(s_done, n - 1)
                        act.wait_ge(scaled, n - 1)
                        act.wait_ge(xw_done, n - 1)
                    act.activation(e3[:, n % 2, :], ps[0][:, 0:3 * SSD_H], ACT.Exp).then_inc(exps_done, 1)
                    if n >= 2:
                        act.wait_ge(intra_mm, n - 1)
                    act.wait_ge(diff_mm, n + 1)
                    for b in range(2):
                        last = act.activation(w[:, n % 2, 4 * b:4 * b + 4, :].rearrange("p h t -> p (h t)"),
                                              ps[3 + b][:, :], ACT.Exp)
                    last.then_inc(decay_done, 1)
                act.wait_ge(z_in, 16)
                for c in range(NT):
                    act.activation(z[:, c, :], z[:, c, :], ACT.Silu).then_inc(z_act, 1)
                for c in range(NT):
                    act.wait_ge(gated, c + 1)
                    act.activation(z[:, c, :], y_tok[:, c, 0:SSD_W], ACT.Square, accum_out=ss[:, c:c + 1])\
                        .then_inc(squared, 1)
                act.wait_ge(squared, NT)
                act.activation(rs[:, 0, :], ss[:, :], ACT.Sqrt, bias=eps[:, 0:1], scale=1.0 / SSD_W)\
                    .then_inc(rooted, 1)

            @block.gpsimd
            def _(pool):
                pool.wait_ge(g_ready, 1)
                for n, (way, c, _, _, _) in enumerate(steps):
                    if n >= 2:
                        pool.wait_ge(diff_mm, n - 1)
                    m = tri[:, GE if way else LE, :].rearrange("p (a t) -> p a t", a=1).to_broadcast([P, SSD_H, P])
                    pool.tensor_tensor(gu[:, n % 2, :, :], m, bcast(g[:, c, way, :], P), ALU.mult)\
                        .then_inc(gu_done, 1)
                    if n >= 2:
                        pool.wait_ge(intra_mm, n - 1)
                    pool.tensor_tensor(xdt[:, n % 2, :].rearrange("p (h v) -> p h v", v=SSD_P),
                                       x_tok[:, c, :].rearrange("p (h v) -> p h v", v=SSD_P),
                                       bcast(dt[:, c, way, :], SSD_P), ALU.mult).then_inc(xdt_done, 1)
                    pool.wait_ge(exps_done, n + 1)
                    pool.wait_ge(xdt_done, n + 1)
                    if n >= 2:
                        pool.wait_ge(state_mm, n - 1)
                    pool.tensor_tensor(xw[:, n % 2, :].rearrange("p (h v) -> p h v", v=SSD_P),
                                       xdt[:, n % 2, :].rearrange("p (h v) -> p h v", v=SSD_P),
                                       bcast(e3[:, n % 2, SSD_H:2 * SSD_H], SSD_P), ALU.mult).then_inc(xw_done, 1)
                for c in range(NT):
                    if c >= 1:
                        pool.wait_ge(skipped, 2 * c)
                    pool.tensor_tensor(dx[:, :].rearrange("p (h v) -> p h v", v=SSD_P),
                                       x_tok[:, c, :].rearrange("p (h v) -> p h v", v=SSD_P),
                                       bcast(skip, SSD_P), ALU.mult).then_inc(skipped, 1)

            @block.tensor
            def _(pe):
                def sums(n):
                    way, c, _, _, _ = steps[n]
                    if n >= 1:
                        pe.wait_ge(exps_done, n)
                    gr = g[:, c, way, :]
                    for k, m in enumerate(((LE, GT_), (GE, LT))[way]):
                        pe.matmul(ps[0][:, k * SSD_H:(k + 1) * SSD_H], tri[:, m, :], gr, start=True, stop=True)
                    pe.matmul(ps[0][:, 2 * SSD_H:3 * SSD_H], ones[:, :], gr, start=True, stop=True)\
                        .then_inc(sums_mm, 1)
                    if n >= 1:
                        pe.wait_ge(sm_done, n)
                    if n >= 2:
                        pe.wait_ge(s_done, n - 1)
                    for q in range(SSD_G):
                        rows = slice(q * SSD_P, (q + 1) * SSD_P)
                        last = pe.matmul(ps[1 + q][:, 0:P], k_t[rows, c * P:(c + 1) * P],
                                         q_t[rows, c * P:(c + 1) * P], start=True, stop=True)
                    last.then_inc(score_mm, 1)
                    pe.wait_ge(gu_done, n + 1)
                    if n >= 1:
                        pe.wait_ge(decay_done, n)
                    for b in range(2):
                        last = pe.matmul(ps[3 + b][:, :], tri[:, LT if way else GT_, :],
                                         gu[:, n % 2, 4 * b:4 * b + 4, :].rearrange("p h t -> p (h t)"),
                                         start=True, stop=True)
                    last.then_inc(diff_mm, 1)

                def outputs(n):
                    way, c, st_, _, before = steps[n]
                    pe.wait_ge(w_done, n + 1)
                    pe.wait_ge(xdt_done, n + 1)
                    if n >= 1:
                        pe.wait_ge(y_done, n)
                    for h in range(SSD_H):
                        last = pe.matmul(ps[5][:, h * SSD_P:(h + 1) * SSD_P], w[:, n % 2, h, :],
                                         xdt[:, n % 2, h * SSD_P:(h + 1) * SSD_P], start=True, stop=True)
                    last.then_inc(intra_mm, 1)
                    if before is not None:
                        pe.wait_ge(s_done, before + 1)
                    if n >= 1:
                        pe.wait_ge(scaled, n)
                    for q in range(SSD_G):
                        rows = slice(q * SSD_P, (q + 1) * SSD_P)
                        last = pe.matmul(ps[6 + q][:, 0:256], q_t[rows, c * P:(c + 1) * P],
                                         state[rows, st_, :], start=True, stop=True)
                    last.then_inc(inter_mm, 1)
                    pe.wait_ge(xw_done, n + 1)
                    pe.wait_ge(sm_done, min(n + 2, n_steps))
                    for q in range(SSD_G):
                        rows = slice(q * SSD_P, (q + 1) * SSD_P)
                        last = pe.matmul(ps[1][rows, 256:512], k_tok[:, c, rows], xw[:, n % 2, q * 256:(q + 1) * 256],
                                         start=True, stop=True)
                    last.then_inc(state_mm, 1)

                pe.wait_ge(state_in, 16)
                pe.wait_ge(zeroed, 1)
                pe.wait_ge(g_ready, 1)
                sums(0)
                for n in range(n_steps):
                    if n + 1 < n_steps:
                        sums(n + 1)
                    outputs(n)

            @block.vector
            def _(dve):
                dve.memset(state[:, 0:2, :], 0.0).then_inc(zeroed, 1)
                dve.wait_ge(dt_in, 16)
                dve.wait_ge(dt_step, 1)
                n_dt = [1]

                def chain(op):
                    op.then_inc(dt_step, 1)
                    n_dt[0] += 1
                    dve.wait_ge(dt_step, n_dt[0])

                dt_r = dt[:, :, :, :].rearrange("p t w h -> p t (w h)")
                st_r = [st[:, j, :].rearrange("p (t n) -> p t n", t=NT) for j in range(3)]
                bias_b = bias.rearrange("p (a n) -> p a n", a=1).to_broadcast([P, NT, 2 * SSD_H])
                dve.tensor_tensor(st_r[0], dt_r, bias_b, ALU.add).then_inc(dt_step, 1)
                n_dt[0] = 4
                dve.wait_ge(dt_step, 4)
                chain(dve.tensor_scalar(st[:, 2, :], st[:, 1, :], 2.0, None, ALU.add))
                chain(dve.reciprocal(st[:, 2, :], st[:, 2, :]))
                chain(dve.tensor_tensor(st[:, 1, :], st[:, 1, :], st[:, 2, :], ALU.mult))
                chain(dve.tensor_tensor(st[:, 2, :], st[:, 1, :], st[:, 1, :], ALU.mult))
                poly = dt[:, :, :, :].rearrange("p t w h -> p (t w h)")
                chain(dve.tensor_scalar(poly, st[:, 2, :], 1.0 / 15, None, ALU.mult))
                for odd in (13, 11, 9, 7, 5, 3):
                    chain(dve.scalar_tensor_tensor(poly, poly, 1.0 / odd, st[:, 2, :], ALU.add, ALU.mult))
                chain(dve.scalar_tensor_tensor(poly, poly, 1.0, st[:, 1, :], ALU.add, ALU.mult))
                chain(dve.tensor_scalar(st[:, 0, :], st[:, 0, :], 0.0, None, ALU.max))
                chain(dve.scalar_tensor_tensor(poly, poly, 2.0, st[:, 0, :], ALU.mult, ALU.add))
                a_b = neg_a[:, :].rearrange("p (a n) -> p a n", a=1).to_broadcast([P, NT, 2 * SSD_H])
                dve.scalar_tensor_tensor(g[:, :, :, :].rearrange("p t w h -> p t (w h)"), dt_r, -1.0, a_b,
                                         ALU.mult, ALU.mult).then_inc(g_ready, 1)

                def weigh(n):
                    way, c, _, _, _ = steps[n]
                    dve.wait_ge(score_mm, n + 1)
                    if n >= 2:
                        dve.wait_ge(w_done, n - 1)
                    for q in range(SSD_G):
                        last = dve.tensor_tensor(sm[:, n % 2, q, :], ps[1 + q][:, 0:P],
                                                 tri[:, GE if way else LE, :], ALU.mult)
                    last.then_inc(sm_done, 1)
                    dve.wait_ge(decay_done, n + 1)
                    dve.wait_ge(sm_done, n + 1)
                    for q in range(SSD_G):
                        mb = sm[:, n % 2, q, :].rearrange("p (a t) -> p a t", a=1).to_broadcast([P, HG, P])
                        last = dve.tensor_tensor(w[:, n % 2, HG * q:HG * (q + 1), :],
                                                 w[:, n % 2, HG * q:HG * (q + 1), :], mb, ALU.mult)
                    last.then_inc(w_done, 1)

                ys = [0]

                def gather(n):
                    way, c, st_, first, _ = steps[n]
                    y = y_tok[:, c, 0:SSD_W]
                    dve.wait_ge(inter_mm, n + 1)
                    dve.wait_ge(exps_done, n + 1)
                    if n >= 2:
                        dve.wait_ge(y_done, n - 1)
                    for q in range(SSD_G):
                        last = dve.tensor_tensor(
                            t1[:, n % 2, q * 256:(q + 1) * 256].rearrange("p (h v) -> p h v", v=SSD_P),
                            ps[6 + q][:, 0:256].rearrange("p (h v) -> p h v", v=SSD_P),
                            bcast(e3[:, n % 2, q * HG:(q + 1) * HG], SSD_P), ALU.mult)
                    last.then_inc(scaled, 1)
                    for q in range(SSD_G):
                        rows = slice(q * SSD_P, (q + 1) * SSD_P)
                        e = e3[rows, n % 2, 2 * SSD_H + q * HG:2 * SSD_H + (q + 1) * HG]
                        sr = state[rows, st_, :].rearrange("p (h v) -> p h v", v=SSD_P)
                        dve.tensor_tensor(sr, sr, bcast(e, SSD_P), ALU.mult).then_inc(faded, 1)
                    dve.wait_ge(state_mm, n + 1)
                    dve.wait_ge(faded, 2 * n + 2)
                    dve.tensor_tensor(state[:, st_, :], state[:, st_, :], ps[1][:, 256:512], ALU.add)\
                        .then_inc(s_done, 1)
                    dve.wait_ge(intra_mm, n + 1)
                    dve.wait_ge(scaled, n + 1)
                    if first:
                        dve.tensor_tensor(y, t1[:, n % 2, :], ps[5][:, :], ALU.add).then_inc(y_done, 1)
                    else:
                        dve.tensor_tensor(t1[:, n % 2, :], t1[:, n % 2, :], ps[5][:, :], ALU.add)\
                            .then_inc(y_step, 1)
                        ys[0] += 1
                        dve.wait_ge(y_step, ys[0])
                        dve.tensor_tensor(y, y, t1[:, n % 2, :], ALU.add).then_inc(y_done, 1)

                weigh(0)
                for n in range(n_steps):
                    if n + 1 < n_steps:
                        weigh(n + 1)
                    if n == 0:
                        dve.wait_ge(zeroed, 1)
                        dve.wait_ge(state_in, 16)
                    before = steps[n][4]
                    if before is not None:
                        dve.wait_ge(s_done, before + 1)
                    gather(n)
                dve.wait_ge(y_done, n_steps)
                for c in range(NT):
                    y = y_tok[:, c, 0:SSD_W]
                    dve.wait_ge(skipped, 2 * c + 1)
                    dve.tensor_tensor(y, y, dx[:, :], ALU.add).then_inc(skipped, 1)
                    dve.wait_ge(skipped, 2 * c + 2)
                    dve.wait_ge(z_act, c + 1)
                    dve.tensor_tensor(y, y, z[:, c, :], ALU.mult).then_inc(gated, 1)
                dve.wait_ge(rooted, 1)
                dve.reciprocal(rs[:, 1, :], rs[:, 0, :]).then_inc(rooted, 1)
                dve.wait_ge(rooted, 2)
                for c in range(NT):
                    y = y_tok[:, c, 0:SSD_W]
                    dve.scalar_tensor_tensor(y, y, rs[:, 1, c:c + 1], norm_w, ALU.mult, ALU.mult).then_inc(normed, 1)


GRID_W, GRID_H = 64, LAT // 64
WIN_R, WIN_C = 8, 16
NA_H, NA_D = 8, 64
PAIRS = NA_H // 2
LOC = WIN_R * GRID_W
KEYS = LOC + CTX


def na(nc, tag, d, y_tok, ident, eps):
    units = [(r, p) for r in range(GRID_H) for p in range(PAIRS)] + [(None, h) for h in range(NA_H)]
    with Scope(nc, tag) as s:
        q_two = s.sb("q_two", [P, PAIRS, GRID_H, 2, GRID_W])
        q_ctx = s.sb("q_ctx", [P, PAIRS, CTX])
        k_t = s.sb("k_t", [P, PAIRS, TOK])
        k_old = s.sb("k_old", [P, PAIRS, CTX])
        bias = s.sb("bias", [P, PAIRS, 2 * WIN_R - 1, GRID_W])
        v_even, v_odd = s.sb("v_even", [P, 8, 512]), s.sb("v_odd", [P, 7, 512])
        v_ctx = s.sb("v_ctx", [P, 2, 512])
        ps = s.banks(8)
        loaded = s.sem("loaded")
        with Scope(nc, tag + "n") as c:
            u = c.sb("u", [P, 2, TOK])
            sq = c.sb("sq", [P, 2, TOK])
            root, inv = c.sb("root", [P, TOK]), c.sb("inv", [P, 1, TOK])
            half = c.sb("half", [P, P])
            gain = c.sb("gain", [P, 2])
            small, kept = c.sem("small"), c.sem("kept")
            arrived = [c.sem("arrived0"), c.sem("arrived1")]
            zeroed, squared, summed, rooted = c.sem("zeroed"), c.sem("squared"), c.sem("summed"), c.sem("rooted")
            inverted, normed, scaled = c.sem("inverted"), c.sem("normed"), c.sem("scaled")
            ends = [3 * min(j, PAIRS) + max(j - PAIRS, 0) for j in range(2 * PAIRS + 1)]
            with nc.Block() as block:
                @block.sync
                def _(sp):
                    sp.dma_start(half[:, :], d["half"]).then_inc(small, 16)
                    sp.dma_start(gain[:, :], d["qk_gain"]).then_inc(small, 16)
                    for j in range(2 * PAIRS):
                        if j >= 2:
                            sp.wait_ge(normed, ends[j - 1])
                        sp.dma_start(u[:, j % 2, :], d["u0_t"][6 + j]).then_inc(arrived[j % 2], 16)
                    tok = d["u0_tok"].rearrange("t p n -> (t p) n")
                    sp.dma_start(k_old[:, :, :], d["k_old"]).then_inc(loaded, 16)
                    sp.dma_start(bias[:, :, :, :], d["na_bias"]).then_inc(loaded, 16)
                    sp.dma_start(v_ctx[:, 0, :], d["v_old"]).then_inc(loaded, 16)
                    sp.dma_start(v_ctx[:, 1, :], tok[0:CTX, 512:1024]).then_inc(loaded, 16)
                    sp.dma_start(v_even[:, :, :], tok[CTX:TOK, 512:1024].rearrange("(t p) n -> p t n", p=P))\
                        .then_inc(loaded, 16)
                    sp.dma_start(v_odd[:, :, :], tok[CTX + 64:TOK - 64, 512:1024].rearrange("(t p) n -> p t n", p=P))\
                        .then_inc(loaded, 16)
                    sp.wait_ge(loaded, 96)
                    sp.dma_start(d["o_v"], v_ctx[:, 1, :]).then_inc(kept, 16)
                    sp.wait_ge(normed, ends[-1])
                    sp.dma_start(d["o_k"], k_t[:, :, 0:CTX]).then_inc(kept, 16)
                    sp.wait_ge(kept, 32)

                @block.gpsimd
                def _(pool):
                    pool.memset(q_two[:, :, :, :, :], 0.0).then_inc(zeroed, 1)

                @block.scalar
                def _(act):
                    def roots(j):
                        for b in range(NB):
                            act.wait_ge(summed, j + 1)
                            if j >= 1:
                                act.wait_ge(inverted, j)
                            act.activation(root[:, b * BLK:(b + 1) * BLK], ps[3 * (j % 2) + b][:, 0:BLK], ACT.Sqrt,
                                           bias=eps[:, 0:1], scale=1.0 / NA_D).then_inc(rooted, 1)
                    for j in range(2 * PAIRS):
                        act.wait_ge(arrived[j % 2], 16 * (j // 2 + 1))
                        if j >= 2:
                            act.wait_ge(summed, j - 1)
                        act.activation(sq[:, j % 2, :], u[:, j % 2, :], ACT.Square).then_inc(squared, 1)
                        if j >= 1:
                            roots(j - 1)
                    roots(2 * PAIRS - 1)

                @block.tensor
                def _(pe):
                    pe.wait_ge(small, 32)
                    for j in range(2 * PAIRS):
                        pe.wait_ge(squared, j + 1)
                        if j >= 2:
                            pe.wait_ge(rooted, NB * (j - 1))
                        for b in range(NB):
                            last = pe.matmul(ps[3 * (j % 2) + b][:, 0:BLK], half[:, :],
                                             sq[:, j % 2, b * BLK:(b + 1) * BLK], start=True, stop=True)
                        last.then_inc(summed, 1)

                @block.vector
                def _(dve):
                    dve.wait_ge(small, 32)
                    dve.tensor_scalar(gain[:, 0:1], gain[:, 0:1], NA_D ** -0.5, None, ALU.mult).then_inc(scaled, 1)
                    dve.wait_ge(scaled, 1)
                    dve.wait_ge(zeroed, 1)
                    for j in range(2 * PAIRS):
                        pair = j % PAIRS
                        dve.wait_ge(rooted, NB * (j + 1))
                        if j >= 1:
                            dve.wait_ge(normed, ends[j])
                        dve.reciprocal(inv[:, 0, :], root[:, :]).then_inc(inverted, 1)
                        dve.wait_ge(inverted, j + 1)
                        if j < PAIRS:
                            dve.scalar_tensor_tensor(q_ctx[:, pair, :], u[:, j % 2, 0:CTX], gain[:, 0:1],
                                                     inv[:, 0, 0:CTX], ALU.mult, ALU.mult).then_inc(normed, 1)
                            for e in range(2):
                                rows = slice(64 * e, 64 * e + 64)
                                shape = "p (r c) -> p r c"
                                dve.scalar_tensor_tensor(q_two[rows, pair, :, e, :],
                                                         u[rows, j % 2, CTX:TOK].rearrange(shape, c=GRID_W),
                                                         gain[rows, 0:1],
                                                         inv[rows, 0, CTX:TOK].rearrange(shape, c=GRID_W),
                                                         ALU.mult, ALU.mult).then_inc(normed, 1)
                        else:
                            dve.scalar_tensor_tensor(k_t[:, pair, :], u[:, j % 2, :], gain[:, 1:2], inv[:, 0, :],
                                                     ALU.mult, ALU.mult).then_inc(normed, 1)

        sc = s.sb("sc", [P, 3, KEYS])
        pt = s.sb("pt", [P, 2, 5, P])
        zero = s.sb("zero", [P, CTX])
        mx = s.sb("mx", [P, 3, 3])
        den = s.sb("den", [P, 2, 2])
        zeroed, scored, peak, biased = s.sem("zeroed"), s.sem("scored"), s.sem("peak"), s.sem("biased")
        exp_done, rec, weighed = s.sem("exp_done"), s.sem("rec"), s.sem("weighed")
        turned, copied, pv_mm, stored = s.sem("turned"), s.sem("copied"), s.sem("pv_mm"), s.sem("stored")
        n_units = len(units)

        def window(r):
            return min(max(r - WIN_R // 2, 0), GRID_H - WIN_R)

        with nc.Block() as block:
            @block.tensor
            def _(pe):
                pe.wait_ge(loaded, 96)

                def score(n):
                    r, p = units[n]
                    if n >= 2:
                        pe.wait_ge(biased, n - 1)
                    if r is None:
                        rows = slice(64 * (p % 2), 64 * (p % 2) + 64)
                        pe.matmul(ps[2 + n % 2][:, 0:CTX], q_ctx[rows, p // 2, :], k_t[rows, p // 2, 0:CTX],
                                  start=True, stop=True).then_inc(scored, 1)
                        return
                    q = q_two[:, p, r, :, :].rearrange("p e c -> p (e c)")
                    at = CTX + window(r) * GRID_W
                    pe.matmul(ps[n % 2][:, :], q, k_t[:, p, at:at + LOC], start=True, stop=True)
                    pe.matmul(ps[2 + n % 2][:, 0:CTX], q, k_old[:, p, :], start=True, stop=True).then_inc(scored, 1)

                def turn(n):
                    r, p = units[n]
                    pe.wait_ge(weighed, n + 1)
                    if n >= 1:
                        pe.wait_ge(copied, n)
                    for c in range(4 if r is None else 0, 5):
                        bank = ps[4][:, c * P:(c + 1) * P] if c < 4 else ps[5][:, 0:P]
                        last = pe.transpose(bank, sc[:, n % 3, c * P:(c + 1) * P], ident[:, :])
                    last.then_inc(turned, 1)

                def values(n):
                    r, p = units[n]
                    pe.wait_ge(copied, n + 1)
                    if n >= 2:
                        pe.wait_ge(stored, n - 1)
                    bank = ps[6 + n % 2]
                    if r is None:
                        pe.matmul(bank[:, 0:NA_D], pt[:, n % 2, 4, :], v_ctx[:, 1, p * NA_D:(p + 1) * NA_D],
                                  start=True, stop=True).then_inc(pv_mm, 1)
                        return
                    rs, rows = window(r), slice(64 * (r % 2), 64 * (r % 2) + 64)
                    tiles_ = [(v_odd if rs % 2 else v_even)[:, rs // 2 + c, :] for c in range(4)] + [v_ctx[:, 0, :]]
                    for e in range(2):
                        col = slice((2 * p + e) * NA_D, (2 * p + e + 1) * NA_D)
                        for c in range(5):
                            last = pe.matmul(bank[rows, e * NA_D:(e + 1) * NA_D], pt[:, n % 2, c, 64 * e:64 * e + 64],
                                             tiles_[c][:, col], start=(c == 0), stop=(c == 4))
                    last.then_inc(pv_mm, 1)

                for i in range(n_units + 3):
                    if i < n_units:
                        score(i)
                    if 0 <= i - 2 < n_units:
                        turn(i - 2)
                    if i >= 3:
                        values(i - 3)

            @block.vector
            def _(dve):
                dve.memset(zero[:, :], 0.0).then_inc(zeroed, 1)
                dve.wait_ge(zeroed, 1)
                dve.wait_ge(loaded, 96)
                peaks = [0]

                def scores(n):
                    r, p = units[n]
                    dve.wait_ge(scored, n + 1)
                    if n >= 3:
                        dve.wait_ge(turned, n - 2)
                    m = mx[:, n % 3, :]
                    first = m[:, 1:2] if r is None else m[:, 0:1]
                    dve.tensor_tensor_reduce(sc[:, n % 3, LOC:KEYS], ps[2 + n % 2][:, 0:CTX], zero[:, :], 1.0, -3e38,
                                             ALU.add, ALU.max, first).then_inc(peak, 1)
                    peaks[0] += 1
                    dve.wait_ge(peak, peaks[0])
                    if r is not None:
                        dr = window(r) - r + WIN_R - 1
                        dve.tensor_tensor_reduce(sc[:, n % 3, 0:LOC], ps[n % 2][:, :],
                                                 bias[:, p, dr:dr + WIN_R, :].rearrange("p a c -> p (a c)"), 1.0,
                                                 m[:, 0:1], ALU.add, ALU.max, m[:, 1:2]).then_inc(peak, 1)
                        peaks[0] += 1
                        dve.wait_ge(peak, peaks[0])
                    dve.tensor_scalar(m[:, 2:3], m[:, 1:2], -1.0, None, ALU.mult).then_inc(biased, 1)

                def weigh(n):
                    lo = 0 if units[n][0] is not None else LOC
                    dve.wait_ge(exp_done, n + 1)
                    dve.reciprocal(den[:, n % 2, 1:2], den[:, n % 2, 0:1]).then_inc(rec, 1)
                    dve.wait_ge(rec, n + 1)
                    dve.tensor_scalar(sc[:, n % 3, lo:KEYS], sc[:, n % 3, lo:KEYS], den[:, n % 2, 1:2], None,
                                      ALU.mult).then_inc(weighed, 1)

                for i in range(n_units + 1):
                    if i < n_units:
                        scores(i)
                    if i >= 1:
                        weigh(i - 1)

            @block.scalar
            def _(act):
                def exps(n):
                    lo = 0 if units[n][0] is not None else LOC
                    act.wait_ge(biased, n + 1)
                    if n >= 2:
                        act.wait_ge(weighed, n - 1)
                    act.activation(sc[:, n % 3, lo:KEYS], sc[:, n % 3, lo:KEYS], ACT.Exp, bias=mx[:, n % 3, 2:3],
                                   accum_out=den[:, n % 2, 0:1]).then_inc(exp_done, 1)

                def copy(n):
                    act.wait_ge(turned, n + 1)
                    if n >= 2:
                        act.wait_ge(pv_mm, n - 1)
                    if units[n][0] is not None:
                        act.activation(pt[:, n % 2, 0:4, :].rearrange("p c q -> p (c q)"), ps[4][:, :], ACT.Copy)
                    act.activation(pt[:, n % 2, 4, :], ps[5][:, 0:P], ACT.Copy).then_inc(copied, 1)

                def store(n):
                    r, p = units[n]
                    act.wait_ge(pv_mm, n + 1)
                    if r is None:
                        out, src = y_tok[:, 0, 512 + p * NA_D:512 + (p + 1) * NA_D], ps[6 + n % 2][:, 0:NA_D]
                    else:
                        rows = slice(64 * (r % 2), 64 * (r % 2) + 64)
                        out = y_tok[rows, 1 + r // 2, 512 + 2 * p * NA_D:512 + 2 * (p + 1) * NA_D]
                        src = ps[6 + n % 2][rows, 0:2 * NA_D]
                    act.activation(out, src, ACT.Copy).then_inc(stored, 1)

                for i in range(n_units + 3):
                    if i < n_units:
                        exps(i)
                    if 0 <= i - 2 < n_units:
                        copy(i - 2)
                    if i >= 3:
                        store(i - 3)


LIN_PAIRS = LIN_H // 2
RANK = 16
CH = 3
UW = CH * P
LEVELS = (64, 32, 16, 8, 4, 2, 1)
NL = len(LEVELS)


def lin_gates(nc, tag, d, ident):
    with Scope(nc, tag) as s:
        a_tok = s.sb("a_tok", [P, NT, 2 * RANK])
        a_t = s.sb("a_t", [2 * RANK, TOK])
        wa = s.sb("wa", [2 * RANK, 2, 2, P])
        vec = s.sb("vec", [P, 2, 2, 3])
        lb = s.sb("lb", [P, 4, 5])
        lw = s.sb("lw", [P, 4, 2])
        x = s.sb("x", [P, 4, TOK])
        neg, log1 = s.sb("neg", [P, 2, TOK]), s.sb("log1", [P, 2, TOK])
        g = s.sb("g", [P, 2, TOK])
        k = s.sb("k", [P, 2, TOK])
        ps = s.banks(8)
        small, arrived = s.sem("small"), s.sem("arrived")
        turned, copied, gate_mm = s.sem("turned"), s.sem("copied"), s.sem("gate_mm")
        bound, sig, f_done, k_done, ln_done = s.sem("bound"), s.sem("sig"), s.sem("f_done"), s.sem("k_done"), s.sem("ln_done")
        abs_done, exp_done, log_done, neg_done, g_done = (s.sem("abs_done"), s.sem("exp_done"), s.sem("log_done"),
                                                          s.sem("neg_done"), s.sem("g_done"))
        q_scaled, added = s.sem("q_scaled"), s.sem("added")
        st_k = [s.sem("st_k0"), s.sem("st_k1")]
        st_f = [s.sem(f"st_f{i}") for i in range(4)]
        st_g = [s.sem("st_g0"), s.sem("st_g1")]
        qs, q_in, st_q = s.sb("qs", [P, 2, TOK]), s.sem("q_in"), s.sem("st_q")
        with nc.Block() as block:
            @block.sync
            def _(sp):
                sp.dma_start(a_tok[:, :, :], d["u1_small"]).then_inc(small, 16)
                sp.dma_start(wa[:, :, :, :], d["wa2"]).then_inc(small, 16)
                sp.dma_start(vec[:, :, :, :], d["lin_vec"]).then_inc(small, 16)
                for j in range(4):
                    sp.dma_start(x[:, j, :], d["u1_t"][6 + j]).then_inc(arrived, 16)
                for j in range(2):
                    sp.dma_start(qs[:, j, :], d["u1_t"][j]).then_inc(q_in, 16)
                for j in range(4):
                    way, tile = divmod(j, 2)
                    sp.wait_ge(k_done, j + 1)
                    sp.dma_start(d["lin_k"][2 * tile + way], k[:, j % 2, :]).then_inc(st_k[j % 2], 16)
                sp.wait_ge(q_scaled, 2)
                for j in range(2):
                    sp.dma_start(d["lin_q"][j], qs[:, j, :]).then_inc(st_q, 16)
                for j in range(4):
                    way, tile = divmod(j, 2)
                    sp.wait_ge(ln_done, j + 1)
                    sp.dma_start(d["lin_g"][2 * (2 + tile) + way], x[:, j, :]).then_inc(st_f[j], 16)
                for j in range(4):
                    way, tile = divmod(j, 2)
                    sp.wait_ge(g_done, j + 1)
                    sp.dma_start(d["lin_g"][2 * tile + way], g[:, j % 2, :]).then_inc(st_g[j % 2], 16)
                for j in range(2):
                    sp.wait_ge(st_k[j], 32)
                    sp.wait_ge(st_g[j], 32)
                for j in range(4):
                    sp.wait_ge(st_f[j], 16)
                sp.wait_ge(st_q, 32)

            @block.tensor
            def _(pe):
                pe.wait_ge(small, 48)
                for i in range(NT):
                    last = pe.transpose(ps[i // 4][0:2 * RANK, i % 4 * P:(i % 4 + 1) * P], a_tok[:, i, :], ident[:, :])
                last.then_inc(turned, 1)
                pe.wait_ge(copied, 3)
                for j in range(4):
                    way, tile = divmod(j, 2)
                    if j >= 1:
                        pe.wait_ge(abs_done, 3 * j)
                        pe.wait_ge(neg_done, 3 * j)
                    for b in range(NB):
                        pe.matmul(ps[3 + b][:, 0:BLK], wa[:, way, tile, :], a_t[:, b * BLK:(b + 1) * BLK],
                                  start=True, stop=True).then_inc(gate_mm, 1)

            @block.scalar
            def _(act):
                act.wait_ge(turned, 1)
                for i in range(3):
                    w = min(4 * P, TOK - 4 * P * i)
                    act.activation(a_t[:, 4 * P * i:4 * P * i + w], ps[i][0:2 * RANK, 0:w], ACT.Copy).then_inc(copied, 1)
                act.wait_ge(bound, 2)
                act.activation(lw[:, :, :], lw[:, :, :], ACT.Exp).then_inc(bound, 1)
                act.wait_ge(arrived, 64)
                for j in range(4):
                    act.activation(x[:, j, :], x[:, j, :], ACT.Sigmoid).then_inc(sig, 1)
                act.wait_ge(q_in, 32)
                for j in range(2):
                    act.activation(qs[:, j, :], qs[:, j, :], ACT.Copy, scale=LIN_K ** -0.5).then_inc(q_scaled, 1)
                act.wait_ge(f_done, 8)
                act.wait_ge(k_done, 4)
                for j in range(4):
                    act.activation(x[:, j, :], x[:, j, :], ACT.Ln).then_inc(ln_done, 1)
                for j in range(4):
                    way, tile = divmod(j, 2)
                    if j >= 2:
                        act.wait_ge(added, j - 1)
                    for b in range(NB):
                        c = slice(b * BLK, (b + 1) * BLK)
                        act.wait_ge(gate_mm, 3 * j + b + 1)
                        act.activation(log1[:, j % 2, c], ps[3 + b][:, 0:BLK], ACT.Abs, bias=vec[:, way, tile, 0:1])\
                            .then_inc(abs_done, 1)
                    act.wait_ge(abs_done, 3 * j + 3)
                    act.wait_ge(neg_done, 3 * j + 3)
                    act.activation(log1[:, j % 2, :], log1[:, j % 2, :], ACT.Exp, scale=-1.0).then_inc(exp_done, 1)
                    act.wait_ge(exp_done, j + 1)
                    act.activation(log1[:, j % 2, :], log1[:, j % 2, :], ACT.Ln, bias=1.0).then_inc(log_done, 1)

            @block.vector
            def _(dve):
                dve.wait_ge(small, 48)
                v = vec[:, :, :, :].rearrange("p w t n -> p (w t) n")
                dve.tensor_tensor(lb[:, :, 0], v[:, :, 1], v[:, :, 2], ALU.max).then_inc(bound, 1)
                dve.wait_ge(bound, 1)
                dve.tensor_tensor(lw[:, :, :], v[:, :, 1:3], bcast(lb[:, :, 0], 2), ALU.subtract).then_inc(bound, 1)
                dve.wait_ge(bound, 3)
                dve.tensor_tensor(lb[:, :, 1], lw[:, :, 0], lw[:, :, 1], ALU.add).then_inc(bound, 1)
                dve.wait_ge(bound, 4)
                dve.reciprocal(lb[:, :, 2], lb[:, :, 1]).then_inc(bound, 1)
                dve.wait_ge(bound, 5)
                dve.tensor_tensor(lb[:, :, 3], lw[:, :, 1], lb[:, :, 2], ALU.mult).then_inc(bound, 1)
                dve.wait_ge(bound, 6)
                dve.tensor_scalar(lb[:, :, 4], lb[:, :, 3], -1.0, 1.0, ALU.mult, ALU.add).then_inc(bound, 1)
                dve.wait_ge(bound, 7)
                for j in range(4):
                    dve.wait_ge(sig, j + 1)
                    dve.tensor_scalar(x[:, j, :], x[:, j, :], lb[:, j, 4:5], lb[:, j, 3:4], ALU.mult, ALU.add)\
                        .then_inc(f_done, 1)
                    dve.wait_ge(f_done, j + 1)
                    if j >= 2:
                        dve.wait_ge(st_k[j % 2], 16)
                    dve.tensor_scalar(k[:, j % 2, :], x[:, j, :], -1.0, 1.0, ALU.mult, ALU.add).then_inc(k_done, 1)
                for j in range(4):
                    dve.wait_ge(k_done, 4)
                    dve.tensor_scalar(x[:, j, :], x[:, j, :], 2.0 ** -63, None, ALU.max).then_inc(f_done, 1)
                for j in range(4):
                    way, tile = divmod(j, 2)
                    if j >= 2:
                        dve.wait_ge(added, j - 1)
                    for b in range(NB):
                        c = slice(b * BLK, (b + 1) * BLK)
                        dve.wait_ge(gate_mm, 3 * j + b + 1)
                        dve.wait_ge(abs_done, 3 * j + b + 1)
                        dve.tensor_scalar(neg[:, j % 2, c], ps[3 + b][:, 0:BLK], vec[:, way, tile, 0:1], 0.0,
                                          ALU.add, ALU.min).then_inc(neg_done, 1)
                    dve.wait_ge(log_done, j + 1)
                    dve.wait_ge(neg_done, 3 * j + 3)
                    dve.tensor_tensor(neg[:, j % 2, :], neg[:, j % 2, :], log1[:, j % 2, :], ALU.subtract)\
                        .then_inc(added, 1)
                    dve.wait_ge(added, j + 1)
                    if j >= 2:
                        dve.wait_ge(st_g[j % 2], 16)
                    dve.tensor_scalar(g[:, j % 2, :], neg[:, j % 2, :], 1.0 / 16, None, ALU.mult).then_inc(g_done, 1)


def lin_units():
    out = []
    for pair in range(LIN_PAIRS):
        for way in range(2):
            for n in range(NT // CH):
                c0 = CH * n if way == FWD else NT - CH * (n + 1)
                out.append((pair, way, 2 * pair + way, c0, n))
    return out


def linear_scans(nc, tag, d, y_tok, ident):
    units = lin_units()
    n_units = len(units)
    per_item = NT // CH
    half = P // 2
    pieces = 3
    per_piece = (NL + 2) // pieces

    def piece(j):
        return (2 + j) // per_piece

    with Scope(nc, tag) as s:
        q, k, g = s.sb("q", [P, 2, TOK]), s.sb("k", [P, 2, TOK]), s.sb("g", [P, 2, TOK])
        v = s.sb("v", [P, 2, NT, 2 * LIN_V])
        reset = s.sb("reset", [P, TOK], BF16)
        run = s.sb("run", [P, 2, TOK])
        f = s.sb("f", [P, 2, NL + 2, UW])
        qz = s.sb("qz", [P, 2, NL, CH, 2, half])
        kq = s.sb("kq", [P, UW])
        q_in, k_end = s.sb("q_in", [P, 2, 2, UW]), s.sb("k_end", [P, UW])
        k_tok = s.sb("k_tok", [P, UW])
        sel = s.sb("sel", [P, 2])
        decay = s.sb("decay", [P, 2, CH])
        dot = s.sb("dot", [P, CH, 2])
        att = s.sb("att", [P, 2, CH, 2, P])
        state = s.sb("state", [P, 2, NT + 2, LIN_V])
        mask = s.sb("mask", [P, 2, NL, half], I16)
        ps = s.banks(8)
        masks_in = s.sem("masks_in")
        arrived = [s.sem("arrived0"), s.sem("arrived1")]
        kept = [s.sem("kept0"), s.sem("kept1")]
        zeroed, ran, inclusive, z_done = s.sem("zeroed"), s.sem("ran"), s.sem("inclusive"), s.sem("z_done")
        short, reset_done, sel_done = s.sem("short"), s.sem("reset_done"), s.sem("sel_done")
        expo, fact, mixed, ends = s.sem("expo"), s.sem("fact"), s.sem("mixed"), s.sem("ends")
        turned, k_copied, gain_mm, s_done = s.sem("turned"), s.sem("k_copied"), s.sem("gain_mm"), s.sem("s_done")
        q_done = s.sem("q_done")
        dotted, diag = s.sem("dotted"), s.sem("diag")
        score_mm, picked, out_mm = s.sem("score_mm"), s.sem("picked"), s.sem("out_mm")
        y_done = [s.sem("y_fwd"), s.sem("y_bwd")]

        def keep(sp, it):
            a, way = it % 2, it % 2
            sp.wait_ge(s_done, CH * (per_item * it + (1 if way == FWD else per_item)))
            sp.dma_start(d["o_lin"][it], state[:, a, NT, :]).then_inc(kept[a], 16)

        def blocks(ap, size):
            return ap.rearrange("p (b w) -> p b w", w=2 * size)

        def by_tile(ap, size, lo):
            return ap.rearrange("p (c b w) -> p c b w", c=CH, w=2 * size)[:, :, :, lo:lo + size]

        def rows_of(h):
            return slice(half * h, half * (h + 1))

        def q_row(way):
            return 0 if way == FWD else 1

        with nc.Block() as block:
            @block.sync
            def _(sp):
                sp.dma_start(mask[:, :, :, :], d["lin_mask"]).then_inc(masks_in, 16)
                sp.wait_ge(zeroed, 1)
                for it in range(2 * LIN_PAIRS):
                    pair, way = divmod(it, 2)
                    a = it % 2
                    if it >= 2:
                        sp.wait_ge(y_done[way], 2 * per_item * (it // 2))
                        sp.wait_ge(kept[a], 16 * (it // 2))
                    sp.dma_start(g[:, a, :], d["lin_g"][it]).then_inc(arrived[a], 16)
                    sp.dma_start(q[:, a, :], d["lin_q"][pair] if pair < 2 else d["u1_t"][2 + pair])\
                        .then_inc(arrived[a], 16)
                    sp.dma_start(k[:, a, :], d["u1_t"][2 + pair] if pair < 2 else d["lin_k"][it - 4])\
                        .then_inc(arrived[a], 16)
                    at = 2 * pair * LIN_V + (512 if pair >= 2 else 0)
                    sp.dma_start(v[:, a, :, :], d["u1_tok"][:, :, at:at + 2 * LIN_V].rearrange("t p n -> p t n"))\
                        .then_inc(arrived[a], 16)
                    sp.dma_start(state[:, a, 1 if way == FWD else NT - 1, :], d["lin_state"][it])\
                        .then_inc(arrived[a], 16)
                    if it >= 1:
                        keep(sp, it - 1)
                keep(sp, 2 * LIN_PAIRS - 1)
                for a in range(2):
                    sp.wait_ge(kept[a], 16 * LIN_PAIRS)

            @block.gpsimd
            def _(pool):
                pool.memset(state[:, :, 0, :], 0.0).then_inc(zeroed, 1)

                def level(n, j):
                    _, way, it, c0, _ = units[n]
                    size = LEVELS[j]
                    xb = blocks(run[:, it % 2, c0 * P:(c0 + CH) * P], size)
                    ob = blocks(f[:, n % 2, 2 + j, :], size)
                    mid = size - 1 if way == FWD else size
                    ref = xb[:, :, mid:mid + 1].to_broadcast([P, UW // (2 * size), size])
                    pool.tensor_tensor(ob[:, :, size:2 * size], xb[:, :, size:2 * size], ref, ALU.subtract)
                    return pool.tensor_tensor(ob[:, :, 0:size], ref, xb[:, :, 0:size], ALU.subtract)

                def free(n, p):
                    if n >= 2:
                        pool.wait_ge(score_mm, NL * (n - 2) + per_piece * (p + 1) - 2)

                def against_state(n):
                    _, way, it, c0, first = units[n]
                    cols = slice(c0 * P, (c0 + CH) * P)
                    xb = blocks(run[:, it % 2, cols], half)
                    gb = blocks(g[:, it % 2, cols], half)
                    out = blocks(f[:, n % 2, 1, :], half)
                    last = xb[:, :, P - 1:P].to_broadcast([P, CH, P])
                    instr = pool.tensor_tensor(out, last, xb, ALU.subtract)
                    if way == BWD:
                        own = gb[:, :, P - 1:P].to_broadcast([P, CH, P])
                        instr.then_inc(short, 1)
                        pool.wait_ge(short, it // 2 * per_item + first + 1)
                        pool.tensor_tensor(out, out, own, ALU.add)

                for n, (pair, way, it, c0, _) in enumerate(units):
                    a, r = it % 2, n % 2
                    cols = slice(c0 * P, (c0 + CH) * P)
                    pool.wait_ge(ran, it + 1)
                    free(n, 0)
                    if n >= 2:
                        pool.wait_ge(ends, n - 1)
                        pool.wait_ge(q_done, n - 1)
                    against_state(n)
                    level(n, 0).then_inc(expo, 1)
                    free(n, 1)
                    for j in range(1, NL):
                        if piece(j) != 1:
                            break
                        last = level(n, j)
                    last.then_inc(expo, 1)
                    if n >= 1:
                        pool.wait_ge(turned, n)
                    pool.tensor_tensor(kq[:, :], q[:, a, cols], k[:, a, cols], ALU.mult)
                    pool.wait_ge(fact, pieces * n + 1)
                    if n >= 2:
                        pool.wait_ge(s_done, CH * (n - 1))
                    at = P - 1 if way == FWD else 0
                    pool.tensor_copy(decay[:, r, :], f[:, r, q_row(way), at:UW:P])
                    pool.tensor_tensor(k_end[:, :], k[:, a, cols], f[:, r, 1 - q_row(way), :], ALU.mult)\
                        .then_inc(ends, 1)
                    free(n, 2)
                    for j in range(NL):
                        if piece(j) == 2:
                            last = level(n, j)
                    last.then_inc(expo, 1)

            @block.scalar
            def _(act):
                def factors(n, p):
                    _, way, it, c0, _ = units[n]
                    r = n % 2
                    act.wait_ge(expo, pieces * n + p + 1)
                    if p == 0:
                        if n >= 2:
                            act.wait_ge(ends, n - 1)
                            act.wait_ge(q_done, n - 1)
                        act.activation(f[:, r, 0, :], run[:, it % 2, c0 * P:(c0 + CH) * P], ACT.Exp)
                        rows = slice(1, per_piece)
                    else:
                        rows = slice(p * per_piece, (p + 1) * per_piece)
                    act.activation(f[:, r, rows, :], f[:, r, rows, :], ACT.Exp).then_inc(fact, 1)

                def diagonals(n):
                    act.wait_ge(turned, n + 1)
                    if n >= 1:
                        act.wait_ge(diag, n)
                    act.activation(dot[:, :, :], ps[6][:, UW:UW + 2 * CH].rearrange("p (c h) -> p c h", h=2), ACT.Copy)\
                        .then_inc(dotted, 1)
                    act.wait_ge(dotted, n + 1)
                    if n >= 2:
                        act.wait_ge(out_mm, 2 * (n - 1))
                    for c in range(CH):
                        for h in range(2):
                            last = act.activation(att[:, n % 2, c, h, :], ident[:, :], ACT.Copy,
                                                  scale=dot[:, c, h:h + 1])
                    last.then_inc(diag, 1)

                def copy_k(n):
                    act.wait_ge(turned, n + 1)
                    if n >= 1:
                        act.wait_ge(gain_mm, n)
                    act.activation(k_tok[:, :], ps[6][:, 0:UW], ACT.Copy).then_inc(k_copied, 1)

                def take(n):
                    pair, way, it, c0, _ = units[n]
                    if way == FWD:
                        for h in range(2):
                            act.wait_ge(out_mm, 2 * n + h + 1)
                            col = slice((2 * pair + h) * LIN_V, (2 * pair + h + 1) * LIN_V)
                            act.activation(y_tok[:, c0:c0 + CH, col],
                                           ps[4 + h][:, 0:UW].rearrange("p (a t) -> p a t", t=P), ACT.Copy)\
                                .then_inc(y_done[FWD], 1)

                for p in range(pieces):
                    factors(0, p)
                for n in range(n_units + 1):
                    if n < n_units:
                        copy_k(n)
                        diagonals(n)
                    if n + 1 < n_units:
                        factors(n + 1, 0)
                        factors(n + 1, 1)
                    if n >= 1:
                        take(n - 1)
                    if n + 1 < n_units:
                        factors(n + 1, 2)

            @block.tensor
            def _(pe):
                pe.wait_ge(masks_in, 16)
                pe.wait_ge(z_done, 4)
                pe.wait_ge(sel_done, 3)

                def turn(n):
                    pe.wait_ge(ends, n + 1)
                    if n >= 1:
                        pe.wait_ge(dotted, n)
                        pe.wait_ge(k_copied, n)
                    for c in range(CH):
                        pe.matmul(ps[6][:, UW + 2 * c:UW + 2 * c + 2], kq[:, c * P:(c + 1) * P], sel[:, :],
                                         start=True, stop=True)
                    for c in range(CH):
                        last = pe.transpose(ps[6][:, c * P:(c + 1) * P], k_end[:, c * P:(c + 1) * P], ident[:, :])
                    last.then_inc(turned, 1)

                def adds(n):
                    pair, way, it, c0, _ = units[n]
                    pe.wait_ge(k_copied, n + 1)
                    pe.wait_ge(arrived[it % 2], 80 * (it // 2 + 1))
                    if n >= 1:
                        pe.wait_ge(s_done, CH * n)
                    for c in range(CH):
                        for h in range(2):
                            last = pe.matmul(ps[7][rows_of(h), c * P:(c + 1) * P],
                                             k_tok[:, c * P + half * h:c * P + half * (h + 1)],
                                             v[:, it % 2, c0 + c, h * LIN_V:(h + 1) * LIN_V], start=True, stop=True)
                    last.then_inc(gain_mm, 1)

                def score(n, j):
                    m = NL * n + j
                    pe.wait_ge(mixed, m + 1)
                    if m >= 4:
                        pe.wait_ge(picked, m - 3)
                    for c in range(CH):
                        last = pe.matmul(ps[m % 4][:, c * P:(c + 1) * P], f[:, n % 2, 2 + j, c * P:(c + 1) * P],
                                         qz[:, n % 2, j, c, :, :].rearrange("p h t -> p (h t)"),
                                         start=True, stop=True)
                    last.then_inc(score_mm, 1)

                def outputs(n, h):
                    pair, way, it, c0, _ = units[n]
                    pe.wait_ge(picked, NL * (n + 1))
                    pe.wait_ge(q_done, n + 1)
                    pe.wait_ge(s_done, CH * (n + 1))
                    if n >= 1:
                        before = units[n - 1]
                        pe.wait_ge(y_done[before[1]], 2 * (before[0] * per_item + before[4]) + h + 1)
                    for c in range(CH):
                        out = ps[4 + h][:, c * P:(c + 1) * P]
                        pe.matmul(out, att[:, n % 2, c, h, :],
                                  v[:, it % 2, c0 + c, h * LIN_V:(h + 1) * LIN_V], start=True, stop=False)
                        last = pe.matmul(out, q_in[:, n % 2, h, c * P:(c + 1) * P],
                                         state[:, it % 2, c0 + c, :], start=False, stop=True)
                    last.then_inc(out_mm, 1)

                for n in range(n_units + 1):
                    if n < n_units:
                        turn(n)
                        for j in range(NL):
                            score(n, j)
                            if j == 2:
                                adds(n)
                            if n >= 1 and j in (3, 5):
                                outputs(n - 1, (j - 3) // 2)
                    else:
                        for h in range(2):
                            outputs(n - 1, h)

            @block.vector
            def _(dve):
                dve.wait_ge(masks_in, 16)
                dve.wait_ge(zeroed, 1)
                dve.memset(sel[:, :], 0.0).then_inc(sel_done, 1)
                dve.memset(reset[:, :], 1.0).then_inc(reset_done, 1)
                dve.wait_ge(sel_done, 1)
                for h in range(2):
                    dve.memset(sel[rows_of(h), h:h + 1], 1.0).then_inc(sel_done, 1)
                dve.wait_ge(reset_done, 1)
                dve.memset(reset[:, 0:TOK:P], 0.0).then_inc(reset_done, 1)
                dve.wait_ge(reset_done, 2)

                def sums(it):
                    a, way = it % 2, it % 2
                    dve.wait_ge(arrived[a], 80 * (it // 2 + 1))
                    if it >= 2:
                        dve.wait_ge(fact, pieces * per_item * (it - 1))
                    dve.tensor_tensor_scan(run[:, a, :], reset[:, :], g[:, a, :], 0.0, ALU.mult, ALU.add)\
                        .then_inc(ran if way == FWD else inclusive, 1)
                    if way == BWD:
                        dve.wait_ge(inclusive, it // 2 + 1)
                        dve.tensor_tensor(run[:, a, :], run[:, a, :], g[:, a, :], ALU.subtract).then_inc(ran, 1)

                def mix(n, j):
                    pair, way, it, c0, _ = units[n]
                    size, r, a = LEVELS[j], n % 2, it % 2
                    cols = slice(c0 * P, (c0 + CH) * P)
                    dve.wait_ge(fact, pieces * n + piece(j) + 1)
                    if n >= 2:
                        dve.wait_ge(score_mm, NL * (n - 2) + j + 1)
                    late, early = (size, 0) if way == FWD else (0, size)
                    for h in range(2):
                        rows = rows_of(h)
                        dve.tensor_tensor(qz[rows, r, j, :, h, :].rearrange("p c (b w) -> p c b w", w=size),
                                          by_tile(q[rows, a, cols], size, late),
                                          by_tile(f[rows, r, 2 + j, :], size, late), ALU.mult)
                    kf = by_tile(f[:, r, 2 + j, :], size, early)
                    dve.tensor_tensor(kf, by_tile(k[:, a, cols], size, early), kf, ALU.mult).then_inc(mixed, 1)

                def q_ins(n):
                    pair, way, it, c0, _ = units[n]
                    dve.wait_ge(fact, pieces * n + 1)
                    if n >= 2:
                        dve.wait_ge(out_mm, 2 * (n - 1))
                    for h in range(2):
                        last = dve.tensor_tensor(q_in[rows_of(h), n % 2, h, :],
                                                 q[rows_of(h), it % 2, c0 * P:(c0 + CH) * P],
                                                 f[rows_of(h), n % 2, q_row(way), :], ALU.mult)
                    last.then_inc(q_done, 1)

                def pick(n, j):
                    way, m, size = units[n][1], NL * n + j, LEVELS[j]
                    dve.wait_ge(score_mm, m + 1)
                    if j == 0:
                        dve.wait_ge(diag, n + 1)
                    else:
                        dve.wait_ge(picked, m)
                    late = size if way == FWD else 0
                    out = att[:, n % 2, :, :, :].rearrange("p c h (b w) -> p (c h) b w", w=2 * size)
                    msk = mask[:, way, j, :].rearrange("p (a b w) -> p a b w", a=1, w=size)
                    dve.copy_predicated(out[:, :, :, late:late + size],
                                        msk.to_broadcast([P, 2 * CH, half // size, size]),
                                        ps[m % 4][:, 0:UW].rearrange("p (a b w) -> p a b w", a=2 * CH, w=size))\
                        .then_inc(picked, 1)

                def states(n):
                    pair, way, it, c0, _ = units[n]
                    a = it % 2
                    dve.wait_ge(gain_mm, n + 1)
                    for i in range(CH):
                        c = c0 + i if way == FWD else c0 + CH - 1 - i
                        src = 0 if c == 0 else c
                        dst = NT if c == 0 else (c + 1 if way == FWD else c - 1)
                        if c == (NT - 1 if way == FWD else 1):
                            dst = NT + 1
                        if CH * n + i:
                            dve.wait_ge(s_done, CH * n + i)
                        dve.scalar_tensor_tensor(state[:, a, dst, :], state[:, a, src, :],
                                                 decay[:, n % 2, c - c0:c - c0 + 1],
                                                 ps[7][:, (c - c0) * P:(c - c0 + 1) * P], ALU.mult, ALU.add)\
                            .then_inc(s_done, 1)

                def take(n):
                    pair, way, it, c0, _ = units[n]
                    if way == BWD:
                        for h in range(2):
                            dve.wait_ge(out_mm, 2 * n + h + 1)
                            col = slice((2 * pair + h) * LIN_V, (2 * pair + h + 1) * LIN_V)
                            y = y_tok[:, c0:c0 + CH, col]
                            dve.tensor_tensor(y, y, ps[4 + h][:, 0:UW].rearrange("p (a t) -> p a t", t=P), ALU.add)\
                                .then_inc(y_done[BWD], 1)

                sums(0)
                for h in range(2):
                    dve.memset(q_in[rows_of(1 - h), :, h, :], 0.0).then_inc(z_done, 1)
                    dve.memset(qz[rows_of(1 - h), :, :, :, h, :], 0.0).then_inc(z_done, 1)
                for j in range(NL):
                    mix(0, j)
                q_ins(0)
                for n in range(n_units + 1):
                    if n < n_units:
                        if n % per_item == per_item - 2 and n // per_item + 1 < 2 * LIN_PAIRS:
                            sums(n // per_item + 1)
                        for j in range(NL):
                            if n + 1 < n_units:
                                mix(n + 1, j)
                            pick(n, j)
                        states(n)
                        if n + 1 < n_units:
                            q_ins(n + 1)
                    if n >= 1:
                        take(n - 1)


def lin_finish(nc, tag, d, y_tok, eps):
    with Scope(nc, tag) as s:
        gate = s.sb("gate", [P, 3, D])
        norm_w = s.sb("norm_w", [P, D])
        sq = s.sb("sq", [P, 2, D])
        ss, root, inv = s.sb("ss", [P, NT, LIN_H]), s.sb("root", [P, NT, LIN_H]), s.sb("inv", [P, NT, LIN_H])
        w_in, arrived = s.sem("w_in"), [s.sem(f"arrived{i}") for i in range(3)]
        squared, summed, rooted, inverted = s.sem("squared"), s.sem("summed"), s.sem("rooted"), s.sem("inverted")
        active, weighed, normed, done = s.sem("active"), s.sem("weighed"), s.sem("normed"), s.sem("done")
        with nc.Block() as block:
            @block.sync
            def _(sp):
                sp.dma_start(norm_w[:, :], d["lin_norm"]).then_inc(w_in, 16)
                for c in range(NT):
                    if c >= 3:
                        sp.wait_ge(done, c - 2)
                    for half in range(2):
                        sp.dma_start(gate[:, c % 3, half * 512:(half + 1) * 512],
                                     d["u1_tok"][c, :, half * D + 512:half * D + D]).then_inc(arrived[c % 3], 16)

            @block.scalar
            def _(act):
                for c in range(NT):
                    if c >= 2:
                        act.wait_ge(summed, c - 1)
                    act.activation(sq[:, c % 2, :], y_tok[:, c, :], ACT.Square).then_inc(squared, 1)
                act.wait_ge(summed, NT)
                act.activation(root[:, :, :], ss[:, :, :], ACT.Sqrt, bias=eps[:, 0:1], scale=1.0 / LIN_V)\
                    .then_inc(rooted, 1)
                for c in range(NT):
                    act.wait_ge(arrived[c % 3], 32 * (c // 3 + 1))
                    act.activation(gate[:, c % 3, :], gate[:, c % 3, :], ACT.Silu).then_inc(active, 1)

            @block.gpsimd
            def _(pool):
                pool.wait_ge(w_in, 16)
                for c in range(NT):
                    pool.wait_ge(active, c + 1)
                    pool.tensor_tensor(gate[:, c % 3, :], gate[:, c % 3, :], norm_w[:, :], ALU.mult)\
                        .then_inc(weighed, 1)

            @block.vector
            def _(dve):
                for c in range(NT):
                    dve.wait_ge(squared, c + 1)
                    dve.tensor_reduce(ss[:, c, :], sq[:, c % 2, :].rearrange("p (h v) -> p h v", v=LIN_V), AX.X,
                                      ALU.add).then_inc(summed, 1)
                dve.wait_ge(rooted, 1)
                dve.reciprocal(inv[:, :, :], root[:, :, :]).then_inc(inverted, 1)
                dve.wait_ge(inverted, 1)
                for c in range(NT):
                    y = y_tok[:, c, :]
                    yh = y.rearrange("p (h v) -> p h v", v=LIN_V)
                    dve.tensor_tensor(yh, yh, bcast(inv[:, c, :], LIN_V), ALU.mult).then_inc(normed, 1)
                    dve.wait_ge(normed, c + 1)
                    dve.wait_ge(weighed, c + 1)
                    dve.tensor_tensor(y, y, gate[:, c % 3, :], ALU.mult).then_inc(done, 1)


def trunk(nc, d):
    def dram(name, shape):
        d[name] = nc.dram_tensor(name, shape, F32).ap()

    dram("u0_t", (14, P, TOK))
    dram("u0_tok", (NT, P, 1024))
    dram("u0_small", (P, NT * 16))
    dram("u1_t", (10, P, TOK))
    dram("u1_tok", (NT, P, 2048))
    dram("u1_small", (P, NT, 32))
    dram("lin_g", (8, P, TOK))
    dram("lin_k", (4, P, TOK))
    dram("lin_q", (2, P, TOK))
    with Scope(nc, "all") as s:
        x_t = s.sb("x_t", [P, KT, TOK])
        mods = s.sb("mods", [P, DEPTH * ADA, 2])
        gains = s.sb("gains", [P, DEPTH, 2, KT, 2])
        ones, ident, eps = s.sb("ones", [P, P]), s.sb("ident", [P, P]), s.sb("eps", [P, 1])
        x_in, filled, out = s.sem("x_in"), s.sem("filled"), s.sem("out")
        u_stored = [[s.sem(f"u{l}_stored{i}", True) for i in range(5)] for l in range(DEPTH)]
        with nc.Block() as block:
            @block.sync
            def _(sp):
                sp.dma_start(x_t[:, :, :], d["x_t"]).then_inc(x_in, 16)
                sp.dma_start(ident[:, :], d["ident"]).then_inc(x_in, 16)
                sp.wait_ge(x_in, 32)

            @block.vector
            def _(dve):
                dve.memset(ones[:, :], 1.0).then_inc(filled, 1)
                dve.memset(eps[:, :], EPS).then_inc(filled, 1)
                dve.wait_ge(filled, 2)
        modulation(nc, d, mods, gains)
        for l in range(DEPTH):
            with Scope(nc, f"hm{l}") as hs:
                h_hi, h_lo = hs.sb("h_hi", [P, KT, TOK], F32R), hs.sb("h_lo", [P, KT, TOK], F32R)
                norm(nc, f"n{l}a", l, 0, x_t, ones, eps, mods, gains, h_hi, h_lo)
                small = d["u0_small"].rearrange("p (t n) -> p t n", n=16) if l == 0 else d["u1_small"]
                in_project(nc, f"in{l}", u_stored[l], d[f"w{l}_t"], d[f"w{l}_tok"], d[f"w{l}_small"], h_hi, h_lo, d[f"u{l}_t"],
                           d[f"u{l}_tok"], small)
            if l == 1:
                lin_gates(nc, "gates", d, ident)
            with Scope(nc, f"mix{l}") as ms:
                y_tok = ms.sb("y", [P, NT, D])
                if l == 0:
                    with Scope(nc, "masks") as t:
                        tri = t.sb("tri", [P, 4, P])
                        tri_in = t.sem("tri_in")
                        with nc.Block() as block:
                            @block.sync
                            def _(sp):
                                sp.dma_start(tri[:, :, :], d["tri"]).then_inc(tri_in, 16)
                                sp.wait_ge(tri_in, 16)
                        ssd(nc, "ssd", d, y_tok, ident, tri, ones, eps)
                    na(nc, "na", d, y_tok, ident, eps)
                else:
                    linear_scans(nc, "lin", d, y_tok, ident)
                    lin_finish(nc, "fin", d, y_tok, eps)
                out_project(nc, f"out{l}", l, d["w_out"][l], y_tok, ident, x_t, mods)
            with Scope(nc, f"hf{l}") as hs:
                h_hi, h_lo = hs.sb("h_hi", [P, KT, TOK], F32R), hs.sb("h_lo", [P, KT, TOK], F32R)
                norm(nc, f"n{l}b", l, 1, x_t, ones, eps, mods, gains, h_hi, h_lo)
                conv_ffn(nc, f"ffn{l}", l, d, x_t, mods, h_hi, h_lo)
        with nc.Block() as block:
            @block.sync
            def _(sp):
                sp.dma_start(d["o_x"], x_t[:, :, :]).then_inc(out, 16)
                sp.wait_ge(out, 16)


def t_form(a):
    return a.reshape(a.shape[0], -1, P).transpose(2, 1, 0)


def tiles(w, cols=P):
    k, n = w.shape
    return w.reshape(k // P, P, n // cols, cols).transpose(2, 1, 0, 3).reshape(n // cols, P, k // P * cols)


def layout(np, i):
    o = {}
    rows = np.concatenate([i["x_prompt"].reshape(CTX, D), i["x_sample"].reshape(LAT, D)], axis=0)
    o["x_t"] = t_form(rows)
    o["c_t"] = t_form(np.stack([i["c_ctx"], i["c"].reshape(D)]))
    o["w_ada"] = np.stack([tiles(w) for w in i["w_ada"]]).reshape(DEPTH * ADA // 4, 4, P, KT, P)
    twice = lambda a: np.stack([a, a], axis=-1)
    o["b_ada"] = twice(i["b_ada"].reshape(DEPTH * ADA, P).transpose(1, 0))
    o["norm_w"] = twice(i["norm_w"].reshape(DEPTH, 2, KT, P).transpose(3, 0, 1, 2))
    up = np.stack([tiles(w) for w in i["ffn_w_up"]]).reshape(DEPTH, 2, FT, P, D)
    o["w_up"] = up.transpose(0, 2, 1, 3, 4).reshape(DEPTH, 2 * FT, P, D)
    o["w_down"] = i["ffn_w_down"].reshape(DEPTH, FT, P, D)
    taps = np.concatenate([i["ffn_conv_w"], i["ffn_conv_b"][:, None]], axis=1)
    o["ffn_conv"] = taps.reshape(DEPTH, 4, 2, FT, P).transpose(0, 4, 3, 2, 1)
    w0 = i["w_in_l0"]
    o["w0_t"] = tiles(np.concatenate([w0[:, 512:1280], w0[:, 1296:2320]], axis=1))
    o["w0_tok"] = tiles(np.concatenate([w0[:, 0:512], w0[:, 2320:2832]], axis=1), 256)
    o["w0_small"] = w0[:, 1280:1296].reshape(KT, P, 16).transpose(1, 0, 2)
    o["w_out"] = np.stack([tiles(i["w_out_l0"]), tiles(i["w_out_l1"])])
    taps = np.concatenate([i["ssd_conv_w_l0"], i["ssd_conv_b_l0"][None]])
    o["ssd_conv"] = taps.reshape(4, 6, P).transpose(2, 1, 0)
    row = np.concatenate([i["ssd_dt_bias_l0"].reshape(16), i["ssd_a_log_l0"].reshape(16), i["ssd_d_l0"],
                          i["ssd_norm_w_l0"]])
    o["ssd_row"] = np.repeat(row[None], P, axis=0)
    st = np.stack([i["state_ssd_fwd_l0"], i["state_ssd_bwd_l0"]]).reshape(2, 2, 4, 64, 64)
    o["ssd_state"] = st.transpose(1, 3, 0, 2, 4).reshape(P, 2, 256)
    r = np.arange(P)
    o["tri"] = np.stack([r[:, None] <= r, r[:, None] >= r, r[:, None] < r, r[:, None] > r], axis=1).astype(np.float32)
    o["ident"] = np.eye(P, dtype=np.float32)
    o["half"] = np.kron(np.eye(2), np.ones((64, 64))).astype(np.float32)
    o["qk_gain"] = np.tile(np.stack([i["na_q_norm_l0"], i["na_k_norm_l0"]], axis=1), (2, 1))
    o["k_old"] = i["cache_na_k_l0"].reshape(4, 2, P, 64).transpose(1, 3, 0, 2).reshape(P, 4, P)
    o["v_old"] = i["cache_na_v_l0"].reshape(8, P, 64).transpose(1, 0, 2).reshape(P, 512)
    q, k = np.arange(64)[:, None], np.arange(64)[None]
    start = np.clip(q - 8, 0, 48)
    rel = i["na_rpb_l0"][:, :, np.clip(k - q, -15, 15) + 15]
    rel = np.where((k >= start) & (k < start + 16), rel, np.float32(-1e30))
    o["na_bias"] = rel.reshape(4, 2, 15, 64, 64).transpose(1, 3, 0, 2, 4).reshape(P, 4, 15, 64)
    w1 = i["w_in_l1"]
    o["w1_t"] = tiles(np.concatenate([w1[:, 0:512], w1[:, 1568:2336]], axis=1))
    o["w1_tok"] = tiles(np.concatenate([w1[:, 512:1536], w1[:, 2336:3360]], axis=1), 256)
    o["w1_small"] = w1[:, 1536:1568].reshape(KT, P, 32).transpose(1, 0, 2)
    wa = i["gla_wa2_l1"].reshape(2, 16, 2, P)
    zero = np.zeros((16, 2, P), np.float32)
    o["wa2"] = np.stack([np.concatenate([wa[0], zero]), np.concatenate([zero, wa[1]])], axis=1)
    lin = np.concatenate([i["gla_ba2_l1"][:, None], i["hgrn_lb_logits"]], axis=1)
    o["lin_vec"] = lin.reshape(2, 3, 2, P).transpose(3, 0, 2, 1)
    s_idx, t_idx = r[:, None], r[None]
    fwd = [(s_idx // (2 * b) == t_idx // (2 * b)) & (s_idx // b % 2 == 0) & (t_idx // b % 2 == 1)
                              for b in LEVELS]
    fwd = np.stack(fwd)
    later = [np.array([t for t in range(P) if t // b % 2 == 1]) for b in LEVELS]
    sooner = [np.array([t for t in range(P) if t // b % 2 == 0]) for b in LEVELS]
    o["lin_mask"] = np.stack([np.stack([m[:, t] for m, t in zip(fwd, later)]),
                              np.stack([m.T[:, t] for m, t in zip(fwd, sooner)])]).transpose(2, 0, 1, 3).astype(np.int16)
    st = np.stack([np.stack([i[f"state_{m}_{w}_l1"].reshape(4, 64, 128) for w in ("fwd", "bwd")])
                   for m in ("gla", "hgrn")])
    o["lin_state"] = st.reshape(2, 2, 2, P, 128).transpose(0, 2, 1, 3, 4).reshape(8, P, 128)
    o["lin_norm"] = np.repeat(np.concatenate([np.tile(i["gla_norm_w_l1"], 4), np.tile(i["hgrn_norm_w_l1"], 4)])[None],
                              P, axis=0)
    return {k: np.ascontiguousarray(v) for k, v in o.items()}


OUTS = {"o_x": (P, KT, TOK), "o_k": (P, 4, P), "o_v": (P, 512), "o_ssd": (P, 2, 256), "o_lin": (8, P, P)}


def kernel(**inputs):
    import numpy as np
    import concourse.bacc as bacc
    from concourse.bass_utils import run_bass_kernel_spmd

    arrays = layout(np, {k: np.asarray(v) for k, v in inputs.items()})
    nc = bacc.Bacc("TRN2", target_bir_lowering=False, num_devices=1)
    d = {n: nc.dram_tensor(n, a.shape, mybir.dt.from_np(a.dtype), kind="ExternalInput").ap()
         for n, a in arrays.items()}
    d.update({n: nc.dram_tensor(n, shape, F32, kind="ExternalOutput").ap() for n, shape in OUTS.items()})
    trunk(nc, d)
    r = run_bass_kernel_spmd(nc, [arrays], core_ids=[0]).results[0]

    y = r["o_x"].transpose(2, 1, 0).reshape(TOK, D)
    na_k = r["o_k"].reshape(2, 64, 4, P).transpose(2, 0, 3, 1).reshape(1, 8, P, 64)
    na_v = r["o_v"].reshape(P, 8, 64).transpose(1, 0, 2).reshape(1, 8, P, 64)
    ssd_out = r["o_ssd"].reshape(2, 64, 2, 4, 64).transpose(2, 0, 3, 1, 4).reshape(2, 1, 8, 64, 64)
    lin = r["o_lin"].reshape(2, 2, 2, 2, 64, 128).transpose(0, 2, 1, 3, 4, 5).reshape(2, 2, 1, 4, 64, 128)
    return (y[:CTX].reshape(1, CTX, D), y[CTX:].reshape(1, LAT, D), na_k, na_v, ssd_out[0], ssd_out[1],
            lin[0, 0], lin[0, 1], lin[1, 0], lin[1, 1])
```

```python
from contextlib import ExitStack

import concourse.bass as bass
from concourse import mybir

F32 = mybir.dt.float32
F32R = mybir.dt.float32r
BF16 = mybir.dt.bfloat16
I16 = mybir.dt.int16
ACT = mybir.ActivationFunctionType
ALU = mybir.AluOpType
AX = mybir.AxisListType

P = 128
D = 1024
KT = D // P
CTX = 128
LAT = 1024
TOK = CTX + LAT
NT = TOK // P
BLK = 384
NB = TOK // BLK
DEPTH = 2
EPS = 1e-6
RANGES = ((0, CTX, 0), (CTX, TOK, 1))
UPAD = TOK + 4
URANGES = ((0, CTX, 1), (CTX, TOK, CTX + 2))
PIECES = ((0, CTX, 1), (CTX, 640, CTX + 2), (640, TOK, 642))
NP = len(PIECES)
FFN = 2816
FT = FFN // P
GT = FT // 2
ADA = 6 * D // P
SH1, SC1, G1, SH2, SC2, G2 = range(6)


class Scope:

    def __init__(self, nc, tag):
        self.nc, self.tag, self.stack, self.sems = nc, tag, ExitStack(), []

    def sb(self, name, shape, dt=F32):
        return self.stack.enter_context(self.nc.sbuf_tensor(f"{self.tag}__{name}", shape, dt))

    def banks(self, n):
        return [self.stack.enter_context(self.nc.psum_tensor(f"{self.tag}__bank{i}", [P, 512], F32)) for i in range(n)]

    def sem(self, name, for_pool_dma=False):
        s = self.stack.enter_context(self.nc.semaphore(f"{self.tag}__{name}"))
        if not for_pool_dma:
            self.sems.append(s)
        return s

    def __enter__(self):
        return self

    def __exit__(self, *exc):
        self.stack.close()
        if exc[0] is None and self.sems:
            with self.nc.Block() as block:
                @block.gpsimd
                def _(pool):
                    for s in self.sems:
                        pool.sem_clear(s)


def split_matmul(pe, out, w_hi, w_lo, v_hi, v_lo, first, last):
    pe.matmul(out, w_hi, v_lo, start=first, stop=False)
    pe.matmul(out, w_lo, v_hi, start=False, stop=False)
    return pe.matmul(out, w_hi, v_hi, start=False, stop=last)


ADA_PER = 4
BESIDE = 4
WIDE = 96


def silu_wide(act, c_act, c_in):
    return act.activation(c_act[:, :, :].rearrange("p k (a c) -> p k a c", c=2),
                          c_in[:, :, :].rearrange("p k (a c) -> p k a c", a=1).to_broadcast([P, KT, WIDE // 2, 2]),
                          ACT.Silu)


def gains_of(dve, l, mods, gains, norm_w):
    for w_, part in enumerate((SC1, SC2)):
        last = dve.scalar_tensor_tensor(gains[:, l, w_, :, :], mods[:, l * ADA + part * KT:l * ADA + (part + 1) * KT, :],
                                        1.0, norm_w[:, w_, :, :], ALU.add, ALU.mult)
    return last


def modulation(nc, d, mods, gains, x_t, ident):
    per = ADA_PER
    here = DEPTH * ADA - 2 * per * BESIDE
    slots = 4
    rounds = here // (slots * per)
    with Scope(nc, "ada") as s:
        c_in = s.sb("c_in", [P, KT, 2])
        c_act = s.sb("c_act", [P, KT, WIDE])
        bias = s.sb("bias", [P, here, 2])
        norm_w = s.sb("norm_w", [P, 2, KT, 2])
        w = s.sb("w", [P, slots, per, KT, P])
        ps = s.banks(slots)
        small_in, silu_done, x_in = s.sem("small_in"), s.sem("silu_done"), s.sem("x_in")
        w_in = [s.sem(f"w_in{u}") for u in range(slots)]
        product, added, gained = s.sem("product"), s.sem("added"), s.sem("gained")
        with nc.Block() as block:
            @block.sync
            def _(sp):
                sp.dma_start(c_in[:, :, :], d["c_t"]).then_inc(small_in, 16)
                sp.dma_start(bias[:, :, :], d["b_ada"][:, 0:here, :]).then_inc(small_in, 16)
                sp.dma_start(norm_w[:, :, :, :], d["norm_w"][:, 0, :, :, :]).then_inc(small_in, 16)

                def load(i, u):
                    sp.dma_start(w[:, u, :, :, :], d["w_ada"][bass.ds(slots * i + u, 1), :, :, :, :]
                                 .rearrange("a t p k c -> p (a t) k c")).then_inc(w_in[u], 16)
                for u in range(slots):
                    load(0, u)
                sp.dma_start(x_t[:, :, :], d["x_t"]).then_inc(x_in, 16)
                sp.dma_start(ident[:, :], d["ident"]).then_inc(x_in, 16)
                with sp.Fori(1, rounds) as i:
                    for u in range(slots):
                        sp.wait_ge(product, slots * (i - 1) + u + 1)
                        load(i, u)
                sp.wait_ge(x_in, 32)

            @block.scalar
            def _(act):
                act.wait_ge(small_in, 48)
                silu_wide(act, c_act, c_in).then_inc(silu_done, 1)

            @block.tensor
            def _(pe):
                pe.wait_ge(silu_done, 1)

                def round_(i, u, wait):
                    pe.wait_ge(w_in[u], 16 * (i + 1))
                    if wait:
                        pe.wait_ge(added, slots * (i - 1) + u + 1)
                    for t in range(per):
                        for k in range(KT):
                            last = pe.matmul(ps[u][:, WIDE * t:WIDE * (t + 1)], w[:, u, t, k, :], c_act[:, k, :],
                                             start=(k == 0), stop=(k == KT - 1))
                    last.then_inc(product, 1)
                for u in range(slots):
                    round_(0, u, False)
                with pe.Fori(1, rounds) as i:
                    for u in range(slots):
                        round_(i, u, True)

            @block.vector
            def _(dve):
                dve.wait_ge(small_in, 48)
                mods_r = mods[:, 0:here, :].rearrange("p (r t) c -> p r t c", t=per)
                bias_r = bias[:, :, :].rearrange("p (r t) c -> p r t c", t=per)
                with dve.Fori(0, rounds) as i:
                    for u in range(slots):
                        dve.wait_ge(product, slots * i + u + 1)
                        dve.tensor_tensor(mods_r[:, bass.ds(slots * i + u, 1), :, :],
                                          ps[u][:, 0:WIDE * per].rearrange("p (a t n) -> p a t n", a=1, t=per)[:, :, :, 0:2],
                                          bias_r[:, bass.ds(slots * i + u, 1), :, :], ALU.add).then_inc(added, 1)
                dve.wait_ge(added, slots * rounds)
                gains_of(dve, 0, mods, gains, norm_w).then_inc(gained, 1)


def mod(mods, l, part, k, c):
    return mods[:, l * ADA + part * KT + k, c:c + 1]


def norm(nc, tag, l, which, x_t, ones, eps, mods, gains, h_hi, h_lo, d, ahead):
    beside = BESIDE if l == 0 else 0
    part0 = DEPTH * ADA // ADA_PER - (2 - which) * BESIDE
    tile0 = part0 * ADA_PER
    shift = (SH1, SH2)[which]
    pairs = KT // 2
    with Scope(nc, tag) as s:
        sq = s.sb("sq", [P, 4, TOK])
        inv = s.sb("inv", [P, TOK])
        h = s.sb("h", [P, 4, TOK])
        ps = s.banks(NB + 2)
        if beside:
            c_in, c_act = s.sb("c_in", [P, KT, 2]), s.sb("c_act", [P, KT, WIDE])
            w = s.sb("w", [P, 2, ADA_PER, KT, P])
            bias, norm_w = s.sb("bias", [P, beside * ADA_PER, 2]), s.sb("norm_w", [P, 2, KT, 2])
            small_in, silu_done, gained_all = s.sem("small_in"), s.sem("silu_done"), s.sem("gained_all")
            w_in = [s.sem("w_in0"), s.sem("w_in1")]
            ada_mm, ada_added = s.sem("ada_mm"), s.sem("ada_added")
        squared, squared_too, paired = s.sem("squared"), s.sem("squared_too"), s.sem("paired")
        summed, logged, inverted = s.sem("summed"), s.sem("logged"), s.sem("inverted")
        gained = s.sem("gained")
        scaled, scaled_too, hi_done, lo_done = s.sem("scaled"), s.sem("scaled_too"), s.sem("hi_done"), s.sem("lo_done")
        own = (1, 3, 5)
        with nc.Block() as block:
            @block.sync
            def _(sp):
                if beside:
                    sp.dma_start(c_in[:, :, :], d["c_t"]).then_inc(small_in, 16)
                    sp.dma_start(bias[:, :, :], d["b_ada"][:, tile0:tile0 + beside * ADA_PER, :]).then_inc(small_in, 16)
                    sp.dma_start(norm_w[:, :, :, :], d["norm_w"][:, 1, :, :, :]).then_inc(small_in, 16)
                for i in range(beside):
                    if i >= 2:
                        sp.wait_ge(ada_mm, i - 1)
                    sp.dma_start(w[:, i % 2, :, :, :], d["w_ada"][part0 + i].rearrange("t p k c -> p t k c"))\
                        .then_inc(w_in[i % 2], 16)
                for buffer, source, arrived in ahead:
                    sp.dma_start(buffer, source).then_inc(arrived, 16)

            @block.scalar
            def _(act):
                for k in range(KT):
                    if k not in own:
                        if k >= 4:
                            act.wait_ge(summed, NB * (k // 2 - 1))
                        act.activation(sq[:, k % 4, :], x_t[:, k, :], ACT.Square).then_inc(squared, 1)
                if beside:
                    act.wait_ge(small_in, 48)
                    silu_wide(act, c_act, c_in).then_inc(silu_done, 1)
                for b in range(NB):
                    act.wait_ge(summed, NB * (pairs - 1) + b + 1)
                    act.activation(inv[:, b * BLK:(b + 1) * BLK], ps[b][:, 0:BLK], ACT.Ln, bias=eps[:, 0:1],
                                   scale=1.0 / D).then_inc(logged, 1)
                for b in range(NB):
                    act.wait_ge(logged, b + 1)
                    act.activation(inv[:, b * BLK:(b + 1) * BLK], inv[:, b * BLK:(b + 1) * BLK], ACT.Exp, scale=-0.5)\
                        .then_inc(inverted, 1)
                for k in range(KT):
                    if k % 2 == 0:
                        act.wait_ge(scaled, k // 2 + 1)
                    else:
                        act.wait_ge(scaled_too, k // 2 + 1)
                        for a, b, c in RANGES:
                            act.activation(h[:, k % 4, a:b], h[:, k % 4, a:b], ACT.Copy,
                                           scale=gains[:, l, which, k, c:c + 1]).then_inc(gained, 1)
                        act.wait_ge(gained, k + 1)
                    for a, b, c in RANGES:
                        act.activation(h_hi[:, k, a:b], h[:, k % 4, a:b], ACT.Identity,
                                       bias=mod(mods, l, shift, k, c)).then_inc(hi_done, 1)

            @block.tensor
            def _(pe):
                for m in range(pairs):
                    pe.wait_ge(paired, m + 1)
                    for b in range(NB):
                        pe.matmul(ps[b][:, 0:BLK], ones[:, :], sq[:, 2 * m % 4, b * BLK:(b + 1) * BLK],
                                  start=(m == 0), stop=(m == pairs - 1)).then_inc(summed, 1)
                for i in range(beside):
                    pe.wait_ge(silu_done, 1)
                    pe.wait_ge(w_in[i % 2], 16 * (i // 2 + 1))
                    if i >= 2:
                        pe.wait_ge(ada_added, i - 1)
                    for t in range(ADA_PER):
                        for k in range(KT):
                            last = pe.matmul(ps[NB + i % 2][:, WIDE * t:WIDE * (t + 1)], w[:, i % 2, t, k, :],
                                             c_act[:, k, :], start=(k == 0), stop=(k == KT - 1))
                    last.then_inc(ada_mm, 1)

            @block.gpsimd
            def _(pool):
                pool.wait_ge(inverted, NB)
                for k in range(1, KT, 2):
                    if k >= 5:
                        pool.wait_ge(lo_done, 2 * (k - 3))
                    pool.tensor_tensor(h[:, k % 4, :], x_t[:, k, :], inv[:, :], ALU.mult).then_inc(scaled_too, 1)

            @block.vector
            def _(dve):
                taken = 0
                for m in range(pairs):
                    if 2 * m + 1 in own:
                        if m >= 2:
                            dve.wait_ge(paired, m - 1)
                        x = x_t[:, 2 * m + 1, :]
                        dve.tensor_tensor(sq[:, (2 * m + 1) % 4, :], x, x, ALU.mult).then_inc(squared_too, 1)
                        taken += 1
                    dve.wait_ge(squared_too, taken)
                    dve.wait_ge(squared, 2 * m + 2 - taken)
                    dve.tensor_tensor(sq[:, 2 * m % 4, :], sq[:, 2 * m % 4, :], sq[:, (2 * m + 1) % 4, :], ALU.add)\
                        .then_inc(paired, 1)

                def low(k):
                    dve.wait_ge(hi_done, 2 * (k + 1))
                    for a, b, c in RANGES:
                        dve.scalar_tensor_tensor(h_lo[:, k, a:b], h[:, k % 4, a:b], mod(mods, l, shift, k, c),
                                                 h_hi[:, k, a:b].bitcast(F32), ALU.add, ALU.subtract).then_inc(lo_done, 1)

                def add_bias(i):
                    dve.wait_ge(ada_mm, i + 1)
                    at = i * ADA_PER
                    dve.tensor_tensor(mods[:, tile0 + at:tile0 + at + ADA_PER, :],
                                      ps[NB + i % 2][:, 0:ADA_PER * WIDE].rearrange("p (t c) -> p t c", c=WIDE)[:, :, 0:2],
                                      bias[:, at:at + ADA_PER, :], ALU.add).then_inc(ada_added, 1)

                dve.wait_ge(inverted, NB)
                for k in range(KT + 1):
                    if k < KT and k % 2 == 0:
                        if k >= 4:
                            dve.wait_ge(lo_done, 2 * (k - 3))
                        for a, b, c in RANGES:
                            last = dve.scalar_tensor_tensor(h[:, k % 4, a:b], x_t[:, k, a:b],
                                                            gains[:, l, which, k, c:c + 1], inv[:, a:b],
                                                            ALU.mult, ALU.mult)
                        last.then_inc(scaled, 1)
                    if k >= 1:
                        low(k - 1)
                    if beside and k in (1, 4, 6, 8):
                        add_bias((1, 4, 6, 8).index(k))
                if beside and which == 1:
                    dve.wait_ge(ada_added, beside)
                    gains_of(dve, 1, mods, gains, norm_w).then_inc(gained_all, 1)


def load_split_ring(s, name, cols, slots=2, raw=None, arrived=None):
    return dict(raw=raw or s.sb(name + "_raw", [P, slots, cols]), hi=s.sb(name + "_hi", [P, slots, cols], F32R),
                lo=s.sb(name + "_lo", [P, slots, cols], F32R),
                arrived=arrived or [s.sem(f"{name}_arrived{i}") for i in range(slots)],
                hi_done=s.sem(name + "_hi_done"), lo_done=s.sem(name + "_lo_done"))


def conv_ffn(nc, tag, l, d, x_t, mods, h_hi, h_lo, raw, arrived):
    units = KT * NB
    with Scope(nc, tag) as s:
        up = load_split_ring(s, "up", KT * P, raw=raw, arrived=arrived)
        dn_raw = s.sb("dn_raw", [P, D])
        dn_hi, dn_lo = s.sb("dn_hi", [P, 2, D], F32R), s.sb("dn_lo", [P, 2, D], F32R)
        u = s.sb("u", [P, 2, UPAD])
        ca = s.sb("ca", [P, TOK])
        g_hi, g_lo = s.sb("g_hi", [P, 4, TOK], F32R), s.sb("g_lo", [P, 4, TOK], F32R)
        cw = s.sb("cw", [P, FT, 2, 4])
        ps = s.banks(8)
        cw_in, padded = s.sem("cw_in"), s.sem("padded")
        dn_arrived, dn_hi_done, dn_lo_done = s.sem("dn_arrived"), s.sem("dn_hi_done"), s.sem("dn_lo_done")
        up_mm, evicted, tapped, silu_done = s.sem("up_mm"), s.sem("evicted"), s.sem("tapped"), s.sem("silu_done")
        gated, g_hi_done, g_lo_done = s.sem("gated"), s.sem("g_hi_done"), s.sem("g_lo_done")
        dn_mm, x_added = s.sem("dn_mm"), s.sem("x_added")

        def groups(eng, first, body, last=None):
            first()
            with eng.Fori(0, (GT - 1) // 2) as q:
                for v in range(2):
                    body(2 * q + v + 1, (v + 1) % 2)
            if last:
                last()

        with nc.Block() as block:
            @block.sync
            def _(sp):
                sp.dma_start(cw[:, :, :, :], d["ffn_conv"][l]).then_inc(cw_in, 16)

                def load_up(t, half, wait=True):
                    if wait:
                        sp.wait_ge(up["lo_done"], 2 * t + half - 1)
                    sp.dma_start(up["raw"][:, half, :], d["w_up"][l, bass.ds(2 * t + half, 1), :, :]
                                 .rearrange("a p n -> p (a n)")).then_inc(up["arrived"][half], 16)

                def load_down(f, wait=True):
                    if wait:
                        sp.wait_ge(dn_lo_done, f)
                    sp.dma_start(dn_raw[:, :], d["w_down"][l, bass.ds(f, 1), :, :]
                                 .rearrange("a p n -> p (a n)")).then_inc(dn_arrived, 16)

                def first():
                    for half in range(2):
                        load_up(1, half)
                    load_down(0, False)

                def group(m, par):
                    for j in range(2):
                        for half in range(2):
                            load_up(2 * m + j, half)
                        load_down(2 * m + j - 1)
                groups(sp, first, group, lambda: load_down(FT - 1))

            @block.scalar
            def _(act):
                def hi_up(t, half, wait=True):
                    act.wait_ge(up["arrived"][half], 16 * (t + 1))
                    if wait:
                        act.wait_ge(up_mm, 6 * t + 3 * half - 3)
                    act.activation(up["hi"][:, half, :], up["raw"][:, half, :], ACT.Copy)\
                        .then_inc(up["hi_done"], 1)

                def hi_down(m, j, wait=True):
                    act.wait_ge(dn_arrived, 16 * (2 * m + j + 1))
                    if wait:
                        act.wait_ge(dn_mm, units * m)
                    act.activation(dn_hi[:, j, :], dn_raw[:, :], ACT.Copy).then_inc(dn_hi_done, 1)

                def evict(t, half, wait=True):
                    if wait and half == 0:
                        act.wait_ge(gated, NP * t)
                    if wait and half == 1:
                        act.wait_ge(tapped, 6 * NP * t)
                    for b in range(NB):
                        act.wait_ge(up_mm, 6 * t + 3 * half + b + 1)
                        for lo, hi, at in ((0, CTX, 1), (CTX, BLK, CTX + 2)) if b == 0 else \
                                ((b * BLK, (b + 1) * BLK, b * BLK + 2),):
                            last = act.activation(u[:, half, at:at + hi - lo],
                                                  ps[3 * half + b][:, lo - b * BLK:hi - b * BLK], ACT.Copy)
                        last.then_inc(evicted, 1)

                def gate(t, slot, group, wait):
                    act.wait_ge(tapped, 6 * NP * t + 3 * NP)
                    act.activation(ca[:, :], ca[:, :], ACT.Silu).then_inc(silu_done, 1)
                    act.wait_ge(gated, NP * t + NP)
                    if wait:
                        act.wait_ge(dn_mm, units * (group - 1))
                    act.activation(g_hi[:, slot, :], ca[:, :], ACT.Copy).then_inc(g_hi_done, 1)

                def tile(m, par, j, first):
                    t = 2 * m + j
                    more = not (first and j == 0)
                    evict(t, 0, more)
                    hi_up(t + 1, 0)
                    if j == 1:
                        hi_down(m, 0, not first)
                    evict(t, 1, more)
                    hi_up(t + 1, 1)
                    if j == 1:
                        hi_down(m, 1, not first)
                    gate(t, 2 * par + j, m, not first)

                act.wait_ge(padded, 1)
                for half in range(2):
                    hi_up(0, half, False)
                for j in range(2):
                    tile(0, 0, j, True)
                with act.Fori(0, (GT - 3) // 2) as q:
                    for v in range(2):
                        for j in range(2):
                            tile(2 * q + v + 1, (v + 1) % 2, j, False)
                for m, par in [(GT - 2, (GT - 2) % 2), (GT - 1, (GT - 1) % 2)]:
                    for j in range(2):
                        t = 2 * m + j
                        if t < FT - 1:
                            tile(m, par, j, False)
                        else:
                            evict(t, 0)
                            hi_down(m, 0)
                            evict(t, 1)
                            hi_down(m, 1)
                            gate(t, 2 * par + j, m, True)

            @block.tensor
            def _(pe):
                def up_tile(t, wait=True):
                    for half in range(2):
                        pe.wait_ge(up["lo_done"], 2 * t + half + 1)
                        for b in range(NB):
                            if wait:
                                pe.wait_ge(evicted, 6 * t + 3 * half + b - 5)
                            for k in range(KT):
                                w = slice(k * P, (k + 1) * P)
                                c = slice(b * BLK, (b + 1) * BLK)
                                last = split_matmul(pe, ps[3 * half + b][:, 0:BLK], up["hi"][:, half, w],
                                                    up["lo"][:, half, w], h_hi[:, k, c], h_lo[:, k, c],
                                                    k == 0, k == KT - 1)
                            last.then_inc(up_mm, 1)

                def down(m, par, wait=True):
                    pe.wait_ge(g_lo_done, 2 * NP * m + 2 * NP)
                    pe.wait_ge(dn_lo_done, 2 * m + 2)
                    for v in range(units):
                        k, b = divmod(v, NB)
                        if wait or v >= 2:
                            pe.wait_ge(x_added, units * m + v - 1)
                        for j in range(2):
                            w, c = slice(k * P, (k + 1) * P), slice(b * BLK, (b + 1) * BLK)
                            last = split_matmul(pe, ps[6 + v % 2][:, 0:BLK], dn_hi[:, j, w], dn_lo[:, j, w],
                                                g_hi[:, 2 * par + j, c], g_lo[:, 2 * par + j, c], j == 0, j == 1)
                        last.then_inc(dn_mm, 1)

                up_tile(0, False)
                up_tile(1)
                up_tile(2)
                down(0, 0, False)
                up_tile(3)
                with pe.Fori(0, (GT - 3) // 2) as q:
                    for v in range(2):
                        m = 2 * q + v + 2
                        up_tile(2 * m)
                        down(m - 1, (v + 1) % 2)
                        up_tile(2 * m + 1)
                up_tile(2 * (GT - 1))
                down(GT - 2, (GT - 2) % 2)
                up_tile(2 * (GT - 1) + 1)
                down(GT - 1, (GT - 1) % 2)

            @block.vector
            def _(dve):
                dve.memset(u[:, :, :], 0.0).then_inc(padded, 1)
                dve.wait_ge(cw_in, 16)

                def lo_up(t, half):
                    dve.wait_ge(up["hi_done"], 2 * t + half + 1)
                    dve.tensor_tensor(up["lo"][:, half, :], up["raw"][:, half, :], up["hi"][:, half, :].bitcast(F32),
                                      ALU.subtract).then_inc(up["lo_done"], 1)

                def lo_down(m, j):
                    dve.wait_ge(dn_hi_done, 2 * m + j + 1)
                    dve.tensor_tensor(dn_lo[:, j, :], dn_raw[:, :], dn_hi[:, j, :].bitcast(F32), ALU.subtract)\
                        .then_inc(dn_lo_done, 1)

                def taps(t, half, n, piece, wait=True):
                    if n == 0 and piece == 0:
                        dve.wait_ge(evicted, 6 * t + 3 * half + 3)
                        if half == 0 and wait:
                            dve.wait_ge(g_lo_done, NP * t)
                        if half == 1:
                            dve.wait_ge(tapped, 6 * NP * t + 3 * NP)
                    if n:
                        dve.wait_ge(tapped, 6 * NP * t + 3 * NP * half + NP * (n - 1) + piece + 1)
                    for a, b, at in (PIECES[piece],):
                        out = ca[:, a:b] if half == 0 else u[:, 0, at:at + b - a]
                        w = cw[:, bass.ds(t, 1), half, :].rearrange("p a n -> p (a n)")
                        if n == 0:
                            op = dve.tensor_scalar(out, u[:, half, at:at + b - a], w[:, 1:2], w[:, 3:4],
                                                   ALU.mult, ALU.add)
                        else:
                            off, tap = ((-1, 0), (1, 2))[n - 1]
                            op = dve.scalar_tensor_tensor(out, u[:, half, at + off:at + off + b - a],
                                                          w[:, tap:tap + 1], out, ALU.mult, ALU.add)
                        op.then_inc(tapped, 1)

                def product(t, piece):
                    dve.wait_ge(silu_done, t + 1)
                    dve.wait_ge(tapped, 6 * NP * t + 5 * NP + piece + 1)
                    for a, b, at in (PIECES[piece],):
                        dve.tensor_tensor(ca[:, a:b], ca[:, a:b], u[:, 0, at:at + b - a], ALU.mult)\
                            .then_inc(gated, 1)

                def g_low(t, slot, piece):
                    dve.wait_ge(g_hi_done, t + 1)
                    c = slice(*PIECES[piece][0:2])
                    dve.tensor_tensor(g_lo[:, slot, c], ca[:, c], g_hi[:, slot, c].bitcast(F32), ALU.subtract)\
                        .then_inc(g_lo_done, 1)

                def add_x(m, v, again):
                    k, b = divmod(v, NB)
                    dve.wait_ge(dn_mm, units * m + v + 1)
                    if again:
                        dve.wait_ge(x_added, units * (m - 1) + v + 1)
                    for lo, hi, c in ((0, CTX, 0), (CTX, BLK, 1)) if b == 0 else ((b * BLK, (b + 1) * BLK, 1),):
                        last = dve.scalar_tensor_tensor(x_t[:, k, lo:hi], ps[6 + v % 2][:, lo - b * BLK:hi - b * BLK],
                                                        mod(mods, l, G2, k, c), x_t[:, k, lo:hi], ALU.mult, ALU.add)
                    last.then_inc(x_added, 1)

                def tile(m, par, j, last_tile=False, down=True, again=True):
                    t = 2 * m + j
                    slot = 2 * par + j
                    if not last_tile:
                        lo_up(t + 1, 0)
                    for n in range(3):
                        for piece in range(NP):
                            taps(t, 0, n, piece, down or j == 1)
                    if j == 1:
                        lo_down(m, 0)
                    if not last_tile:
                        lo_up(t + 1, 1)
                    if j == 1:
                        lo_down(m, 1)
                    rest = [lambda n=n, i=i: taps(t, 1, n, i) for n in range(3) for i in range(NP)]
                    rest += [lambda i=i: product(t, i) for i in range(NP)] + [lambda i=i: g_low(t, slot, i) for i in range(NP)]
                    for v in range(units if j == 0 and down else 0):
                        add_x(m - 1, v, again)
                        if v >= 2 and rest:
                            rest.pop(0)()
                    for step in rest:
                        step()

                for half in range(2):
                    lo_up(0, half)
                tile(0, 0, 0, down=False)
                tile(0, 0, 1)
                tile(1, 1, 0, again=False)
                tile(1, 1, 1)
                with dve.Fori(0, (GT - 3) // 2) as q:
                    for v in range(2):
                        for j in range(2):
                            tile(2 * q + v + 2, v % 2, j)
                for j in range(2):
                    tile(GT - 1, (GT - 1) % 2, j, j == 1)
                for v in range(units):
                    add_x(GT - 1, v, True)


TC = 256


def in_project(nc, tag, stored, w_t, w_tok, h_hi, h_lo, u_t, u_tok, u_small, small, turn, ident, raw, arrived):
    n_t, n_tok = w_t.shape[0] - 1, w_tok.shape[0]
    loops = n_t // 2
    with Scope(nc, tag) as s:
        wt = load_split_ring(s, "wt", KT * P, raw=raw, arrived=arrived)
        wk = load_split_ring(s, "wk", KT * TC)
        out_t = s.sb("out_t", [P, 2, TOK])
        out_tok = s.sb("out_tok", [P, 2, TC])
        ps = s.banks(8)
        t_mm, t_out = s.sem("t_mm"), s.sem("t_out")
        t_stored, k_stored, s_stored = stored[0:2], stored[2:4], stored[4]
        k_mm, k_out = s.sem("k_mm"), s.sem("k_out")
        if turn:
            out_s = s.sb("out_s", [P, NT, small])
            s_mm, s_out = s.sem("s_mm"), s.sem("s_out")
        with nc.Block() as block:
            @block.sync
            def _(sp):
                def load_tok(c):
                    if c >= 2:
                        sp.wait_ge(wk["lo_done"], c - 1)
                    sp.dma_start(wk["raw"][:, c % 2, :], w_tok[c]).then_inc(wk["arrived"][c % 2], 16)

                def load_t(i, j):
                    sp.wait_ge(wt["lo_done"], 2 * i + j - 1)
                    sp.dma_start(wt["raw"][:, j, :], w_t[bass.ds(2 * i + j, 1), :, :]
                                 .rearrange("a p n -> p (a n)")).then_inc(wt["arrived"][j], 16)
                for c in range(2):
                    load_tok(c)
                with sp.Fori(1, loops) as i:
                    for j in range(2):
                        load_t(i, j)
                load_t(loops, 0)
                for c in range(2, n_tok):
                    load_tok(c)

            def split_hi(act, ring, slot, n, free=None):
                act.wait_ge(ring["arrived"][slot], 16 * n)
                if free:
                    act.wait_ge(*free)
                act.activation(ring["hi"][:, slot, :], ring["raw"][:, slot, :], ACT.Copy)\
                    .then_inc(ring["hi_done"], 1)

            def split_lo(dve, ring, slot, n):
                dve.wait_ge(ring["hi_done"], n)
                dve.tensor_tensor(ring["lo"][:, slot, :], ring["raw"][:, slot, :],
                                  ring["hi"][:, slot, :].bitcast(F32), ALU.subtract).then_inc(ring["lo_done"], 1)

            @block.scalar
            def _(act):
                def evict_t(i, j, wait=True):
                    if wait:
                        act.wait_ge(t_stored[j], 16 * i)
                    for b in range(NB):
                        act.wait_ge(t_mm, NB * (2 * i + j) + b + 1)
                        act.activation(out_t[:, j, b * BLK:(b + 1) * BLK], ps[3 * j + b][:, 0:BLK], ACT.Copy)\
                            .then_inc(t_out, 1)

                for j in range(2):
                    split_hi(act, wt, j, 1)
                for c in range(2):
                    split_hi(act, wk, c, 1)
                evict_t(0, 0, False)
                split_hi(act, wt, 0, 2, (t_mm, NB))
                evict_t(0, 1, False)
                split_hi(act, wt, 1, 2, (t_mm, 2 * NB))
                with act.Fori(1, loops - 1) as i:
                    for j in range(2):
                        evict_t(i, j)
                        split_hi(act, wt, j, i + 2, (t_mm, NB * (2 * i + j + 1)))
                evict_t(loops - 1, 0)
                split_hi(act, wt, 0, loops + 1, (t_mm, NB * (2 * loops - 1)))
                evict_t(loops - 1, 1)
                evict_t(loops, 0)
                for c in range(n_tok):
                    if turn and c == 1:
                        act.wait_ge(s_mm, 1)
                        act.activation(out_s[:, :, :], ps[0][:, 0:NT * small].rearrange("p (t n) -> p t n", n=small),
                                       ACT.Copy).then_inc(s_out, 1)
                    for i in range(NT):
                        n = c * NT + i
                        if i == 0 and 2 <= c + 1 < n_tok:
                            split_hi(act, wk, (c + 1) % 2, (c + 1) // 2 + 1, (k_mm, NT * c))
                        if n >= 2:
                            act.wait_ge(k_stored[n % 2], 16 * (n // 2))
                        act.wait_ge(k_mm, n + 1)
                        act.activation(out_tok[:, n % 2, :], ps[6 + n % 2][:, 0:TC], ACT.Copy).then_inc(k_out, 1)

            @block.vector
            def _(dve):
                for j in range(2):
                    split_lo(dve, wt, j, j + 1)
                for c in range(2):
                    split_lo(dve, wk, c, c + 1)
                with dve.Fori(1, loops) as i:
                    for j in range(2):
                        split_lo(dve, wt, j, 2 * i + j + 1)
                split_lo(dve, wt, 0, 2 * loops + 1)
                for c in range(2, n_tok):
                    split_lo(dve, wk, c % 2, c + 1)

            @block.tensor
            def _(pe):
                def t_tile(i, j, wait=True):
                    pe.wait_ge(wt["lo_done"], 2 * i + j + 1)
                    for b in range(NB):
                        if wait:
                            pe.wait_ge(t_out, NB * (2 * i + j - 2) + b + 1)
                        for k in range(KT):
                            w, c = slice(k * P, (k + 1) * P), slice(b * BLK, (b + 1) * BLK)
                            last = split_matmul(pe, ps[3 * j + b][:, 0:BLK], wt["hi"][:, j, w], wt["lo"][:, j, w],
                                                h_hi[:, k, c], h_lo[:, k, c], k == 0, k == KT - 1)
                        last.then_inc(t_mm, 1)

                for j in range(2):
                    t_tile(0, j, False)
                with pe.Fori(1, loops) as i:
                    for j in range(2):
                        t_tile(i, j)
                t_tile(loops, 0)
                for c in range(n_tok):
                    if turn and c == 1:
                        pe.wait_ge(t_out, NB * (n_t + 1))
                        for i in range(NT):
                            last = pe.transpose(ps[0][:, i * small:(i + 1) * small],
                                                out_t[0:small, 0, i * P:(i + 1) * P], ident[0:small, 0:small])
                        last.then_inc(s_mm, 1)
                    pe.wait_ge(wk["lo_done"], c + 1)
                    for i in range(NT):
                        n = c * NT + i
                        if n >= 2:
                            pe.wait_ge(k_out, n - 1)
                        for k in range(KT):
                            w, t = slice(k * TC, (k + 1) * TC), slice(i * P, (i + 1) * P)
                            last = split_matmul(pe, ps[6 + n % 2][:, 0:TC], h_hi[:, k, t], h_lo[:, k, t],
                                                wk["hi"][:, c % 2, w], wk["lo"][:, c % 2, w], k == 0, k == KT - 1)
                        last.then_inc(k_mm, 1)

            @block.gpsimd
            def _(pool):
                with pool.Fori(0, loops) as i:
                    for j in range(2):
                        pool.wait_ge(t_out, NB * (2 * i + j + 1))
                        pool.dma_start(u_t[bass.ds(2 * i + j, 1), :, :].rearrange("a p n -> p (a n)"),
                                       out_t[:, j, :]).then_inc(t_stored[j], 16)
                if not turn:
                    pool.wait_ge(t_out, NB * (n_t + 1))
                    pool.dma_start(u_small, out_t[0:small, 0, :]).then_inc(s_stored, 16)
                for c in range(n_tok):
                    for i in range(NT):
                        n = c * NT + i
                        pool.wait_ge(k_out, n + 1)
                        pool.dma_start(u_tok[i, :, c * TC:(c + 1) * TC], out_tok[:, n % 2, :])\
                            .then_inc(k_stored[n % 2], 16)
                for j in range(2):
                    pool.wait_ge(t_stored[j], 16 * loops)
                    pool.wait_ge(k_stored[j], 16 * ((n_tok * NT + 1 - j) // 2))
                if turn:
                    pool.wait_ge(s_out, 1)
                    pool.dma_start(u_small, out_s[:, :, :]).then_inc(s_stored, 16)
                pool.wait_ge(s_stored, 16)


def out_project(nc, tag, l, w_out, y_tok, ident, x_t, mods):
    with Scope(nc, tag) as s:
        y_hi, y_lo = s.sb("y_hi", [P, KT, TOK], F32R), s.sb("y_lo", [P, KT, TOK], F32R)
        w = load_split_ring(s, "w", KT * P)
        ps = s.banks(8)
        turned, y_hi_done, y_lo_done = s.sem("turned"), s.sem("y_hi_done"), s.sem("y_lo_done")
        mm, x_added = s.sem("mm"), s.sem("x_added")
        quads = [(k, i, min(3, NT - i)) for k in range(KT) for i in range(0, NT, 3)]
        with nc.Block() as block:
            @block.sync
            def _(sp):
                for n in range(KT):
                    if n >= 2:
                        sp.wait_ge(w["lo_done"], n - 1)
                    sp.dma_start(w["raw"][:, n % 2, :], w_out[n]).then_inc(w["arrived"][n % 2], 16)

            @block.scalar
            def _(act):
                def split(n):
                    act.wait_ge(w["arrived"][n % 2], 16 * (n // 2 + 1))
                    if n >= 2:
                        act.wait_ge(mm, NB * (n - 1))
                    act.activation(w["hi"][:, n % 2, :], w["raw"][:, n % 2, :], ACT.Copy).then_inc(w["hi_done"], 1)
                split(0)
                split(1)
                for n, (k, i, m) in enumerate(quads):
                    act.wait_ge(turned, n + 1)
                    act.activation(y_hi[:, k, i * P:(i + m) * P], ps[n % 8][:, 0:m * P], ACT.Copy)\
                        .then_inc(y_hi_done, 1)
                for n in range(2, KT):
                    split(n)

            @block.tensor
            def _(pe):
                for n, (k, i, m) in enumerate(quads):
                    if n >= 8:
                        pe.wait_ge(y_lo_done, n - 7)
                    for t in range(m):
                        last = pe.transpose(ps[n % 8][:, t * P:(t + 1) * P], y_tok[:, i + t, k * P:(k + 1) * P],
                                            ident[:, :])
                    last.then_inc(turned, 1)
                pe.wait_ge(y_lo_done, len(quads))
                for n in range(KT):
                    pe.wait_ge(w["lo_done"], n + 1)
                    for b in range(NB):
                        v = n * NB + b
                        if v >= 6:
                            pe.wait_ge(x_added, v - 5)
                        for k in range(KT):
                            c, t = slice(k * P, (k + 1) * P), slice(b * BLK, (b + 1) * BLK)
                            last = split_matmul(pe, ps[2 + v % 6][:, 0:BLK], w["hi"][:, n % 2, c], w["lo"][:, n % 2, c],
                                                y_hi[:, k, t], y_lo[:, k, t], k == 0, k == KT - 1)
                        last.then_inc(mm, 1)

            @block.vector
            def _(dve):
                def split(n):
                    dve.wait_ge(w["hi_done"], n + 1)
                    dve.tensor_tensor(w["lo"][:, n % 2, :], w["raw"][:, n % 2, :], w["hi"][:, n % 2, :].bitcast(F32),
                                      ALU.subtract).then_inc(w["lo_done"], 1)
                split(0)
                split(1)
                for n, (k, i, m) in enumerate(quads):
                    dve.wait_ge(y_hi_done, n + 1)
                    c = slice(i * P, (i + m) * P)
                    dve.tensor_tensor(y_lo[:, k, c], ps[n % 8][:, 0:m * P], y_hi[:, k, c].bitcast(F32), ALU.subtract)\
                        .then_inc(y_lo_done, 1)
                for n in range(KT):
                    for b in range(NB):
                        v = n * NB + b
                        dve.wait_ge(mm, v + 1)
                        for lo, hi, c in ((0, CTX, 0), (CTX, BLK, 1)) if b == 0 else ((b * BLK, (b + 1) * BLK, 1),):
                            last = dve.scalar_tensor_tensor(x_t[:, n, lo:hi], ps[2 + v % 6][:, lo - b * BLK:hi - b * BLK],
                                                            mod(mods, l, G1, n, c), x_t[:, n, lo:hi],
                                                            ALU.mult, ALU.add)
                        last.then_inc(x_added, 1)
                    if n + 2 < KT:
                        split(n + 2)


LE, GE, LT, GT_ = range(4)
SSD_H, SSD_P, SSD_G = 8, 64, 2
SSD_W = SSD_H * SSD_P
HG = SSD_H // SSD_G
LIN_H, LIN_K, LIN_V = 8, 64, 128
FWD, BWD = 0, 1


def scan_steps():
    steps, seen, last = [], set(), {}
    order = [(FWD, 0), (BWD, 0)]
    for c in range(1, NT):
        order += [(FWD, c), (BWD, NT - c)]
    for n, (way, c) in enumerate(order):
        state = way if c == 0 else 2 + way
        steps.append((way, c, state, c not in seen, last.get(state)))
        seen.add(c)
        last[state] = n
    return steps


def bcast(ap, n):
    return ap.rearrange("p (h a) -> p h a", a=1).to_broadcast([ap.shape[0], ap.shape[1], n])


def conv_rows(s, nc, d_u, n_tiles, ident, cw_src, kept, turned_out, ps):
    cw = s.sb("cw", [P, n_tiles, 4])
    u = s.sb("u", [P, 2, UPAD])
    acc = s.sb("acc", [P, 2, TOK])
    out = s.sb("act_out", [P, 2, TOK])
    ready, padded, tapped, active = s.sem("cw_ready"), s.sem("padded"), s.sem("tapped"), s.sem("active")
    arrived = [s.sem("u_arrived0"), s.sem("u_arrived1")]
    turned, copied = s.sem("turned"), s.sem("copied")
    parts = [(i, min(4, NT - i)) for i in range(0, NT, 4)]
    jobs = [(j, i, m) for j in range(n_tiles) if turned_out[j] for i, m in parts]
    upto = [sum(1 for q in jobs if q[0] <= j) for j in range(n_tiles)]

    def result(j):
        return kept[j] if kept[j] is not None else out[:, j % 2, :]

    def copy_out(act, j):
        for n, (jj, i, m) in enumerate(jobs):
            if jj == j:
                act.wait_ge(turned, n + 1)
                act.activation(turned_out[j](i, m), ps[n % 2][:, 0:m * P].rearrange("p (t n) -> p t n", n=P),
                               ACT.Copy).then_inc(copied, 1)

    with nc.Block() as block:
        @block.sync
        def _(sp):
            sp.dma_start(cw[:, :, :], cw_src).then_inc(ready, 16)
            sp.wait_ge(padded, 1)
            for j in range(n_tiles):
                if j >= 2:
                    sp.wait_ge(tapped, 6 * (j - 1))
                for a, b, at in URANGES:
                    sp.dma_start(u[:, j % 2, at:at + b - a], d_u[j, :, a:b]).then_inc(arrived[j % 2], 16)

        @block.vector
        def _(dve):
            dve.memset(u[:, :, :], 0.0).then_inc(padded, 1)
            dve.wait_ge(ready, 16)
            for j in range(n_tiles):
                dve.wait_ge(arrived[j % 2], 32 * (j // 2 + 1))
                if j >= 2:
                    dve.wait_ge(active, j - 1)
                for n in range(3):
                    if n:
                        dve.wait_ge(tapped, 6 * j + 2 * n)
                    for a, b, at in URANGES:
                        if n == 0:
                            op = dve.tensor_scalar(acc[:, j % 2, a:b], u[:, j % 2, at:at + b - a], cw[:, j, 1:2],
                                                   cw[:, j, 3:4], ALU.mult, ALU.add)
                        else:
                            off, tap = ((-1, 0), (1, 2))[n - 1]
                            op = dve.scalar_tensor_tensor(acc[:, j % 2, a:b], u[:, j % 2, at + off:at + off + b - a],
                                                          cw[:, j, tap:tap + 1], acc[:, j % 2, a:b],
                                                          ALU.mult, ALU.add)
                        op.then_inc(tapped, 1)

        @block.scalar
        def _(act):
            for j in range(n_tiles):
                act.wait_ge(tapped, 6 * (j + 1))
                if j >= 2 and upto[j - 2]:
                    act.wait_ge(turned, upto[j - 2])
                act.activation(result(j), acc[:, j % 2, :], ACT.Silu).then_inc(active, 1)
                if j >= 1:
                    copy_out(act, j - 1)
            copy_out(act, n_tiles - 1)

        @block.tensor
        def _(pe):
            for n, (j, i, m) in enumerate(jobs):
                pe.wait_ge(active, j + 1)
                if n >= 2:
                    pe.wait_ge(copied, n - 1)
                for t in range(m):
                    last = pe.transpose(ps[n % 2][:, t * P:(t + 1) * P], result(j)[:, (i + t) * P:(i + t + 1) * P],
                                        ident[:, :])
                last.then_inc(turned, 1)


def ssd(nc, tag, d, y_tok, ident, tri, ones, eps):
    steps = scan_steps()
    with Scope(nc, tag) as s:
        x_tok = s.sb("x_tok", [P, NT, SSD_W])
        k_tok = s.sb("k_tok", [P, NT, P])
        k_t, q_t = s.sb("k_t", [P, TOK]), s.sb("q_t", [P, TOK])
        dt, g = s.sb("dt", [P, NT, 2, SSD_H]), s.sb("g", [P, NT, 2, SSD_H])
        row = s.sb("row", [P, 2 * SSD_H * 2 + SSD_H + SSD_W])
        bias, a_log, skip = row[:, 0:16], row[:, 16:32], row[:, 32:40]
        norm_w = row[:, 40:40 + SSD_W]
        ps = s.banks(8)
        with Scope(nc, tag + "c") as c:
            conv_rows(c, nc, d["u0_t"], 6, ident, d["ssd_conv"],
                      [None] * 4 + [k_t[:, :], q_t[:, :]],
                      [lambda i, m, j=j: x_tok[:, i:i + m, j * P:(j + 1) * P] for j in range(4)]
                      + [lambda i, m: k_tok[:, i:i + m, :], None], ps)

        state = s.sb("state", [P, 4, HG * SSD_P])
        gu = s.sb("gu", [P, 2, SSD_H, P])
        w = s.sb("w", [P, 2, SSD_H, P])
        sm = s.sb("sm", [P, 2, SSD_G, P])
        xdt, xw = s.sb("xdt", [P, 2, SSD_W]), s.sb("xw", [P, 2, SSD_W])
        e3 = s.sb("e3", [P, 2, 3 * SSD_H])
        t1 = s.sb("t1", [P, 2, SSD_W])
        st = s.sb("st", [P, 3, NT * 2 * SSD_H])
        neg_a = s.sb("neg_a", [P, 2 * SSD_H])
        z = s.sb("z", [P, NT, SSD_W])
        dx = s.sb("dx", [P, SSD_W])
        ss, rs = s.sb("ss", [P, NT]), s.sb("rs", [P, 2, NT])
        row_in, dt_in, state_in, z_in = s.sem("row_in"), s.sem("dt_in"), s.sem("state_in"), s.sem("z_in")
        zeroed, dt_step, g_ready = s.sem("zeroed"), s.sem("dt_step"), s.sem("g_ready")
        gu_done, xdt_done, xw_done = s.sem("gu_done"), s.sem("xdt_done"), s.sem("xw_done")
        sums_mm, diff_mm, score_mm = s.sem("sums_mm"), s.sem("diff_mm"), s.sem("score_mm")
        exps_done, decay_done = s.sem("exps_done"), s.sem("decay_done")
        sm_done, w_done = s.sem("sm_done"), s.sem("w_done")
        intra_mm, inter_mm, state_mm = s.sem("intra_mm"), s.sem("inter_mm"), s.sem("state_mm")
        scaled, y_step, y_done, faded, s_done = (s.sem("scaled"), s.sem("y_step"), s.sem("y_done"), s.sem("faded"),
                                                 s.sem("s_done"))
        z_act, skipped, gated, squared, rooted, normed, out = (
            s.sem("z_act"), s.sem("skipped"), s.sem("gated"), s.sem("squared"), s.sem("rooted"), s.sem("normed"),
            s.sem("out"))
        n_steps = len(steps)
        with nc.Block() as block:
            @block.sync
            def _(sp):
                sp.dma_start(dt[:, :, :, :].rearrange("p t w h -> p (t w h)"), d["u0_small"]).then_inc(dt_in, 16)
                sp.dma_start(row[:, :], d["ssd_row"]).then_inc(row_in, 16)
                sp.dma_start(state[:, 2:4, :], d["ssd_state"]).then_inc(state_in, 16)
                sp.dma_start(z[:, :, :], d["u0_tok"][:, :, 0:SSD_W].rearrange("t p n -> p t n")).then_inc(z_in, 16)
                sp.wait_ge(s_done, 2)
                sp.dma_start(d["o_ssd"], state[:, 0:2, :]).then_inc(out, 16)
                sp.wait_ge(out, 16)

            @block.scalar
            def _(act):
                act.wait_ge(row_in, 16)
                act.activation(neg_a[:, :], a_log, ACT.Exp).then_inc(dt_step, 1)
                act.wait_ge(dt_step, 2)
                act.activation(st[:, 1, :], st[:, 0, :], ACT.Abs).then_inc(dt_step, 1)
                act.wait_ge(dt_step, 3)
                act.activation(st[:, 1, :], st[:, 1, :], ACT.Exp, scale=-1.0).then_inc(dt_step, 1)
                for n in range(n_steps):
                    act.wait_ge(sums_mm, n + 1)
                    if n >= 2:
                        act.wait_ge(s_done, n - 1)
                        act.wait_ge(scaled, n - 1)
                        act.wait_ge(xw_done, n - 1)
                    act.activation(e3[:, n % 2, :], ps[0][:, 0:3 * SSD_H], ACT.Exp).then_inc(exps_done, 1)
                    if n >= 2:
                        act.wait_ge(intra_mm, n - 1)
                    act.wait_ge(diff_mm, n + 1)
                    for b in range(2):
                        last = act.activation(w[:, n % 2, 4 * b:4 * b + 4, :].rearrange("p h t -> p (h t)"),
                                              ps[3 + b][:, :], ACT.Exp)
                    last.then_inc(decay_done, 1)
                act.wait_ge(z_in, 16)
                for c in range(NT):
                    act.activation(z[:, c, :], z[:, c, :], ACT.Silu).then_inc(z_act, 1)
                for c in range(NT):
                    act.wait_ge(gated, c + 1)
                    act.activation(z[:, c, :], y_tok[:, c, 0:SSD_W], ACT.Square, accum_out=ss[:, c:c + 1])\
                        .then_inc(squared, 1)
                act.wait_ge(squared, NT)
                act.activation(rs[:, 0, :], ss[:, :], ACT.Sqrt, bias=eps[:, 0:1], scale=1.0 / SSD_W)\
                    .then_inc(rooted, 1)

            @block.gpsimd
            def _(pool):
                pool.wait_ge(g_ready, 1)
                for n, (way, c, _, _, _) in enumerate(steps):
                    if n >= 2:
                        pool.wait_ge(diff_mm, n - 1)
                    m = tri[:, GE if way else LE, :].rearrange("p (a t) -> p a t", a=1).to_broadcast([P, SSD_H, P])
                    pool.tensor_tensor(gu[:, n % 2, :, :], m, bcast(g[:, c, way, :], P), ALU.mult)\
                        .then_inc(gu_done, 1)
                    if n >= 2:
                        pool.wait_ge(intra_mm, n - 1)
                    pool.tensor_tensor(xdt[:, n % 2, :].rearrange("p (h v) -> p h v", v=SSD_P),
                                       x_tok[:, c, :].rearrange("p (h v) -> p h v", v=SSD_P),
                                       bcast(dt[:, c, way, :], SSD_P), ALU.mult).then_inc(xdt_done, 1)
                    pool.wait_ge(exps_done, n + 1)
                    pool.wait_ge(xdt_done, n + 1)
                    if n >= 2:
                        pool.wait_ge(state_mm, n - 1)
                    pool.tensor_tensor(xw[:, n % 2, :].rearrange("p (h v) -> p h v", v=SSD_P),
                                       xdt[:, n % 2, :].rearrange("p (h v) -> p h v", v=SSD_P),
                                       bcast(e3[:, n % 2, SSD_H:2 * SSD_H], SSD_P), ALU.mult).then_inc(xw_done, 1)
                for c in range(NT):
                    if c >= 1:
                        pool.wait_ge(skipped, 2 * c)
                    pool.tensor_tensor(dx[:, :].rearrange("p (h v) -> p h v", v=SSD_P),
                                       x_tok[:, c, :].rearrange("p (h v) -> p h v", v=SSD_P),
                                       bcast(skip, SSD_P), ALU.mult).then_inc(skipped, 1)

            @block.tensor
            def _(pe):
                def sums(n):
                    way, c, _, _, _ = steps[n]
                    if n >= 1:
                        pe.wait_ge(exps_done, n)
                    gr = g[:, c, way, :]
                    for k, m in enumerate(((LE, GT_), (GE, LT))[way]):
                        pe.matmul(ps[0][:, k * SSD_H:(k + 1) * SSD_H], tri[:, m, :], gr, start=True, stop=True)
                    pe.matmul(ps[0][:, 2 * SSD_H:3 * SSD_H], ones[:, :], gr, start=True, stop=True)\
                        .then_inc(sums_mm, 1)
                    if n >= 1:
                        pe.wait_ge(sm_done, n)
                    if n >= 2:
                        pe.wait_ge(s_done, n - 1)
                    for q in range(SSD_G):
                        rows = slice(q * SSD_P, (q + 1) * SSD_P)
                        last = pe.matmul(ps[1 + q][:, 0:P], k_t[rows, c * P:(c + 1) * P],
                                         q_t[rows, c * P:(c + 1) * P], start=True, stop=True)
                    last.then_inc(score_mm, 1)
                    pe.wait_ge(gu_done, n + 1)
                    if n >= 1:
                        pe.wait_ge(decay_done, n)
                    for b in range(2):
                        last = pe.matmul(ps[3 + b][:, :], tri[:, LT if way else GT_, :],
                                         gu[:, n % 2, 4 * b:4 * b + 4, :].rearrange("p h t -> p (h t)"),
                                         start=True, stop=True)
                    last.then_inc(diff_mm, 1)

                def outputs(n):
                    way, c, st_, _, before = steps[n]
                    pe.wait_ge(w_done, n + 1)
                    pe.wait_ge(xdt_done, n + 1)
                    if n >= 1:
                        pe.wait_ge(y_done, n)
                    for h in range(SSD_H):
                        last = pe.matmul(ps[5][:, h * SSD_P:(h + 1) * SSD_P], w[:, n % 2, h, :],
                                         xdt[:, n % 2, h * SSD_P:(h + 1) * SSD_P], start=True, stop=True)
                    last.then_inc(intra_mm, 1)
                    if before is not None:
                        pe.wait_ge(s_done, before + 1)
                    if n >= 1:
                        pe.wait_ge(scaled, n)
                    for q in range(SSD_G):
                        rows = slice(q * SSD_P, (q + 1) * SSD_P)
                        last = pe.matmul(ps[6 + q][:, 0:256], q_t[rows, c * P:(c + 1) * P],
                                         state[rows, st_, :], start=True, stop=True)
                    last.then_inc(inter_mm, 1)
                    pe.wait_ge(xw_done, n + 1)
                    pe.wait_ge(sm_done, min(n + 2, n_steps))
                    for q in range(SSD_G):
                        rows = slice(q * SSD_P, (q + 1) * SSD_P)
                        last = pe.matmul(ps[1][rows, 256:512], k_tok[:, c, rows], xw[:, n % 2, q * 256:(q + 1) * 256],
                                         start=True, stop=True)
                    last.then_inc(state_mm, 1)

                pe.wait_ge(state_in, 16)
                pe.wait_ge(zeroed, 1)
                pe.wait_ge(g_ready, 1)
                sums(0)
                for n in range(n_steps):
                    if n + 1 < n_steps:
                        sums(n + 1)
                    outputs(n)

            @block.vector
            def _(dve):
                dve.memset(state[:, 0:2, :], 0.0).then_inc(zeroed, 1)
                dve.wait_ge(dt_in, 16)
                dve.wait_ge(dt_step, 1)
                n_dt = [1]

                def chain(op):
                    op.then_inc(dt_step, 1)
                    n_dt[0] += 1
                    dve.wait_ge(dt_step, n_dt[0])

                dt_r = dt[:, :, :, :].rearrange("p t w h -> p t (w h)")
                st_r = [st[:, j, :].rearrange("p (t n) -> p t n", t=NT) for j in range(3)]
                bias_b = bias.rearrange("p (a n) -> p a n", a=1).to_broadcast([P, NT, 2 * SSD_H])
                dve.tensor_tensor(st_r[0], dt_r, bias_b, ALU.add).then_inc(dt_step, 1)
                n_dt[0] = 4
                dve.wait_ge(dt_step, 4)
                chain(dve.tensor_scalar(st[:, 2, :], st[:, 1, :], 2.0, None, ALU.add))
                chain(dve.reciprocal(st[:, 2, :], st[:, 2, :]))
                chain(dve.tensor_tensor(st[:, 1, :], st[:, 1, :], st[:, 2, :], ALU.mult))
                chain(dve.tensor_tensor(st[:, 2, :], st[:, 1, :], st[:, 1, :], ALU.mult))
                poly = dt[:, :, :, :].rearrange("p t w h -> p (t w h)")
                chain(dve.tensor_scalar(poly, st[:, 2, :], 1.0 / 15, None, ALU.mult))
                for odd in (13, 11, 9, 7, 5, 3):
                    chain(dve.scalar_tensor_tensor(poly, poly, 1.0 / odd, st[:, 2, :], ALU.add, ALU.mult))
                chain(dve.scalar_tensor_tensor(poly, poly, 1.0, st[:, 1, :], ALU.add, ALU.mult))
                chain(dve.tensor_scalar(st[:, 0, :], st[:, 0, :], 0.0, None, ALU.max))
                chain(dve.scalar_tensor_tensor(poly, poly, 2.0, st[:, 0, :], ALU.mult, ALU.add))
                a_b = neg_a[:, :].rearrange("p (a n) -> p a n", a=1).to_broadcast([P, NT, 2 * SSD_H])
                dve.scalar_tensor_tensor(g[:, :, :, :].rearrange("p t w h -> p t (w h)"), dt_r, -1.0, a_b,
                                         ALU.mult, ALU.mult).then_inc(g_ready, 1)

                def weigh(n):
                    way, c, _, _, _ = steps[n]
                    dve.wait_ge(score_mm, n + 1)
                    if n >= 2:
                        dve.wait_ge(w_done, n - 1)
                    for q in range(SSD_G):
                        last = dve.tensor_tensor(sm[:, n % 2, q, :], ps[1 + q][:, 0:P],
                                                 tri[:, GE if way else LE, :], ALU.mult)
                    last.then_inc(sm_done, 1)
                    dve.wait_ge(decay_done, n + 1)
                    dve.wait_ge(sm_done, n + 1)
                    for q in range(SSD_G):
                        mb = sm[:, n % 2, q, :].rearrange("p (a t) -> p a t", a=1).to_broadcast([P, HG, P])
                        last = dve.tensor_tensor(w[:, n % 2, HG * q:HG * (q + 1), :],
                                                 w[:, n % 2, HG * q:HG * (q + 1), :], mb, ALU.mult)
                    last.then_inc(w_done, 1)

                ys = [0]

                def gather(n):
                    way, c, st_, first, _ = steps[n]
                    y = y_tok[:, c, 0:SSD_W]
                    dve.wait_ge(inter_mm, n + 1)
                    dve.wait_ge(exps_done, n + 1)
                    if n >= 2:
                        dve.wait_ge(y_done, n - 1)
                    for q in range(SSD_G):
                        last = dve.tensor_tensor(
                            t1[:, n % 2, q * 256:(q + 1) * 256].rearrange("p (h v) -> p h v", v=SSD_P),
                            ps[6 + q][:, 0:256].rearrange("p (h v) -> p h v", v=SSD_P),
                            bcast(e3[:, n % 2, q * HG:(q + 1) * HG], SSD_P), ALU.mult)
                    last.then_inc(scaled, 1)
                    for q in range(SSD_G):
                        rows = slice(q * SSD_P, (q + 1) * SSD_P)
                        e = e3[rows, n % 2, 2 * SSD_H + q * HG:2 * SSD_H + (q + 1) * HG]
                        sr = state[rows, st_, :].rearrange("p (h v) -> p h v", v=SSD_P)
                        dve.tensor_tensor(sr, sr, bcast(e, SSD_P), ALU.mult).then_inc(faded, 1)
                    dve.wait_ge(state_mm, n + 1)
                    dve.wait_ge(faded, 2 * n + 2)
                    dve.tensor_tensor(state[:, st_, :], state[:, st_, :], ps[1][:, 256:512], ALU.add)\
                        .then_inc(s_done, 1)
                    dve.wait_ge(intra_mm, n + 1)
                    dve.wait_ge(scaled, n + 1)
                    if first:
                        dve.tensor_tensor(y, t1[:, n % 2, :], ps[5][:, :], ALU.add).then_inc(y_done, 1)
                    else:
                        dve.tensor_tensor(t1[:, n % 2, :], t1[:, n % 2, :], ps[5][:, :], ALU.add)\
                            .then_inc(y_step, 1)
                        ys[0] += 1
                        dve.wait_ge(y_step, ys[0])
                        dve.tensor_tensor(y, y, t1[:, n % 2, :], ALU.add).then_inc(y_done, 1)

                weigh(0)
                for n in range(n_steps):
                    if n + 1 < n_steps:
                        weigh(n + 1)
                    if n == 0:
                        dve.wait_ge(zeroed, 1)
                        dve.wait_ge(state_in, 16)
                    before = steps[n][4]
                    if before is not None:
                        dve.wait_ge(s_done, before + 1)
                    gather(n)
                dve.wait_ge(y_done, n_steps)
                for c in range(NT):
                    y = y_tok[:, c, 0:SSD_W]
                    dve.wait_ge(skipped, 2 * c + 1)
                    dve.tensor_tensor(y, y, dx[:, :], ALU.add).then_inc(skipped, 1)
                    dve.wait_ge(skipped, 2 * c + 2)
                    dve.wait_ge(z_act, c + 1)
                    dve.tensor_tensor(y, y, z[:, c, :], ALU.mult).then_inc(gated, 1)
                dve.wait_ge(rooted, 1)
                dve.reciprocal(rs[:, 1, :], rs[:, 0, :]).then_inc(rooted, 1)
                dve.wait_ge(rooted, 2)
                for c in range(NT):
                    y = y_tok[:, c, 0:SSD_W]
                    dve.scalar_tensor_tensor(y, y, rs[:, 1, c:c + 1], norm_w, ALU.mult, ALU.mult).then_inc(normed, 1)


GRID_W, GRID_H = 64, LAT // 64
WIN_R, WIN_C = 8, 16
NA_H, NA_D = 8, 64
PAIRS = NA_H // 2
LOC = WIN_R * GRID_W
KEYS = LOC + CTX


def na(nc, tag, d, y_tok, ident, eps):
    units = [(r, p) for r in range(GRID_H) for p in range(PAIRS)] + [(None, h) for h in range(NA_H)]
    with Scope(nc, tag) as s:
        q_two = s.sb("q_two", [P, PAIRS, GRID_H, 2, GRID_W])
        q_ctx = s.sb("q_ctx", [P, PAIRS, CTX])
        k_t = s.sb("k_t", [P, PAIRS, TOK])
        k_old = s.sb("k_old", [P, PAIRS, CTX])
        bias = s.sb("bias", [P, PAIRS, 2 * WIN_R - 1, GRID_W])
        v_even, v_odd = s.sb("v_even", [P, 8, 512]), s.sb("v_odd", [P, 7, 512])
        v_ctx = s.sb("v_ctx", [P, 2, 512])
        ps = s.banks(8)
        loaded = s.sem("loaded")
        with Scope(nc, tag + "n") as c:
            tiles = [(kind, pair + i) for pair in range(0, PAIRS, 2) for kind in "qk" for i in range(2)]
            u = c.sb("u", [P, 2, TOK])
            sq = c.sb("sq", [P, 4, TOK])
            half = c.sb("half", [P, P])
            gain = c.sb("gain", [P, 2])
            small, kept = c.sem("small"), c.sem("kept")
            arrived = [c.sem(f"arrived{j}") for j in range(2 * PAIRS)]
            zeroed, squared, summed, logged = c.sem("zeroed"), c.sem("squared"), c.sem("summed"), c.sem("logged")
            inverted, normed, scaled = c.sem("inverted"), c.sem("normed"), c.sem("scaled")
            ends = [sum(3 if kind == "q" else 1 for kind, _ in tiles[:j]) for j in range(2 * PAIRS + 1)]

            def source(j):
                kind, pair = tiles[j]
                return u[:, pair % 2, :] if kind == "q" else k_t[:, pair, :]

            with nc.Block() as block:
                @block.sync
                def _(sp):
                    for j, (kind, pair) in enumerate(tiles):
                        if kind == "q" and pair >= 2:
                            sp.wait_ge(normed, ends[tiles.index(("q", pair - 2)) + 1])
                        sp.dma_start(source(j), d["u0_t"][6 + pair + (0 if kind == "q" else PAIRS)])\
                            .then_inc(arrived[j], 16)
                        if j == 0:
                            sp.dma_start(half[:, :], d["half"]).then_inc(small, 16)
                            sp.dma_start(gain[:, :], d["qk_gain"]).then_inc(small, 16)
                    tok = d["u0_tok"].rearrange("t p n -> (t p) n")
                    sp.dma_start(k_old[:, :, :], d["k_old"]).then_inc(loaded, 16)
                    sp.dma_start(bias[:, :, :, :], d["na_bias"]).then_inc(loaded, 16)
                    sp.dma_start(v_ctx[:, 0, :], d["v_old"]).then_inc(loaded, 16)
                    sp.dma_start(v_ctx[:, 1, :], tok[0:CTX, 512:1024]).then_inc(loaded, 16)
                    sp.dma_start(v_even[:, :, :], tok[CTX:TOK, 512:1024].rearrange("(t p) n -> p t n", p=P))\
                        .then_inc(loaded, 16)
                    sp.dma_start(v_odd[:, :, :], tok[CTX + 64:TOK - 64, 512:1024].rearrange("(t p) n -> p t n", p=P))\
                        .then_inc(loaded, 16)
                    sp.wait_ge(loaded, 96)
                    sp.dma_start(d["o_v"], v_ctx[:, 1, :]).then_inc(kept, 16)
                    sp.wait_ge(normed, ends[-1])
                    sp.dma_start(d["o_k"], k_t[:, :, 0:CTX]).then_inc(kept, 16)
                    sp.wait_ge(kept, 32)

                @block.gpsimd
                def _(pool):
                    pool.memset(q_two[:, :, :, :, :], 0.0).then_inc(zeroed, 1)

                @block.scalar
                def _(act):
                    for m in range(PAIRS):
                        for j in (2 * m, 2 * m + 1):
                            act.wait_ge(summed, j + 1)
                            for b in range(NB):
                                act.activation(sq[:, j % 4, b * BLK:(b + 1) * BLK], ps[3 * (j % 2) + b][:, 0:BLK],
                                               ACT.Ln, bias=eps[:, 0:1], scale=1.0 / NA_D).then_inc(logged, 1)
                        for j in (2 * m, 2 * m + 1):
                            act.wait_ge(logged, NB * (j + 1))
                            act.activation(sq[:, j % 4, :], sq[:, j % 4, :], ACT.Exp, scale=-0.5).then_inc(inverted, 1)

                @block.tensor
                def _(pe):
                    pe.wait_ge(small, 32)
                    for j in range(2 * PAIRS):
                        pe.wait_ge(squared, j + 1)
                        if j >= 2:
                            pe.wait_ge(logged, NB * (j - 1))
                        for b in range(NB):
                            last = pe.matmul(ps[3 * (j % 2) + b][:, 0:BLK], half[:, :],
                                             sq[:, j % 4, b * BLK:(b + 1) * BLK], start=True, stop=True)
                        last.then_inc(summed, 1)

                @block.vector
                def _(dve):
                    def square(j):
                        dve.wait_ge(arrived[j], 16)
                        if j >= 4:
                            dve.wait_ge(normed, ends[j - 3])
                        dve.tensor_tensor(sq[:, j % 4, :], source(j), source(j), ALU.mult).then_inc(squared, 1)

                    for j in range(4):
                        square(j)
                    dve.wait_ge(small, 32)
                    dve.tensor_scalar(gain[:, 0:1], gain[:, 0:1], NA_D ** -0.5, None, ALU.mult).then_inc(scaled, 1)
                    dve.wait_ge(scaled, 1)
                    dve.wait_ge(zeroed, 1)
                    for j, (kind, pair) in enumerate(tiles):
                        dve.wait_ge(inverted, j + 1)
                        src, inv = source(j), sq[:, j % 4, :]
                        if kind == "q":
                            dve.scalar_tensor_tensor(q_ctx[:, pair, :], src[:, 0:CTX], gain[:, 0:1], inv[:, 0:CTX],
                                                     ALU.mult, ALU.mult).then_inc(normed, 1)
                            for e in range(2):
                                rows = slice(64 * e, 64 * e + 64)
                                shape = "p (r c) -> p r c"
                                dve.scalar_tensor_tensor(q_two[rows, pair, :, e, :],
                                                         src[rows, CTX:TOK].rearrange(shape, c=GRID_W),
                                                         gain[rows, 0:1],
                                                         inv[rows, CTX:TOK].rearrange(shape, c=GRID_W),
                                                         ALU.mult, ALU.mult).then_inc(normed, 1)
                        else:
                            dve.scalar_tensor_tensor(src, src, gain[:, 1:2], inv, ALU.mult, ALU.mult).then_inc(normed, 1)
                        if j + 4 < 2 * PAIRS:
                            square(j + 4)

        sc = s.sb("sc", [P, 3, KEYS])
        pt = s.sb("pt", [P, 2, 5, P])
        zero = s.sb("zero", [P, CTX])
        mx = s.sb("mx", [P, 3, 3])
        den = s.sb("den", [P, 2, 2])
        zeroed, scored, peak, biased = s.sem("zeroed"), s.sem("scored"), s.sem("peak"), s.sem("biased")
        exp_done, rec, weighed = s.sem("exp_done"), s.sem("rec"), s.sem("weighed")
        turned, copied, pv_mm, stored = s.sem("turned"), s.sem("copied"), s.sem("pv_mm"), s.sem("stored")
        n_units = len(units)

        def window(r):
            return min(max(r - WIN_R // 2, 0), GRID_H - WIN_R)

        with nc.Block() as block:
            @block.tensor
            def _(pe):
                pe.wait_ge(loaded, 96)

                def score(n):
                    r, p = units[n]
                    if n >= 2:
                        pe.wait_ge(biased, n - 1)
                    if r is None:
                        rows = slice(64 * (p % 2), 64 * (p % 2) + 64)
                        pe.matmul(ps[2 + n % 2][:, 0:CTX], q_ctx[rows, p // 2, :], k_t[rows, p // 2, 0:CTX],
                                  start=True, stop=True).then_inc(scored, 1)
                        return
                    q = q_two[:, p, r, :, :].rearrange("p e c -> p (e c)")
                    at = CTX + window(r) * GRID_W
                    pe.matmul(ps[n % 2][:, :], q, k_t[:, p, at:at + LOC], start=True, stop=True)
                    pe.matmul(ps[2 + n % 2][:, 0:CTX], q, k_old[:, p, :], start=True, stop=True).then_inc(scored, 1)

                def turn(n):
                    r, p = units[n]
                    pe.wait_ge(weighed, n + 1)
                    if n >= 1:
                        pe.wait_ge(copied, n)
                    for c in range(4 if r is None else 0, 5):
                        bank = ps[4][:, c * P:(c + 1) * P] if c < 4 else ps[5][:, 0:P]
                        last = pe.transpose(bank, sc[:, n % 3, c * P:(c + 1) * P], ident[:, :])
                    last.then_inc(turned, 1)

                def values(n):
                    r, p = units[n]
                    pe.wait_ge(copied, n + 1)
                    if n >= 2:
                        pe.wait_ge(stored, n - 1)
                    bank = ps[6 + n % 2]
                    if r is None:
                        pe.matmul(bank[:, 0:NA_D], pt[:, n % 2, 4, :], v_ctx[:, 1, p * NA_D:(p + 1) * NA_D],
                                  start=True, stop=True).then_inc(pv_mm, 1)
                        return
                    rs, rows = window(r), slice(64 * (r % 2), 64 * (r % 2) + 64)
                    tiles_ = [(v_odd if rs % 2 else v_even)[:, rs // 2 + c, :] for c in range(4)] + [v_ctx[:, 0, :]]
                    for e in range(2):
                        col = slice((2 * p + e) * NA_D, (2 * p + e + 1) * NA_D)
                        for c in range(5):
                            last = pe.matmul(bank[rows, e * NA_D:(e + 1) * NA_D], pt[:, n % 2, c, 64 * e:64 * e + 64],
                                             tiles_[c][:, col], start=(c == 0), stop=(c == 4))
                    last.then_inc(pv_mm, 1)

                for i in range(n_units + 3):
                    if i < n_units:
                        score(i)
                    if 0 <= i - 2 < n_units:
                        turn(i - 2)
                    if i >= 3:
                        values(i - 3)

            @block.vector
            def _(dve):
                dve.memset(zero[:, :], 0.0).then_inc(zeroed, 1)
                dve.wait_ge(zeroed, 1)
                dve.wait_ge(loaded, 96)
                peaks = [0]

                def scores(n):
                    r, p = units[n]
                    dve.wait_ge(scored, n + 1)
                    if n >= 3:
                        dve.wait_ge(turned, n - 2)
                    m = mx[:, n % 3, :]
                    first = m[:, 1:2] if r is None else m[:, 0:1]
                    dve.tensor_tensor_reduce(sc[:, n % 3, LOC:KEYS], ps[2 + n % 2][:, 0:CTX], zero[:, :], 1.0, -3e38,
                                             ALU.add, ALU.max, first).then_inc(peak, 1)
                    peaks[0] += 1
                    dve.wait_ge(peak, peaks[0])
                    if r is not None:
                        dr = window(r) - r + WIN_R - 1
                        dve.tensor_tensor_reduce(sc[:, n % 3, 0:LOC], ps[n % 2][:, :],
                                                 bias[:, p, dr:dr + WIN_R, :].rearrange("p a c -> p (a c)"), 1.0,
                                                 m[:, 0:1], ALU.add, ALU.max, m[:, 1:2]).then_inc(peak, 1)
                        peaks[0] += 1
                        dve.wait_ge(peak, peaks[0])
                    dve.tensor_scalar(m[:, 2:3], m[:, 1:2], -1.0, None, ALU.mult).then_inc(biased, 1)

                def weigh(n):
                    lo = 0 if units[n][0] is not None else LOC
                    dve.wait_ge(exp_done, n + 1)
                    dve.reciprocal(den[:, n % 2, 1:2], den[:, n % 2, 0:1]).then_inc(rec, 1)
                    dve.wait_ge(rec, n + 1)
                    dve.tensor_scalar(sc[:, n % 3, lo:KEYS], sc[:, n % 3, lo:KEYS], den[:, n % 2, 1:2], None,
                                      ALU.mult).then_inc(weighed, 1)

                for i in range(n_units + 1):
                    if i < n_units:
                        scores(i)
                    if i >= 1:
                        weigh(i - 1)

            @block.scalar
            def _(act):
                def exps(n):
                    lo = 0 if units[n][0] is not None else LOC
                    act.wait_ge(biased, n + 1)
                    if n >= 2:
                        act.wait_ge(weighed, n - 1)
                    act.activation(sc[:, n % 3, lo:KEYS], sc[:, n % 3, lo:KEYS], ACT.Exp, bias=mx[:, n % 3, 2:3],
                                   accum_out=den[:, n % 2, 0:1]).then_inc(exp_done, 1)

                def copy(n):
                    act.wait_ge(turned, n + 1)
                    if n >= 2:
                        act.wait_ge(pv_mm, n - 1)
                    if units[n][0] is not None:
                        act.activation(pt[:, n % 2, 0:4, :].rearrange("p c q -> p (c q)"), ps[4][:, :], ACT.Copy)
                    act.activation(pt[:, n % 2, 4, :], ps[5][:, 0:P], ACT.Copy).then_inc(copied, 1)

                def store(n):
                    r, p = units[n]
                    act.wait_ge(pv_mm, n + 1)
                    if r is None:
                        out, src = y_tok[:, 0, 512 + p * NA_D:512 + (p + 1) * NA_D], ps[6 + n % 2][:, 0:NA_D]
                    else:
                        rows = slice(64 * (r % 2), 64 * (r % 2) + 64)
                        out = y_tok[rows, 1 + r // 2, 512 + 2 * p * NA_D:512 + 2 * (p + 1) * NA_D]
                        src = ps[6 + n % 2][rows, 0:2 * NA_D]
                    act.activation(out, src, ACT.Copy).then_inc(stored, 1)

                for i in range(n_units + 3):
                    if i < n_units:
                        exps(i)
                    if 0 <= i - 2 < n_units:
                        copy(i - 2)
                    if i >= 3:
                        store(i - 3)


LIN_PAIRS = LIN_H // 2
RANK = 16
CH = 3
UW = CH * P
LEVELS = (64, 32, 16, 8, 4, 2, 1)
NL = len(LEVELS)


def lin_gates(nc, tag, d):
    with Scope(nc, tag) as s:
        a_t = s.sb("a_t", [2 * RANK, TOK])
        wa = s.sb("wa", [2 * RANK, 2, 2, P])
        vec = s.sb("vec", [P, 2, 2, 3])
        lb = s.sb("lb", [P, 4, 5])
        lw = s.sb("lw", [P, 4, 2])
        x = s.sb("x", [P, 4, TOK])
        neg, log1 = s.sb("neg", [P, 4, TOK]), s.sb("log1", [P, 4, TOK])
        g = s.sb("g", [P, 4, TOK])
        k = s.sb("k", [P, 4, TOK])
        ps = s.banks(8)
        small, arrived = s.sem("small"), s.sem("arrived")
        gate_mm = s.sem("gate_mm")
        bound, sig, f_done, k_done, ln_done = s.sem("bound"), s.sem("sig"), s.sem("f_done"), s.sem("k_done"), s.sem("ln_done")
        abs_done, exp_done, log_done, neg_done, g_done = (s.sem("abs_done"), s.sem("exp_done"), s.sem("log_done"),
                                                          s.sem("neg_done"), s.sem("g_done"))
        q_scaled, added = s.sem("q_scaled"), s.sem("added")
        stored = s.sem("stored")
        qs, q_in = s.sb("qs", [P, 2, TOK]), s.sem("q_in")

        def bank(j, b):
            return ps[3 * ((j + 1) % 2) + b][:, 0:BLK]

        with nc.Block() as block:
            @block.sync
            def _(sp):
                sp.dma_start(a_t[:, :], d["u1_small"]).then_inc(small, 16)
                sp.dma_start(wa[:, :, :, :], d["wa2"]).then_inc(small, 16)
                sp.dma_start(vec[:, :, :, :], d["lin_vec"]).then_inc(small, 16)
                for j in range(4):
                    sp.dma_start(x[:, j, :], d["u1_t"][6 + j]).then_inc(arrived, 16)
                for j in range(2):
                    sp.dma_start(qs[:, j, :], d["u1_t"][j]).then_inc(q_in, 16)
                for j in range(4):
                    way, tile = divmod(j, 2)
                    sp.wait_ge(k_done, j + 1)
                    sp.dma_start(d["lin_k"][2 * tile + way], k[:, j, :]).then_inc(stored, 16)
                sp.wait_ge(q_scaled, 2)
                for j in range(2):
                    sp.dma_start(d["lin_q"][j], qs[:, j, :]).then_inc(stored, 16)
                for j in range(4):
                    way, tile = divmod(j, 2)
                    sp.wait_ge(ln_done, j + 1)
                    sp.dma_start(d["lin_g"][2 * (2 + tile) + way], x[:, j, :]).then_inc(stored, 16)
                for j in range(4):
                    way, tile = divmod(j, 2)
                    sp.wait_ge(g_done, j + 1)
                    sp.dma_start(d["lin_g"][2 * tile + way], g[:, j, :]).then_inc(stored, 16)
                sp.wait_ge(stored, 16 * 14)

            @block.tensor
            def _(pe):
                pe.wait_ge(small, 48)
                for j in range(4):
                    way, tile = divmod(j, 2)
                    if j >= 2:
                        pe.wait_ge(abs_done, 3 * (j - 1))
                        pe.wait_ge(neg_done, 3 * (j - 1))
                    for b in range(NB):
                        pe.matmul(bank(j, b), wa[:, way, tile, :], a_t[:, b * BLK:(b + 1) * BLK],
                                  start=True, stop=True).then_inc(gate_mm, 1)

            @block.scalar
            def _(act):
                act.wait_ge(bound, 2)
                act.activation(lw[:, :, :], lw[:, :, :], ACT.Exp).then_inc(bound, 1)
                for j in range(4):
                    way, tile = divmod(j, 2)
                    for b in range(NB):
                        act.wait_ge(gate_mm, 3 * j + b + 1)
                        act.activation(log1[:, j, b * BLK:(b + 1) * BLK], bank(j, b), ACT.Abs,
                                       bias=vec[:, way, tile, 0:1]).then_inc(abs_done, 1)
                for j in range(4):
                    act.wait_ge(abs_done, 3 * j + 3)
                    act.activation(log1[:, j, :], log1[:, j, :], ACT.Exp, scale=-1.0).then_inc(exp_done, 1)
                act.wait_ge(arrived, 64)
                for j in range(4):
                    act.activation(x[:, j, :], x[:, j, :], ACT.Sigmoid).then_inc(sig, 1)
                for j in range(4):
                    act.wait_ge(exp_done, j + 1)
                    act.activation(log1[:, j, :], log1[:, j, :], ACT.Ln, bias=1.0).then_inc(log_done, 1)
                act.wait_ge(q_in, 32)
                for j in range(2):
                    act.activation(qs[:, j, :], qs[:, j, :], ACT.Copy, scale=LIN_K ** -0.5).then_inc(q_scaled, 1)
                act.wait_ge(k_done, 4)
                for j in range(4):
                    act.wait_ge(f_done, 5 + j)
                    act.activation(x[:, j, :], x[:, j, :], ACT.Ln).then_inc(ln_done, 1)

            @block.vector
            def _(dve):
                dve.wait_ge(small, 48)
                v = vec[:, :, :, :].rearrange("p w t n -> p (w t) n")
                dve.tensor_tensor(lb[:, :, 0], v[:, :, 1], v[:, :, 2], ALU.max).then_inc(bound, 1)
                dve.wait_ge(bound, 1)
                dve.tensor_tensor(lw[:, :, :], v[:, :, 1:3], bcast(lb[:, :, 0], 2), ALU.subtract).then_inc(bound, 1)
                dve.wait_ge(bound, 3)
                dve.tensor_tensor(lb[:, :, 1], lw[:, :, 0], lw[:, :, 1], ALU.add).then_inc(bound, 1)
                dve.wait_ge(bound, 4)
                dve.reciprocal(lb[:, :, 2], lb[:, :, 1]).then_inc(bound, 1)
                dve.wait_ge(bound, 5)
                dve.tensor_tensor(lb[:, :, 3], lw[:, :, 1], lb[:, :, 2], ALU.mult).then_inc(bound, 1)
                dve.wait_ge(bound, 6)
                dve.tensor_scalar(lb[:, :, 4], lb[:, :, 3], -1.0, 1.0, ALU.mult, ALU.add).then_inc(bound, 1)
                dve.wait_ge(bound, 7)
                for j in range(4):
                    way, tile = divmod(j, 2)
                    for b in range(NB):
                        dve.wait_ge(gate_mm, 3 * j + b + 1)
                        dve.wait_ge(abs_done, 3 * j + b + 1)
                        dve.tensor_scalar(neg[:, j, b * BLK:(b + 1) * BLK], bank(j, b), vec[:, way, tile, 0:1], 0.0,
                                          ALU.add, ALU.min).then_inc(neg_done, 1)
                for j in range(4):
                    dve.wait_ge(sig, j + 1)
                    dve.tensor_scalar(x[:, j, :], x[:, j, :], lb[:, j, 4:5], lb[:, j, 3:4], ALU.mult, ALU.add)\
                        .then_inc(f_done, 1)
                    dve.wait_ge(f_done, j + 1)
                    dve.tensor_scalar(k[:, j, :], x[:, j, :], -1.0, 1.0, ALU.mult, ALU.add).then_inc(k_done, 1)
                for j in range(4):
                    dve.wait_ge(k_done, 4)
                    dve.tensor_scalar(x[:, j, :], x[:, j, :], 2.0 ** -63, None, ALU.max).then_inc(f_done, 1)
                for j in range(4):
                    dve.wait_ge(log_done, j + 1)
                    dve.wait_ge(neg_done, 3 * j + 3)
                    dve.tensor_tensor(neg[:, j, :], neg[:, j, :], log1[:, j, :], ALU.subtract).then_inc(added, 1)
                    dve.wait_ge(added, j + 1)
                    dve.tensor_scalar(g[:, j, :], neg[:, j, :], 1.0 / 16, None, ALU.mult).then_inc(g_done, 1)


def lin_units():
    out = []
    for pair in range(LIN_PAIRS):
        for way in range(2):
            for n in range(NT // CH):
                c0 = CH * n if way == FWD else NT - CH * (n + 1)
                out.append((pair, way, 2 * pair + way, c0, n))
    return out


def linear_scans(nc, tag, d, y_tok, ident):
    units = lin_units()
    n_units = len(units)
    per_item = NT // CH
    half = P // 2
    pieces = 3
    per_piece = (NL + 2) // pieces

    def piece(j):
        return (2 + j) // per_piece

    with Scope(nc, tag) as s:
        q, k, g = s.sb("q", [P, 2, TOK]), s.sb("k", [P, 2, TOK]), s.sb("g", [P, 2, TOK])
        v = s.sb("v", [P, 2, NT, 2 * LIN_V])
        reset = s.sb("reset", [P, TOK], BF16)
        run = s.sb("run", [P, 2, TOK])
        f = s.sb("f", [P, 2, NL + 2, UW])
        qz = s.sb("qz", [P, 2, NL, CH, 2, half])
        kq = s.sb("kq", [P, UW])
        q_in, k_end = s.sb("q_in", [P, 2, 2, UW]), s.sb("k_end", [P, UW])
        k_tok = s.sb("k_tok", [P, UW])
        sel = s.sb("sel", [P, 2])
        decay = s.sb("decay", [P, 2, CH])
        dot = s.sb("dot", [P, CH, 2])
        att = s.sb("att", [P, 2, CH, 2, P])
        state = s.sb("state", [P, 2, NT + 2, LIN_V])
        mask = s.sb("mask", [P, 2, NL, half], I16)
        ps = s.banks(8)
        masks_in = s.sem("masks_in")
        g_in, qk_in, v_in = ([s.sem(f"{name}{i}") for i in range(2)] for name in ("g_in", "qk_in", "v_in"))
        kept = [s.sem("kept0"), s.sem("kept1")]
        zeroed, ran, inclusive, z_done = s.sem("zeroed"), s.sem("ran"), s.sem("inclusive"), s.sem("z_done")
        short, reset_done, sel_done = s.sem("short"), s.sem("reset_done"), s.sem("sel_done")
        expo, fact, mixed, ends = s.sem("expo"), s.sem("fact"), s.sem("mixed"), s.sem("ends")
        turned, k_copied, gain_mm, s_done = s.sem("turned"), s.sem("k_copied"), s.sem("gain_mm"), s.sem("s_done")
        q_done = s.sem("q_done")
        dotted, diag = s.sem("dotted"), s.sem("diag")
        score_mm, picked, out_mm = s.sem("score_mm"), s.sem("picked"), s.sem("out_mm")
        y_done = [s.sem("y_fwd"), s.sem("y_bwd")]

        def keep(sp, it):
            a, way = it % 2, it % 2
            sp.wait_ge(s_done, CH * (per_item * it + (1 if way == FWD else per_item)))
            sp.dma_start(d["o_lin"][it], state[:, a, NT, :]).then_inc(kept[a], 16)

        def blocks(ap, size):
            return ap.rearrange("p (b w) -> p b w", w=2 * size)

        def by_tile(ap, size, lo):
            return ap.rearrange("p (c b w) -> p c b w", c=CH, w=2 * size)[:, :, :, lo:lo + size]

        def rows_of(h):
            return slice(half * h, half * (h + 1))

        def q_row(way):
            return 0 if way == FWD else 1

        with nc.Block() as block:
            @block.sync
            def _(sp):
                sp.dma_start(mask[:, :, :, :], d["lin_mask"]).then_inc(masks_in, 16)
                sp.wait_ge(zeroed, 1)
                for it in range(2 * LIN_PAIRS):
                    pair, way = divmod(it, 2)
                    a = it % 2
                    done = per_item * (it - 1)
                    if it >= 2:
                        sp.wait_ge(expo, pieces * done)
                    sp.dma_start(g[:, a, :], d["lin_g"][it]).then_inc(g_in[a], 16)
                    if it >= 2:
                        sp.wait_ge(mixed, NL * done)
                        sp.wait_ge(ends, done)
                        sp.wait_ge(q_done, done)
                    sp.dma_start(q[:, a, :], d["lin_q"][pair] if pair < 2 else d["u1_t"][2 + pair])\
                        .then_inc(qk_in[a], 16)
                    sp.dma_start(k[:, a, :], d["u1_t"][2 + pair] if pair < 2 else d["lin_k"][it - 4])\
                        .then_inc(qk_in[a], 16)
                    if it >= 2:
                        sp.wait_ge(y_done[way], 2 * per_item * (it // 2))
                        sp.wait_ge(kept[a], 16 * (it // 2))
                    at = 2 * pair * LIN_V + (512 if pair >= 2 else 0)
                    sp.dma_start(v[:, a, :, :], d["u1_tok"][:, :, at:at + 2 * LIN_V].rearrange("t p n -> p t n"))\
                        .then_inc(v_in[a], 16)
                    sp.dma_start(state[:, a, 1 if way == FWD else NT - 1, :], d["lin_state"][it])\
                        .then_inc(v_in[a], 16)
                    if it >= 1:
                        keep(sp, it - 1)
                keep(sp, 2 * LIN_PAIRS - 1)
                for a in range(2):
                    sp.wait_ge(kept[a], 16 * LIN_PAIRS)

            @block.gpsimd
            def _(pool):
                pool.memset(state[:, :, 0, :], 0.0).then_inc(zeroed, 1)

                def level(n, j):
                    _, way, it, c0, _ = units[n]
                    size = LEVELS[j]
                    xb = blocks(run[:, it % 2, c0 * P:(c0 + CH) * P], size)
                    ob = blocks(f[:, n % 2, 2 + j, :], size)
                    mid = size - 1 if way == FWD else size
                    ref = xb[:, :, mid:mid + 1].to_broadcast([P, UW // (2 * size), size])
                    pool.tensor_tensor(ob[:, :, size:2 * size], xb[:, :, size:2 * size], ref, ALU.subtract)
                    return pool.tensor_tensor(ob[:, :, 0:size], ref, xb[:, :, 0:size], ALU.subtract)

                def free(n, p):
                    if n >= 2:
                        pool.wait_ge(score_mm, NL * (n - 2) + per_piece * (p + 1) - 2)

                def against_state(n):
                    _, way, it, c0, first = units[n]
                    cols = slice(c0 * P, (c0 + CH) * P)
                    xb = blocks(run[:, it % 2, cols], half)
                    gb = blocks(g[:, it % 2, cols], half)
                    out = blocks(f[:, n % 2, 1, :], half)
                    last = xb[:, :, P - 1:P].to_broadcast([P, CH, P])
                    instr = pool.tensor_tensor(out, last, xb, ALU.subtract)
                    if way == BWD:
                        own = gb[:, :, P - 1:P].to_broadcast([P, CH, P])
                        instr.then_inc(short, 1)
                        pool.wait_ge(short, it // 2 * per_item + first + 1)
                        pool.tensor_tensor(out, out, own, ALU.add)

                for n, (pair, way, it, c0, _) in enumerate(units):
                    a, r = it % 2, n % 2
                    cols = slice(c0 * P, (c0 + CH) * P)
                    pool.wait_ge(ran, it + 1)
                    free(n, 0)
                    if n >= 2:
                        pool.wait_ge(ends, n - 1)
                        pool.wait_ge(q_done, n - 1)
                    against_state(n)
                    level(n, 0).then_inc(expo, 1)
                    free(n, 1)
                    for j in range(NL):
                        if piece(j) == 1:
                            last = level(n, j)
                    last.then_inc(expo, 1)
                    if n >= 1:
                        pool.wait_ge(turned, n)
                    pool.wait_ge(qk_in[a], 32 * (it // 2 + 1))
                    pool.tensor_tensor(kq[:, :], q[:, a, cols], k[:, a, cols], ALU.mult)
                    pool.wait_ge(fact, pieces * n + 1)
                    if n >= 2:
                        pool.wait_ge(s_done, CH * (n - 1))
                    at = P - 1 if way == FWD else 0
                    pool.tensor_copy(decay[:, r, :], f[:, r, q_row(way), at:UW:P])
                    pool.tensor_tensor(k_end[:, :], k[:, a, cols], f[:, r, 1 - q_row(way), :], ALU.mult)\
                        .then_inc(ends, 1)
                    free(n, 2)
                    for j in range(NL):
                        if piece(j) == 2:
                            last = level(n, j)
                    last.then_inc(expo, 1)

            @block.scalar
            def _(act):
                def factors(n, p):
                    _, way, it, c0, _ = units[n]
                    r = n % 2
                    act.wait_ge(expo, pieces * n + p + 1)
                    if p == 0:
                        if n >= 2:
                            act.wait_ge(ends, n - 1)
                            act.wait_ge(q_done, n - 1)
                        act.activation(f[:, r, 0, :], run[:, it % 2, c0 * P:(c0 + CH) * P], ACT.Exp)
                        rows = slice(1, per_piece)
                    else:
                        rows = slice(p * per_piece, (p + 1) * per_piece)
                    act.activation(f[:, r, rows, :], f[:, r, rows, :], ACT.Exp).then_inc(fact, 1)

                def diagonals(n):
                    act.wait_ge(turned, n + 1)
                    if n >= 1:
                        act.wait_ge(diag, n)
                    act.activation(dot[:, :, :], ps[6][:, UW:UW + 2 * CH].rearrange("p (c h) -> p c h", h=2), ACT.Copy)\
                        .then_inc(dotted, 1)
                    act.wait_ge(dotted, n + 1)
                    if n >= 2:
                        act.wait_ge(out_mm, 2 * (n - 1))
                    for c in range(CH):
                        for h in range(2):
                            last = act.activation(att[:, n % 2, c, h, :], ident[:, :], ACT.Copy,
                                                  scale=dot[:, c, h:h + 1])
                    last.then_inc(diag, 1)

                def copy_k(n):
                    act.wait_ge(turned, n + 1)
                    if n >= 1:
                        act.wait_ge(gain_mm, n)
                    act.activation(k_tok[:, :], ps[6][:, 0:UW], ACT.Copy).then_inc(k_copied, 1)

                def take(n):
                    pair, way, it, c0, _ = units[n]
                    if way == FWD:
                        for h in range(2):
                            act.wait_ge(out_mm, 2 * n + h + 1)
                            col = slice((2 * pair + h) * LIN_V, (2 * pair + h + 1) * LIN_V)
                            act.activation(y_tok[:, c0:c0 + CH, col],
                                           ps[4 + h][:, 0:UW].rearrange("p (a t) -> p a t", t=P), ACT.Copy)\
                                .then_inc(y_done[FWD], 1)

                for p in range(pieces):
                    factors(0, p)
                for n in range(n_units + 1):
                    if n < n_units:
                        copy_k(n)
                        diagonals(n)
                    if n + 1 < n_units:
                        factors(n + 1, 0)
                        factors(n + 1, 1)
                    if n >= 1:
                        take(n - 1)
                    if n + 1 < n_units:
                        factors(n + 1, 2)

            @block.tensor
            def _(pe):
                pe.wait_ge(masks_in, 16)
                pe.wait_ge(z_done, 4)
                pe.wait_ge(sel_done, 3)

                def turn(n):
                    pe.wait_ge(ends, n + 1)
                    if n >= 1:
                        pe.wait_ge(dotted, n)
                        pe.wait_ge(k_copied, n)
                    for c in range(CH):
                        pe.matmul(ps[6][:, UW + 2 * c:UW + 2 * c + 2], kq[:, c * P:(c + 1) * P], sel[:, :],
                                         start=True, stop=True)
                    for c in range(CH):
                        last = pe.transpose(ps[6][:, c * P:(c + 1) * P], k_end[:, c * P:(c + 1) * P], ident[:, :])
                    last.then_inc(turned, 1)

                def adds(n):
                    pair, way, it, c0, _ = units[n]
                    pe.wait_ge(k_copied, n + 1)
                    pe.wait_ge(v_in[it % 2], 32 * (it // 2 + 1))
                    if n >= 1:
                        pe.wait_ge(s_done, CH * n)
                    for c in range(CH):
                        for h in range(2):
                            last = pe.matmul(ps[7][rows_of(h), c * P:(c + 1) * P],
                                             k_tok[:, c * P + half * h:c * P + half * (h + 1)],
                                             v[:, it % 2, c0 + c, h * LIN_V:(h + 1) * LIN_V], start=True, stop=True)
                    last.then_inc(gain_mm, 1)

                def score(n, j):
                    m = NL * n + j
                    pe.wait_ge(mixed, m + 1)
                    if m >= 4:
                        pe.wait_ge(picked, m - 3)
                    for c in range(CH):
                        last = pe.matmul(ps[m % 4][:, c * P:(c + 1) * P], f[:, n % 2, 2 + j, c * P:(c + 1) * P],
                                         qz[:, n % 2, j, c, :, :].rearrange("p h t -> p (h t)"),
                                         start=True, stop=True)
                    last.then_inc(score_mm, 1)

                def outputs(n, h):
                    pair, way, it, c0, _ = units[n]
                    pe.wait_ge(picked, NL * (n + 1))
                    pe.wait_ge(q_done, n + 1)
                    pe.wait_ge(s_done, CH * (n + 1))
                    if n >= 1:
                        before = units[n - 1]
                        pe.wait_ge(y_done[before[1]], 2 * (before[0] * per_item + before[4]) + h + 1)
                    for c in range(CH):
                        out = ps[4 + h][:, c * P:(c + 1) * P]
                        pe.matmul(out, att[:, n % 2, c, h, :],
                                  v[:, it % 2, c0 + c, h * LIN_V:(h + 1) * LIN_V], start=True, stop=False)
                        last = pe.matmul(out, q_in[:, n % 2, h, c * P:(c + 1) * P],
                                         state[:, it % 2, c0 + c, :], start=False, stop=True)
                    last.then_inc(out_mm, 1)

                for n in range(n_units + 1):
                    if n < n_units:
                        turn(n)
                        for j in range(NL):
                            score(n, j)
                            if j == 2:
                                adds(n)
                            if n >= 1 and j in (3, 5):
                                outputs(n - 1, (j - 3) // 2)
                    else:
                        for h in range(2):
                            outputs(n - 1, h)

            @block.vector
            def _(dve):
                dve.wait_ge(masks_in, 16)
                dve.wait_ge(zeroed, 1)
                dve.memset(sel[:, :], 0.0).then_inc(sel_done, 1)
                dve.memset(reset[:, :], 1.0).then_inc(reset_done, 1)
                dve.wait_ge(sel_done, 1)
                for h in range(2):
                    dve.memset(sel[rows_of(h), h:h + 1], 1.0).then_inc(sel_done, 1)
                dve.wait_ge(reset_done, 1)
                dve.memset(reset[:, 0:TOK:P], 0.0).then_inc(reset_done, 1)
                dve.wait_ge(reset_done, 2)

                def sums(it):
                    a, way = it % 2, it % 2
                    dve.wait_ge(g_in[a], 16 * (it // 2 + 1))
                    if it >= 2:
                        dve.wait_ge(fact, pieces * per_item * (it - 1))
                    dve.tensor_tensor_scan(run[:, a, :], reset[:, :], g[:, a, :], 0.0, ALU.mult, ALU.add)\
                        .then_inc(ran if way == FWD else inclusive, 1)
                    if way == BWD:
                        dve.wait_ge(inclusive, it // 2 + 1)
                        dve.tensor_tensor(run[:, a, :], run[:, a, :], g[:, a, :], ALU.subtract).then_inc(ran, 1)

                def mix(n, j):
                    pair, way, it, c0, _ = units[n]
                    size, r, a = LEVELS[j], n % 2, it % 2
                    cols = slice(c0 * P, (c0 + CH) * P)
                    if j == 0:
                        dve.wait_ge(qk_in[a], 32 * (it // 2 + 1))
                    dve.wait_ge(fact, pieces * n + piece(j) + 1)
                    if n >= 2:
                        dve.wait_ge(score_mm, NL * (n - 2) + j + 1)
                    late, early = (size, 0) if way == FWD else (0, size)
                    for h in range(2):
                        rows = rows_of(h)
                        dve.tensor_tensor(qz[rows, r, j, :, h, :].rearrange("p c (b w) -> p c b w", w=size),
                                          by_tile(q[rows, a, cols], size, late),
                                          by_tile(f[rows, r, 2 + j, :], size, late), ALU.mult)
                    kf = by_tile(f[:, r, 2 + j, :], size, early)
                    dve.tensor_tensor(kf, by_tile(k[:, a, cols], size, early), kf, ALU.mult).then_inc(mixed, 1)

                def q_ins(n):
                    pair, way, it, c0, _ = units[n]
                    dve.wait_ge(fact, pieces * n + 1)
                    if n >= 2:
                        dve.wait_ge(out_mm, 2 * (n - 1))
                    for h in range(2):
                        last = dve.tensor_tensor(q_in[rows_of(h), n % 2, h, :],
                                                 q[rows_of(h), it % 2, c0 * P:(c0 + CH) * P],
                                                 f[rows_of(h), n % 2, q_row(way), :], ALU.mult)
                    last.then_inc(q_done, 1)

                def pick(n, j):
                    way, m, size = units[n][1], NL * n + j, LEVELS[j]
                    dve.wait_ge(score_mm, m + 1)
                    if j == 0:
                        dve.wait_ge(diag, n + 1)
                    else:
                        dve.wait_ge(picked, m)
                    late = size if way == FWD else 0
                    out = att[:, n % 2, :, :, :].rearrange("p c h (b w) -> p (c h) b w", w=2 * size)
                    msk = mask[:, way, j, :].rearrange("p (a b w) -> p a b w", a=1, w=size)
                    dve.copy_predicated(out[:, :, :, late:late + size],
                                        msk.to_broadcast([P, 2 * CH, half // size, size]),
                                        ps[m % 4][:, 0:UW].rearrange("p (a b w) -> p a b w", a=2 * CH, w=size))\
                        .then_inc(picked, 1)

                def states(n):
                    pair, way, it, c0, _ = units[n]
                    a = it % 2
                    dve.wait_ge(gain_mm, n + 1)
                    for i in range(CH):
                        c = c0 + i if way == FWD else c0 + CH - 1 - i
                        src = 0 if c == 0 else c
                        dst = NT if c == 0 else (c + 1 if way == FWD else c - 1)
                        if c == (NT - 1 if way == FWD else 1):
                            dst = NT + 1
                        if CH * n + i:
                            dve.wait_ge(s_done, CH * n + i)
                        dve.scalar_tensor_tensor(state[:, a, dst, :], state[:, a, src, :],
                                                 decay[:, n % 2, c - c0:c - c0 + 1],
                                                 ps[7][:, (c - c0) * P:(c - c0 + 1) * P], ALU.mult, ALU.add)\
                            .then_inc(s_done, 1)

                def take(n):
                    pair, way, it, c0, _ = units[n]
                    if way == BWD:
                        for h in range(2):
                            dve.wait_ge(out_mm, 2 * n + h + 1)
                            col = slice((2 * pair + h) * LIN_V, (2 * pair + h + 1) * LIN_V)
                            y = y_tok[:, c0:c0 + CH, col]
                            dve.tensor_tensor(y, y, ps[4 + h][:, 0:UW].rearrange("p (a t) -> p a t", t=P), ALU.add)\
                                .then_inc(y_done[BWD], 1)

                sums(0)
                for h in range(2):
                    dve.memset(q_in[rows_of(1 - h), :, h, :], 0.0).then_inc(z_done, 1)
                    dve.memset(qz[rows_of(1 - h), :, :, :, h, :], 0.0).then_inc(z_done, 1)
                for j in range(NL):
                    mix(0, j)
                q_ins(0)
                for n in range(n_units + 1):
                    if n < n_units:
                        if n % per_item == per_item - 2 and n // per_item + 1 < 2 * LIN_PAIRS:
                            sums(n // per_item + 1)
                        for j in range(NL):
                            if n + 1 < n_units:
                                mix(n + 1, j)
                            pick(n, j)
                        states(n)
                        if n + 1 < n_units:
                            q_ins(n + 1)
                    if n >= 1:
                        take(n - 1)


def lin_finish(nc, tag, d, y_tok, eps):
    with Scope(nc, tag) as s:
        gate = s.sb("gate", [P, 3, D])
        norm_w = s.sb("norm_w", [P, D])
        sq = s.sb("sq", [P, 2, D])
        ss, root, inv = s.sb("ss", [P, NT, LIN_H]), s.sb("root", [P, NT, LIN_H]), s.sb("inv", [P, NT, LIN_H])
        w_in, arrived = s.sem("w_in"), [s.sem(f"arrived{i}") for i in range(3)]
        squared, summed, rooted, inverted = s.sem("squared"), s.sem("summed"), s.sem("rooted"), s.sem("inverted")
        active, weighed, normed, done = s.sem("active"), s.sem("weighed"), s.sem("normed"), s.sem("done")
        with nc.Block() as block:
            @block.sync
            def _(sp):
                sp.dma_start(norm_w[:, :], d["lin_norm"]).then_inc(w_in, 16)
                for c in range(NT):
                    if c >= 3:
                        sp.wait_ge(done, c - 2)
                    for half in range(2):
                        sp.dma_start(gate[:, c % 3, half * 512:(half + 1) * 512],
                                     d["u1_tok"][c, :, half * D + 512:half * D + D]).then_inc(arrived[c % 3], 16)

            @block.scalar
            def _(act):
                for c in range(NT):
                    if c >= 2:
                        act.wait_ge(summed, c - 1)
                    act.activation(sq[:, c % 2, :], y_tok[:, c, :], ACT.Square).then_inc(squared, 1)
                act.wait_ge(summed, NT)
                act.activation(root[:, :, :], ss[:, :, :], ACT.Sqrt, bias=eps[:, 0:1], scale=1.0 / LIN_V)\
                    .then_inc(rooted, 1)
                for c in range(NT):
                    act.wait_ge(arrived[c % 3], 32 * (c // 3 + 1))
                    act.activation(gate[:, c % 3, :], gate[:, c % 3, :], ACT.Silu).then_inc(active, 1)

            @block.gpsimd
            def _(pool):
                pool.wait_ge(w_in, 16)
                for c in range(NT):
                    pool.wait_ge(active, c + 1)
                    pool.tensor_tensor(gate[:, c % 3, :], gate[:, c % 3, :], norm_w[:, :], ALU.mult)\
                        .then_inc(weighed, 1)

            @block.vector
            def _(dve):
                for c in range(NT):
                    dve.wait_ge(squared, c + 1)
                    dve.tensor_reduce(ss[:, c, :], sq[:, c % 2, :].rearrange("p (h v) -> p h v", v=LIN_V), AX.X,
                                      ALU.add).then_inc(summed, 1)
                dve.wait_ge(rooted, 1)
                dve.reciprocal(inv[:, :, :], root[:, :, :]).then_inc(inverted, 1)
                dve.wait_ge(inverted, 1)
                for c in range(NT):
                    y = y_tok[:, c, :]
                    yh = y.rearrange("p (h v) -> p h v", v=LIN_V)
                    dve.tensor_tensor(yh, yh, bcast(inv[:, c, :], LIN_V), ALU.mult).then_inc(normed, 1)
                    dve.wait_ge(normed, c + 1)
                    dve.wait_ge(weighed, c + 1)
                    dve.tensor_tensor(y, y, gate[:, c % 3, :], ALU.mult).then_inc(done, 1)


def trunk(nc, d):
    def dram(name, shape):
        d[name] = nc.dram_tensor(name, shape, F32).ap()

    dram("u0_t", (14, P, TOK))
    dram("u0_tok", (NT, P, 1024))
    dram("u0_small", (P, NT * 16))
    dram("u1_t", (10, P, TOK))
    dram("u1_tok", (NT, P, 2048))
    dram("u1_small", (2 * RANK, TOK))
    dram("lin_g", (8, P, TOK))
    dram("lin_k", (4, P, TOK))
    dram("lin_q", (2, P, TOK))
    with Scope(nc, "all") as s:
        x_t = s.sb("x_t", [P, KT, TOK])
        mods = s.sb("mods", [P, DEPTH * ADA, 2])
        gains = s.sb("gains", [P, DEPTH, 2, KT, 2])
        ones, ident, eps = s.sb("ones", [P, P]), s.sb("ident", [P, P]), s.sb("eps", [P, 1])
        filled, out = s.sem("filled"), s.sem("out")
        u_stored = [[s.sem(f"u{l}_stored{i}", True) for i in range(5)] for l in range(DEPTH)]
        with nc.Block() as block:
            @block.vector
            def _(dve):
                dve.memset(ones[:, :], 1.0).then_inc(filled, 1)
                dve.memset(eps[:, :], EPS).then_inc(filled, 1)
                dve.wait_ge(filled, 2)
        modulation(nc, d, mods, gains, x_t, ident)
        for l in range(DEPTH):
            with Scope(nc, f"hm{l}") as hs:
                h_hi, h_lo = hs.sb("h_hi", [P, KT, TOK], F32R), hs.sb("h_lo", [P, KT, TOK], F32R)
                raw, arrived = hs.sb("raw", [P, 2, KT * P]), [hs.sem("arrived0"), hs.sem("arrived1")]
                norm(nc, f"n{l}a", l, 0, x_t, ones, eps, mods, gains, h_hi, h_lo, d,
                     [(raw[:, j, :], d[f"w{l}_t"][j], arrived[j]) for j in range(2)])
                small = d["u0_small"].rearrange("p (t n) -> p t n", n=16) if l == 0 else d["u1_small"]
                in_project(nc, f"in{l}", u_stored[l], d[f"w{l}_t"], d[f"w{l}_tok"], h_hi, h_lo, d[f"u{l}_t"],
                           d[f"u{l}_tok"], small, (2 * SSD_H, 2 * RANK)[l], l == 0, ident, raw, arrived)
            if l == 1:
                lin_gates(nc, "gates", d)
            with Scope(nc, f"mix{l}") as ms:
                y_tok = ms.sb("y", [P, NT, D])
                if l == 0:
                    with Scope(nc, "masks") as t:
                        tri = t.sb("tri", [P, 4, P])
                        tri_in = t.sem("tri_in")
                        with nc.Block() as block:
                            @block.sync
                            def _(sp):
                                sp.dma_start(tri[:, :, :], d["tri"]).then_inc(tri_in, 16)
                                sp.wait_ge(tri_in, 16)
                        ssd(nc, "ssd", d, y_tok, ident, tri, ones, eps)
                    na(nc, "na", d, y_tok, ident, eps)
                else:
                    linear_scans(nc, "lin", d, y_tok, ident)
                    lin_finish(nc, "fin", d, y_tok, eps)
                out_project(nc, f"out{l}", l, d["w_out"][l], y_tok, ident, x_t, mods)
            with Scope(nc, f"hf{l}") as hs:
                h_hi, h_lo = hs.sb("h_hi", [P, KT, TOK], F32R), hs.sb("h_lo", [P, KT, TOK], F32R)
                raw, arrived = hs.sb("raw", [P, 2, KT * P]), [hs.sem("arrived0"), hs.sem("arrived1")]
                norm(nc, f"n{l}b", l, 1, x_t, ones, eps, mods, gains, h_hi, h_lo, d,
                     [(raw[:, j, :], d["w_up"][l, j], arrived[j]) for j in range(2)])
                conv_ffn(nc, f"ffn{l}", l, d, x_t, mods, h_hi, h_lo, raw, arrived)
        with nc.Block() as block:
            @block.sync
            def _(sp):
                sp.dma_start(d["o_x"], x_t[:, :, :]).then_inc(out, 16)
                sp.wait_ge(out, 16)


def t_form(a):
    return a.reshape(a.shape[0], -1, P).transpose(2, 1, 0)


def tiles(w, cols=P):
    k, n = w.shape
    return w.reshape(k // P, P, n // cols, cols).transpose(2, 1, 0, 3).reshape(n // cols, P, k // P * cols)


def layout(np, i):
    o = {}
    rows = np.concatenate([i["x_prompt"].reshape(CTX, D), i["x_sample"].reshape(LAT, D)], axis=0)
    o["x_t"] = t_form(rows)
    o["c_t"] = t_form(np.stack([i["c_ctx"], i["c"].reshape(D)]))
    o["w_ada"] = np.stack([tiles(w) for w in i["w_ada"]]).reshape(DEPTH * ADA // 4, 4, P, KT, P)
    twice = lambda a: np.stack([a, a], axis=-1)
    o["b_ada"] = twice(i["b_ada"].reshape(DEPTH * ADA, P).transpose(1, 0))
    o["norm_w"] = twice(i["norm_w"].reshape(DEPTH, 2, KT, P).transpose(3, 0, 1, 2))
    up = np.stack([tiles(w) for w in i["ffn_w_up"]]).reshape(DEPTH, 2, FT, P, D)
    o["w_up"] = up.transpose(0, 2, 1, 3, 4).reshape(DEPTH, 2 * FT, P, D)
    o["w_down"] = i["ffn_w_down"].reshape(DEPTH, FT, P, D)
    taps = np.concatenate([i["ffn_conv_w"], i["ffn_conv_b"][:, None]], axis=1)
    o["ffn_conv"] = taps.reshape(DEPTH, 4, 2, FT, P).transpose(0, 4, 3, 2, 1)
    w0 = i["w_in_l0"]
    filled = lambda a: np.concatenate([a, np.zeros((D, P - a.shape[1]), a.dtype)], axis=1)
    o["w0_t"] = tiles(np.concatenate([w0[:, 512:1280], w0[:, 1296:2320], filled(w0[:, 1280:1296])], axis=1))
    o["w0_tok"] = tiles(np.concatenate([w0[:, 0:512], w0[:, 2320:2832]], axis=1), 256)
    o["w_out"] = np.stack([tiles(i["w_out_l0"]), tiles(i["w_out_l1"])])
    taps = np.concatenate([i["ssd_conv_w_l0"], i["ssd_conv_b_l0"][None]])
    o["ssd_conv"] = taps.reshape(4, 6, P).transpose(2, 1, 0)
    row = np.concatenate([i["ssd_dt_bias_l0"].reshape(16), i["ssd_a_log_l0"].reshape(16), i["ssd_d_l0"],
                          i["ssd_norm_w_l0"]])
    o["ssd_row"] = np.repeat(row[None], P, axis=0)
    st = np.stack([i["state_ssd_fwd_l0"], i["state_ssd_bwd_l0"]]).reshape(2, 2, 4, 64, 64)
    o["ssd_state"] = st.transpose(1, 3, 0, 2, 4).reshape(P, 2, 256)
    r = np.arange(P)
    o["tri"] = np.stack([r[:, None] <= r, r[:, None] >= r, r[:, None] < r, r[:, None] > r], axis=1).astype(np.float32)
    o["ident"] = np.eye(P, dtype=np.float32)
    o["half"] = np.kron(np.eye(2), np.ones((64, 64))).astype(np.float32)
    o["qk_gain"] = np.tile(np.stack([i["na_q_norm_l0"], i["na_k_norm_l0"]], axis=1), (2, 1))
    o["k_old"] = i["cache_na_k_l0"].reshape(4, 2, P, 64).transpose(1, 3, 0, 2).reshape(P, 4, P)
    o["v_old"] = i["cache_na_v_l0"].reshape(8, P, 64).transpose(1, 0, 2).reshape(P, 512)
    q, k = np.arange(64)[:, None], np.arange(64)[None]
    start = np.clip(q - 8, 0, 48)
    rel = i["na_rpb_l0"][:, :, np.clip(k - q, -15, 15) + 15]
    rel = np.where((k >= start) & (k < start + 16), rel, np.float32(-1e30))
    o["na_bias"] = rel.reshape(4, 2, 15, 64, 64).transpose(1, 3, 0, 2, 4).reshape(P, 4, 15, 64)
    w1 = i["w_in_l1"]
    o["w1_t"] = tiles(np.concatenate([w1[:, 0:512], w1[:, 1568:2336], filled(w1[:, 1536:1568])], axis=1))
    o["w1_tok"] = tiles(np.concatenate([w1[:, 512:1536], w1[:, 2336:3360]], axis=1), 256)
    wa = i["gla_wa2_l1"].reshape(2, 16, 2, P)
    zero = np.zeros((16, 2, P), np.float32)
    o["wa2"] = np.stack([np.concatenate([wa[0], zero]), np.concatenate([zero, wa[1]])], axis=1)
    lin = np.concatenate([i["gla_ba2_l1"][:, None], i["hgrn_lb_logits"]], axis=1)
    o["lin_vec"] = lin.reshape(2, 3, 2, P).transpose(3, 0, 2, 1)
    s_idx, t_idx = r[:, None], r[None]
    fwd = [(s_idx // (2 * b) == t_idx // (2 * b)) & (s_idx // b % 2 == 0) & (t_idx // b % 2 == 1)
                              for b in LEVELS]
    fwd = np.stack(fwd)
    later = [np.array([t for t in range(P) if t // b % 2 == 1]) for b in LEVELS]
    sooner = [np.array([t for t in range(P) if t // b % 2 == 0]) for b in LEVELS]
    o["lin_mask"] = np.stack([np.stack([m[:, t] for m, t in zip(fwd, later)]),
                              np.stack([m.T[:, t] for m, t in zip(fwd, sooner)])]).transpose(2, 0, 1, 3).astype(np.int16)
    st = np.stack([np.stack([i[f"state_{m}_{w}_l1"].reshape(4, 64, 128) for w in ("fwd", "bwd")])
                   for m in ("gla", "hgrn")])
    o["lin_state"] = st.reshape(2, 2, 2, P, 128).transpose(0, 2, 1, 3, 4).reshape(8, P, 128)
    o["lin_norm"] = np.repeat(np.concatenate([np.tile(i["gla_norm_w_l1"], 4), np.tile(i["hgrn_norm_w_l1"], 4)])[None],
                              P, axis=0)
    return {k: np.ascontiguousarray(v) for k, v in o.items()}


OUTS = {"o_x": (P, KT, TOK), "o_k": (P, 4, P), "o_v": (P, 512), "o_ssd": (P, 2, 256), "o_lin": (8, P, P)}


def kernel(**inputs):
    import numpy as np
    import concourse.bacc as bacc
    from concourse.bass_utils import run_bass_kernel_spmd

    arrays = layout(np, {k: np.asarray(v) for k, v in inputs.items()})
    nc = bacc.Bacc("TRN2", target_bir_lowering=False, num_devices=1)
    d = {n: nc.dram_tensor(n, a.shape, mybir.dt.from_np(a.dtype), kind="ExternalInput").ap()
         for n, a in arrays.items()}
    d.update({n: nc.dram_tensor(n, shape, F32, kind="ExternalOutput").ap() for n, shape in OUTS.items()})
    trunk(nc, d)
    r = run_bass_kernel_spmd(nc, [arrays], core_ids=[0]).results[0]

    y = r["o_x"].transpose(2, 1, 0).reshape(TOK, D)
    na_k = r["o_k"].reshape(2, 64, 4, P).transpose(2, 0, 3, 1).reshape(1, 8, P, 64)
    na_v = r["o_v"].reshape(P, 8, 64).transpose(1, 0, 2).reshape(1, 8, P, 64)
    ssd_out = r["o_ssd"].reshape(2, 64, 2, 4, 64).transpose(2, 0, 3, 1, 4).reshape(2, 1, 8, 64, 64)
    lin = r["o_lin"].reshape(2, 2, 2, 2, 64, 128).transpose(0, 2, 1, 3, 4, 5).reshape(2, 2, 1, 4, 64, 128)
    return (y[:CTX].reshape(1, CTX, D), y[CTX:].reshape(1, LAT, D), na_k, na_v, ssd_out[0], ssd_out[1],
            lin[0, 0], lin[0, 1], lin[1, 0], lin[1, 1])
```
